# Optimizing a Trainium2 kernel written in Bass

```python
import math
import jax
import jax.numpy as jnp
from jax import lax
import numpy as np

D_MODEL = 2048
BATCH = 1
SEQ = 256
DEPTH = 2
DEC_BATCH = 8
DEC_SEQ = 1
PAST_LEN = 2048
PAGE_SIZE = 128

HEAD_DIM = 128
BRANCH_W = D_MODEL // 4
N_HEADS = BRANCH_W // HEAD_DIM
N_BRANCH = 5
CONV_W = 4
CONV_DIM = 4 * BRANCH_W
CHUNK = 64
QBLOCK = 64
DSA_TOPK = 256
IDX_HEADS = 8
IDX_DIM = 64
LRU_C = 8.0
ROPE_THETA = 10000.0
N_MEM = 256
LN_EPS = 1e-5
NORM_EPS = 1e-6
DEEPNORM_ALPHA = (2 * DEPTH) ** 0.25
DEEPNORM_BETA = (8 * DEPTH) ** -0.25
IN_SPLITS = (CONV_DIM, BRANCH_W, N_HEADS, N_HEADS,
             BRANCH_W, BRANCH_W, BRANCH_W, BRANCH_W, IDX_HEADS * IDX_DIM, IDX_DIM, IDX_HEADS,
             BRANCH_W, BRANCH_W, BRANCH_W, BRANCH_W,
             BRANCH_W,
             BRANCH_W, BRANCH_W,
             N_BRANCH * D_MODEL)
N_IN = sum(IN_SPLITS)

kernel_name = 'hybrid_gdn_dsa_retnet_rglru_step'

def split_in(h):
    offs = [int(o) for o in np.cumsum(IN_SPLITS)[:-1]]
    return jnp.split(h, offs, axis=-1)

def heads(a, d=HEAD_DIM):
    return a.reshape(*a.shape[:-1], a.shape[-1] // d, d)

def layer_norm(x, g, b):
    xf = x.astype(jnp.float32)
    mu = xf.mean(-1, keepdims=True)
    var = jnp.square(xf - mu).mean(-1, keepdims=True)
    y = (xf - mu) * lax.rsqrt(var + LN_EPS) * g.astype(jnp.float32) + b.astype(jnp.float32)
    return y.astype(x.dtype)

def l2norm(x):
    xf = x.astype(jnp.float32)
    return xf * lax.rsqrt(jnp.sum(xf * xf, -1, keepdims=True) + NORM_EPS)

def head_group_norm(o):
    mu = o.mean(-1, keepdims=True)
    var = jnp.square(o - mu).mean(-1, keepdims=True)
    return (o - mu) * lax.rsqrt(var + LN_EPS)

def rope(x, pos):
    half = x.shape[-1] // 2
    inv = ROPE_THETA ** (-jnp.arange(half, dtype=jnp.float32) / half)
    ang = pos.astype(jnp.float32)[:, None] * inv[None, :]
    cos = jnp.cos(ang)[:, None, :]
    sin = jnp.sin(ang)[:, None, :]
    xf = x.astype(jnp.float32)
    x1, x2 = xf[..., :half], xf[..., half:]
    return jnp.concatenate([x1 * cos - x2 * sin, x2 * cos + x1 * sin], -1).astype(x.dtype)

def causal_conv(x, buf, w, b):
    t = x.shape[1]
    xp = jnp.concatenate([buf.astype(x.dtype), x], axis=1)
    y = b + xp[:, 0:t] * w[0]
    for j in range(1, CONV_W):
        y = y + xp[:, j:j + t] * w[j]
    return y, xp[:, t:]

def batch_take(a, idx):
    return jax.vmap(lambda ab, ib: ab[ib])(a, idx)

def to_chunks(a, n, c):
    b, _, h = a.shape[:3]
    a = a.astype(jnp.float32).reshape(b, n, c, h, *a.shape[3:])
    return jnp.moveaxis(a, 3, 2)

def from_chunks(o):
    n, b, h, c, d = o.shape
    return o.transpose(1, 0, 3, 2, 4).reshape(b, n * c, h, d)

def gated_delta_chunked(q, k, v, g, beta, s0):
    t = q.shape[1]
    dv = v.shape[-1]
    c = math.gcd(t, CHUNK)
    n = t // c
    q, k, v, g, beta = (to_chunks(a, n, c) for a in (q, k, v, g, beta))
    gc = jnp.cumsum(g, axis=-1)
    i = jnp.arange(c)
    tril = i[:, None] >= i[None, :]
    strict = i[:, None] > i[None, :]
    decay = jnp.exp(jnp.where(tril, gc[..., :, None] - gc[..., None, :], -jnp.inf))
    kk = jnp.einsum('bnhid,bnhjd->bnhij', k, k)
    m = jnp.eye(c, dtype=jnp.float32) + jnp.where(strict, beta[..., :, None] * kk * decay, 0.0)
    rhs = jnp.concatenate([v * beta[..., None], k * (beta * jnp.exp(gc))[..., None]], axis=-1)
    sol = lax.linalg.triangular_solve(m, rhs, left_side=True, lower=True, unit_diagonal=True)
    u, w = sol[..., :dv], sol[..., dv:]
    qk = jnp.einsum('bnhid,bnhjd->bnhij', q, k) * decay
    q_dec = q * jnp.exp(gc)[..., None]
    k_tail = k * jnp.exp(gc[..., -1:] - gc)[..., None]
    g_last = jnp.exp(gc[..., -1])

    def step(s, xs):
        u_n, w_n, qd_n, qk_n, kt_n, gl_n = xs
        v_new = u_n - jnp.einsum('bhcd,bhde->bhce', w_n, s)
        o = jnp.einsum('bhcd,bhde->bhce', qd_n, s) + jnp.einsum('bhij,bhje->bhie', qk_n, v_new)
        s = s * gl_n[..., None, None] + jnp.einsum('bhcd,bhce->bhde', kt_n, v_new)
        return s, o

    xs = tuple(jnp.moveaxis(a, 1, 0) for a in (u, w, q_dec, qk, k_tail, g_last))
    s_fin, o = lax.scan(step, s0.astype(jnp.float32), xs)
    return from_chunks(o), s_fin

def retention_chunked(q, k, v, r0):
    t, h = q.shape[1], q.shape[2]
    c = math.gcd(t, CHUNK)
    n = t // c
    lg = jnp.log(1.0 - 2.0 ** (-5.0 - jnp.arange(h, dtype=jnp.float32)))
    q, k, v = (to_chunks(a, n, c) for a in (q, k, v))
    i = jnp.arange(c, dtype=jnp.float32)
    tril = i[:, None] >= i[None, :]
    dist = jnp.where(tril, i[:, None] - i[None, :], 0.0)
    dmat = jnp.where(tril, jnp.exp(dist[None] * lg[:, None, None]), 0.0)
    o_in = jnp.einsum('bnhij,bnhje->bnhie', jnp.einsum('bnhid,bnhjd->bnhij', q, k) * dmat, v)
    xi = jnp.exp((i + 1.0)[None, :] * lg[:, None])
    zeta = jnp.exp((c - 1.0 - i)[None, :] * lg[:, None])
    g_c = jnp.exp(c * lg)
    q_x = q * xi[..., None]
    k_z = k * zeta[..., None]

    def step(r, xs):
        qx_n, kz_n, v_n = xs
        o = jnp.einsum('bhcd,bhde->bhce', qx_n, r)
        r = r * g_c[None, :, None, None] + jnp.einsum('bhcd,bhce->bhde', kz_n, v_n)
        return r, o

    xs = tuple(jnp.moveaxis(a, 1, 0) for a in (q_x, k_z, v))
    r_fin, o_cross = lax.scan(step, r0.astype(jnp.float32), xs)
    o = jnp.moveaxis(o_in, 1, 0) + o_cross
    return from_chunks(o), r_fin

def rglru(x, r, i, lam, h0):
    x, r, i = (a.astype(jnp.float32) for a in (x, r, i))
    log_a = -LRU_C * r * jax.nn.softplus(-lam.astype(jnp.float32))
    a = jnp.exp(log_a)
    b = jnp.sqrt(-jnp.expm1(2.0 * log_a)) * (i * x)

    def step(h, ab):
        h = ab[0] * h + ab[1]
        return h, h

    h_fin, hs = lax.scan(step, h0.astype(jnp.float32), (a.swapaxes(0, 1), b.swapaxes(0, 1)))
    return hs.swapaxes(0, 1), h_fin

def dsa_sweep(q, qi, wi, q_pos, ki_all, gather, ksel):
    bsz, t = q.shape[:2]
    qb = math.gcd(t, QBLOCK)
    nb = t // qb
    key_pos = jnp.arange(ki_all.shape[1])
    scale = HEAD_DIM ** -0.5

    def blocks(a):
        return a.reshape(bsz, nb, qb, *a.shape[2:]).swapaxes(0, 1)

    def one_block(args):
        q_blk, qi_blk, w_blk, p_blk = args
        s = jnp.einsum('bqhd,bsd->bqhs', qi_blk, ki_all).astype(jnp.float32)
        score = jnp.einsum('bqhs,bqh->bqs', jax.nn.relu(s), w_blk.astype(jnp.float32))
        score = jnp.where(key_pos[None, None, :] <= p_blk[None, :, None], score, -jnp.inf)
        _, idx = lax.top_k(score, ksel)
        valid = idx <= p_blk[None, :, None]
        k_g, v_g = gather(idx)
        logits = jnp.einsum('bqhd,bqkhd->bqhk', q_blk, k_g).astype(jnp.float32) * scale
        logits = jnp.where(valid[:, :, None, :], logits, -jnp.inf)
        prob = jax.nn.softmax(logits, axis=-1).astype(v_g.dtype)
        return jnp.einsum('bqhk,bqkhd->bqhd', prob, v_g)

    out = lax.map(one_block, (blocks(q), blocks(qi), blocks(wi), q_pos.reshape(nb, qb)))
    return out.swapaxes(0, 1).reshape(bsz, t, *out.shape[3:])

def dsa_prompt(q, k, v, qi, ki, wi, pos):
    ksel = min(DSA_TOPK, q.shape[1] // 4)
    gather = lambda idx: (batch_take(k, idx), batch_take(v, idx))
    return dsa_sweep(q, qi, wi, pos, ki, gather, ksel)

def make_dsa_sample(pool_k, pool_v, pool_ik, page_table):
    def attend(q, k, v, qi, ki, wi, pos):
        db, t = q.shape[:2]
        past = page_table.shape[1] * PAGE_SIZE
        ik_past = pool_ik[page_table].reshape(db, past, IDX_DIM)
        ki_all = jnp.concatenate([ik_past.astype(ki.dtype), ki], axis=1)
        ksel = min(DSA_TOPK, (past + t) // 4)

        def gather(idx):
            in_past = idx < past
            pi = jnp.minimum(idx, past - 1)
            phys = jnp.take_along_axis(page_table, (pi // PAGE_SIZE).reshape(db, -1), axis=1).reshape(idx.shape)
            off = pi % PAGE_SIZE
            ni = jnp.clip(idx - past, 0, t - 1)
            sel = in_past[..., None, None]
            k_g = jnp.where(sel, pool_k[phys, off].astype(k.dtype), batch_take(k, ni))
            v_g = jnp.where(sel, pool_v[phys, off].astype(v.dtype), batch_take(v, ni))
            return k_g, v_g

        return dsa_sweep(q, qi, wi, pos, ki_all, gather, ksel)
    return attend

def mem_attend(q, mk, mv):
    logits = jnp.einsum('bthd,bmhd->bhtm', q, mk).astype(jnp.float32) * HEAD_DIM ** -0.5
    prob = jax.nn.softmax(logits, axis=-1).astype(mv.dtype)
    return jnp.einsum('bhtm,bmhd->bthd', prob, mv)

def mixer_layer(x, pos0, conv_buf, s_gdn, s_ret, h_lru, mem_k, mem_v, dsa_attend, p):
    bsz, t = x.shape[:2]
    dt = x.dtype
    pos = pos0 + jnp.arange(t)
    (conv_in, gdn_z, gdn_a, gdn_b, dsa_q, dsa_k, dsa_v, dsa_z, idx_q, idx_k, idx_w,
     ret_q, ret_k, ret_v, ret_z, lru_z, mem_q, mem_z, gate_pre) = split_in(x @ p['w_in'])

    conv_out, new_conv = causal_conv(conv_in, conv_buf, p['conv_w'], p['conv_b'])
    gq, gk, gv = jnp.split(jax.nn.silu(conv_out[..., :3 * BRANCH_W]), 3, axis=-1)
    lru_x = conv_out[..., 3 * BRANCH_W:]

    q_a = l2norm(heads(gq)) * HEAD_DIM ** -0.5
    k_a = l2norm(heads(gk))
    beta = jax.nn.sigmoid(gdn_b.astype(jnp.float32))
    g = -jnp.exp(p['gdn_a_log'].astype(jnp.float32)) * jax.nn.softplus(gdn_a.astype(jnp.float32) + p['gdn_dt_bias'])
    o_a, new_gdn = gated_delta_chunked(q_a, k_a, heads(gv), g, beta, s_gdn)
    o_a = o_a * lax.rsqrt(jnp.mean(o_a * o_a, -1, keepdims=True) + NORM_EPS) * p['gdn_norm_w']
    y_a = o_a.reshape(bsz, t, BRANCH_W).astype(dt) * jax.nn.silu(gdn_z)

    q_b = rope(heads(dsa_q), pos)
    k_b = rope(heads(dsa_k), pos)
    v_b = heads(dsa_v)
    qi = rope(heads(idx_q, IDX_DIM), pos)
    ki = rope(idx_k[:, :, None, :], pos)[:, :, 0]
    wi = idx_w * (IDX_HEADS * IDX_DIM) ** -0.5
    o_b = dsa_attend(q_b, k_b, v_b, qi, ki, wi, pos)
    y_b = o_b.reshape(bsz, t, BRANCH_W) * jax.nn.silu(dsa_z)

    q_c = rope(heads(ret_q), pos)
    k_c = rope(heads(ret_k), pos) * HEAD_DIM ** -0.5
    o_c, new_ret = retention_chunked(q_c, k_c, heads(ret_v), s_ret)
    y_c = head_group_norm(o_c).reshape(bsz, t, BRANCH_W).astype(dt) * jax.nn.silu(ret_z)

    xb = heads(lru_x)
    r = jax.nn.sigmoid(jnp.einsum('bthi,hij->bthj', xb, p['lru_w_r']).reshape(bsz, t, BRANCH_W) + p['lru_b_r'])
    ig = jax.nn.sigmoid(jnp.einsum('bthi,hij->bthj', xb, p['lru_w_i']).reshape(bsz, t, BRANCH_W) + p['lru_b_i'])
    o_d, new_h = rglru(lru_x, r, ig, p['lru_lambda'], h_lru)
    y_d = o_d.astype(dt) * jax.nn.silu(lru_z)

    y_e = mem_attend(heads(mem_q), mem_k, mem_v).reshape(bsz, t, BRANCH_W) * jax.nn.silu(mem_z)

    ys = (y_a, y_b, y_c, y_d, y_e)
    gates = jax.nn.sigmoid(gate_pre.reshape(bsz, t, N_BRANCH, D_MODEL))
    w_br = p['w_branch']
    merged = gates[:, :, 0] * (ys[0] @ w_br[0])
    for nbr in range(1, N_BRANCH):
        merged = merged + gates[:, :, nbr] * (ys[nbr] @ w_br[nbr])
    out = merged @ p['w_out']
    y = layer_norm(DEEPNORM_ALPHA * x + out, p['ln_g'], p['ln_b'])
    states = (new_conv, new_gdn.astype(dt), new_ret.astype(dt), new_h.astype(dt))
    rows = (k_b, v_b, ki)
    return y, states, rows

def setup_inputs(seed: int = 0) -> dict:
    key = jax.random.key(seed)
    ks = iter(jax.random.split(key, 40))
    f32 = jnp.float32
    n_pages = PAST_LEN // PAGE_SIZE
    used = DEC_BATCH * n_pages
    n_pool = used + max(1, used // 4)

    def normal(shape, scale=1.0):
        return scale * jax.random.normal(next(ks), shape, f32)

    x_prompt = normal((BATCH, SEQ, D_MODEL))
    x_sample = normal((DEC_BATCH, DEC_SEQ, D_MODEL))
    cache_conv = normal((DEPTH, DEC_BATCH, CONV_W - 1, CONV_DIM))
    cache_dsa_k = normal((DEPTH, n_pool, PAGE_SIZE, N_HEADS, HEAD_DIM))
    cache_dsa_v = normal((DEPTH, n_pool, PAGE_SIZE, N_HEADS, HEAD_DIM))
    cache_dsa_idx_k = normal((DEPTH, n_pool, PAGE_SIZE, IDX_DIM))
    cache_mem_k = normal((DEPTH, DEC_BATCH, N_MEM, N_HEADS, HEAD_DIM))
    cache_mem_v = normal((DEPTH, DEC_BATCH, N_MEM, N_HEADS, HEAD_DIM))
    state_gdn = normal((DEPTH, DEC_BATCH, N_HEADS, HEAD_DIM, HEAD_DIM), 0.1)
    state_ret = normal((DEPTH, DEC_BATCH, N_HEADS, HEAD_DIM, HEAD_DIM), 0.5)
    state_lru = normal((DEPTH, DEC_BATCH, BRANCH_W))
    page_table = jax.random.permutation(next(ks), n_pool)[:used].reshape(DEC_BATCH, n_pages).astype(jnp.int32)
    mem_prompt = normal((BATCH, N_MEM, D_MODEL))

    w_in = normal((DEPTH, D_MODEL, N_IN), D_MODEL ** -0.5)
    conv_w = normal((DEPTH, CONV_W, CONV_DIM), 0.5)
    conv_b = normal((DEPTH, CONV_DIM), 0.01)
    a_init = jax.random.uniform(next(ks), (DEPTH, N_HEADS), f32, 1.0, 16.0)
    gdn_a_log = jnp.log(a_init)
    dt_init = jnp.exp(jax.random.uniform(next(ks), (DEPTH, N_HEADS), f32, math.log(1e-3), math.log(1e-1)))
    gdn_dt_bias = dt_init + jnp.log(-jnp.expm1(-dt_init))
    gdn_norm_w = 1.0 + normal((DEPTH, HEAD_DIM), 0.01)
    a0 = jax.random.uniform(next(ks), (DEPTH, BRANCH_W), f32, 0.9, 0.999)
    s0 = a0 ** (1.0 / LRU_C)
    lru_lambda = jnp.log(s0) - jnp.log1p(-s0)
    lru_w_r = normal((DEPTH, N_HEADS, HEAD_DIM, HEAD_DIM), HEAD_DIM ** -0.5)
    lru_b_r = normal((DEPTH, BRANCH_W), 0.01)
    lru_w_i = normal((DEPTH, N_HEADS, HEAD_DIM, HEAD_DIM), HEAD_DIM ** -0.5)
    lru_b_i = normal((DEPTH, BRANCH_W), 0.01)
    w_mem_kv = normal((DEPTH, D_MODEL, 2 * BRANCH_W), D_MODEL ** -0.5)
    w_branch = normal((DEPTH, N_BRANCH, BRANCH_W, D_MODEL), BRANCH_W ** -0.5 * DEEPNORM_BETA)
    w_out = normal((DEPTH, D_MODEL, D_MODEL), D_MODEL ** -0.5 * DEEPNORM_BETA)
    ln_g = 1.0 + normal((DEPTH, D_MODEL), 0.01)
    ln_b = normal((DEPTH, D_MODEL), 0.01)
    return {'x_prompt': x_prompt, 'x_sample': x_sample, 'cache_conv': cache_conv,
            'cache_dsa_k': cache_dsa_k, 'cache_dsa_v': cache_dsa_v, 'cache_dsa_idx_k': cache_dsa_idx_k,
            'cache_mem_k': cache_mem_k, 'cache_mem_v': cache_mem_v, 'state_gdn': state_gdn,
            'state_ret': state_ret, 'state_lru': state_lru, 'page_table': page_table,
            'mem_prompt': mem_prompt, 'w_in': w_in, 'conv_w': conv_w, 'conv_b': conv_b,
            'gdn_a_log': gdn_a_log, 'gdn_dt_bias': gdn_dt_bias, 'gdn_norm_w': gdn_norm_w,
            'lru_lambda': lru_lambda, 'lru_w_r': lru_w_r, 'lru_b_r': lru_b_r, 'lru_w_i': lru_w_i,
            'lru_b_i': lru_b_i, 'w_mem_kv': w_mem_kv, 'w_branch': w_branch, 'w_out': w_out,
            'ln_g': ln_g, 'ln_b': ln_b}

def reference(x_prompt, x_sample, cache_conv, cache_dsa_k, cache_dsa_v, cache_dsa_idx_k,
              cache_mem_k, cache_mem_v, state_gdn, state_ret, state_lru, page_table, mem_prompt,
              w_in, conv_w, conv_b, gdn_a_log, gdn_dt_bias, gdn_norm_w, lru_lambda, lru_w_r,
              lru_b_r, lru_w_i, lru_b_i, w_mem_kv, w_branch, w_out, ln_g, ln_b):
    bsz = x_prompt.shape[0]
    dt = x_prompt.dtype
    past = page_table.shape[1] * PAGE_SIZE
    xp, xs = x_prompt, x_sample
    names = ('conv', 'gdn', 'ret', 'lru', 'dsa_k', 'dsa_v', 'dsa_ik')
    acc_p = {nm: [] for nm in names + ('mem_k', 'mem_v')}
    acc_s = {nm: [] for nm in names}
    for l in range(DEPTH):
        p = {'w_in': w_in[l], 'conv_w': conv_w[l], 'conv_b': conv_b[l], 'gdn_a_log': gdn_a_log[l],
             'gdn_dt_bias': gdn_dt_bias[l], 'gdn_norm_w': gdn_norm_w[l], 'lru_lambda': lru_lambda[l],
             'lru_w_r': lru_w_r[l], 'lru_b_r': lru_b_r[l], 'lru_w_i': lru_w_i[l], 'lru_b_i': lru_b_i[l],
             'w_branch': w_branch[l], 'w_out': w_out[l], 'ln_g': ln_g[l], 'ln_b': ln_b[l]}
        mkv = mem_prompt @ w_mem_kv[l]
        mk, mv = heads(mkv[..., :BRANCH_W]), heads(mkv[..., BRANCH_W:])
        xp, st, rows = mixer_layer(
            xp, 0,
            jnp.zeros((bsz, CONV_W - 1, CONV_DIM), dt),
            jnp.zeros((bsz, N_HEADS, HEAD_DIM, HEAD_DIM), jnp.float32),
            jnp.zeros((bsz, N_HEADS, HEAD_DIM, HEAD_DIM), jnp.float32),
            jnp.zeros((bsz, BRANCH_W), jnp.float32),
            mk, mv, dsa_prompt, p)
        for nm, a in zip(names, st + rows):
            acc_p[nm].append(a)
        acc_p['mem_k'].append(mk)
        acc_p['mem_v'].append(mv)
        dsa_s = make_dsa_sample(cache_dsa_k[l], cache_dsa_v[l], cache_dsa_idx_k[l], page_table)
        xs, st, rows = mixer_layer(
            xs, past, cache_conv[l], state_gdn[l], state_ret[l], state_lru[l],
            cache_mem_k[l], cache_mem_v[l], dsa_s, p)
        for nm, a in zip(names, st + rows):
            acc_s[nm].append(a)
    return (xp, xs,
            jnp.stack(acc_p['conv']), jnp.stack(acc_p['gdn']), jnp.stack(acc_p['ret']), jnp.stack(acc_p['lru']),
            jnp.stack(acc_p['dsa_k']), jnp.stack(acc_p['dsa_v']), jnp.stack(acc_p['dsa_ik']),
            jnp.stack(acc_p['mem_k']), jnp.stack(acc_p['mem_v']),
            jnp.stack(acc_s['conv']), jnp.stack(acc_s['gdn']), jnp.stack(acc_s['ret']), jnp.stack(acc_s['lru']),
            jnp.stack(acc_s['dsa_k']), jnp.stack(acc_s['dsa_v']), jnp.stack(acc_s['dsa_ik']))


_drawn_inputs = setup_inputs


def setup_inputs(seed=0):
    import zlib

    import numpy as np

    out = dict(_drawn_inputs(seed))
    spreads = {}
    factors = {'cache_dsa_k': 8.0,
     'cache_dsa_v': 6.965,
     'cache_dsa_idx_k': 7.635,
     'cache_mem_k': 8.0,
     'cache_mem_v': 6.582,
     'gdn_norm_w': 8.0,
     'lru_b_r': 38.315,
     'lru_b_i': 32.682,
     'ln_g': 3.904,
     'ln_b': 4.17}
    for name, (base, spread) in spreads.items():
        noise = np.random.default_rng([zlib.crc32(name.encode()), seed]).standard_normal(out[name].shape)
        drawn = base * np.exp(spread * noise) if base else spread * noise
        out[name] = jnp.asarray(drawn.astype(out[name].dtype))
    for name, factor in factors.items():
        out[name] = (out[name] * factor).astype(out[name].dtype)
    return out
```

```python
import math
from contextlib import ExitStack
from collections import namedtuple

import numpy as np
import concourse.bass as bass
from concourse import mybir

ALU = mybir.AluOpType
ACT = mybir.ActivationFunctionType
AX = mybir.AxisListType
F32 = mybir.dt.float32
U32 = mybir.dt.uint32
I32 = mybir.dt.int32

P = 128
D = 2048
KC = D // P
W = 512
NH = 4
HD = 128
DEPTH = 2
NP = 256
NB = 8
T = NP + NB
NMEM = 256
PAGE = 128
NPG = 16
PAST = NPG * PAGE
IH, ID = 8, 64
KP = min(256, NP // 4)
KS = min(256, (PAST + 1) // 4)
UC = 256
CPS = W // P
SCALE = HD ** -0.5
WSCALE = (IH * ID) ** -0.5
ALPHA = (2 * DEPTH) ** 0.25
LN_EPS, NORM_EPS = 1e-5, 1e-6
BIG = 1e30
TAKEN = -2.0 ** 127
LRU_C = 8.0

GQ, GK, GV, LX, RQ, RK, RV, DQ, DK, DV, IQ, MQ, GZ, DZ, RZ, LZ, MZ = range(17)
COL = {GQ: 0, GK: 512, GV: 1024, LX: 1536, GZ: 2048, DQ: 2568, DK: 3080, DV: 3592, DZ: 4104, IQ: 4616,
       RQ: 5200, RK: 5712, RV: 6224, RZ: 6736, LZ: 7248, MQ: 7760, MZ: 8272}
COL_AB, COL_IK, COL_GATE = 2560, 5128, 8784
SLOTS = [MQ, IQ, GQ, GK, GV, DQ, DK, DV, LX, RQ, RK, RV, GZ, RZ, LZ, DZ, MZ]
ORDER = [(3, LZ), (2, RZ), (0, GZ), (4, MZ), (1, DZ)]
NSLOT = 4
MEMKV_U = 4
FIRST_U = MEMKV_U + 1
GATE_U = FIRST_U + 2 * len(SLOTS)
OUT_U = GATE_U + 8 * len(ORDER)
ALL_U = OUT_U + 8
MEM_CH, SPECIAL_CH = 8, 2


def landed(u):
    return 16 * (u // NSLOT + 1 + (u % NSLOT == MEMKV_U % NSLOT and u >= MEMKV_U))


def done(u):
    return 2 * (u + 1) + 2 * min(max(u + 1 - GATE_U, 0), OUT_U - GATE_U)


def kv_count(n, i):
    return 16 * (i // 2 + 1) if n == 0 else 16 * NB + 32 * (i // 2 + 1)


def ready(slot):
    return MEM_CH + SPECIAL_CH + CPS * (SLOTS.index(slot) + 1)


def tables():
    at, parts = {}, []

    def add(name, a):
        a = np.asarray(a, np.float32)
        if a.shape[0] < P:
            a = np.concatenate([a, np.zeros((P - a.shape[0], a.shape[1]), np.float32)])
        at[name] = (sum(p.shape[1] for p in parts), a.shape[1])
        parts.append(a)

    i = np.arange(P)
    eye = np.eye(P)
    add("ident", eye)
    add("tri", i[:, None] <= i[None, :])
    add("ones", np.ones((P, P)))

    def rot(half, heads):
        m = np.zeros((P, P))
        for h in range(heads):
            for d in range(half):
                a, b = 2 * half * h + d, 2 * half * h + half + d
                m[b, a], m[a, b] = -1.0, 1.0
        return m

    r64 = rot(ID // 2, 2)
    add("rot128", rot(HD // 2, 1))
    add("rot64", r64)
    lo = np.zeros((P, P))
    lo[:ID] = np.concatenate([eye[:ID, :ID], eye[:ID, :ID]], 1)
    hi = np.zeros((P, P))
    hi[ID:] = lo[:ID]
    rd = np.zeros((P, P))
    rd[:ID] = np.concatenate([r64[:ID, :ID], r64[:ID, :ID]], 1)
    add("dup_lo", lo)
    add("dup_hi", hi)
    add("rot_dup", rd)
    pos = np.concatenate([np.arange(NP), np.full(NB, PAST)]).astype(np.float32)
    for dim in (HD, ID):
        half = dim // 2
        inv = (np.float32(10000.0) ** (-np.arange(half, dtype=np.float32) / np.float32(half))).astype(np.float32)
        ang = (pos[None, :] * inv[:, None]).astype(np.float32)
        reps = P // half
        add(f"cos{dim}", np.tile(np.cos(ang), (reps, 1)))
        add(f"sin{dim}", np.tile(np.sin(ang), (reps, 1)))
    add("future_t", np.where(i[None, :] < i[:, None], -BIG, 0.0))
    add("zeros", np.zeros((P, P)))
    add("future", np.where(i[None, :] > i[:, None], -BIG, 0.0))
    add("never", np.full((P, P), -BIG))
    add("strict_t", i[None, :] > i[:, None])
    gamma = 1.0 - 2.0 ** (-5.0 - np.arange(NH))
    lg = np.log(gamma.astype(np.float32)).astype(np.float64)
    zeta = np.exp((NP - 1 - (np.arange(2)[None, :, None] * P + i[:, None, None])) * lg[None, None, :])
    add("zeta", zeta.reshape(P, 2 * NH))
    add("gamma", np.tile(np.repeat(np.exp(lg), NB)[None], (P, 1)))
    e8 = np.eye(NB)
    add("blk_pages", np.repeat(e8, NPG, 1))
    add("blk_heads", np.repeat(e8, IH, 1))
    add("rep_heads", np.repeat(e8, NH, 1))
    add("parity", np.stack([i < ID, i >= ID], 1))
    add("iota", np.tile(np.arange(NPG)[None], (P, 1)))
    add("eps", np.tile(np.array([[HD * NORM_EPS, NORM_EPS, LN_EPS]]), (P, 1)))
    fixed = np.concatenate(parts, 1)

    def level(s):
        same = i[:, None] // (2 * s) == i[None, :] // (2 * s)
        return same & (i[:, None] % (2 * s) >= s) & (i[None, :] % (2 * s) < s)

    lv = np.concatenate([level(1)] + [level(s).T for s in (1, 2, 4, 8, 16, 32, 64)], 1)
    k = np.arange(NP)
    dist = k[None, None, :] - i[:, None, None]
    rd = np.where(dist >= 0, np.exp(np.maximum(dist, 0) * lg[None, :, None]), 0.0)
    return fixed, at, lv.astype(np.float32), rd.reshape(P, NH * NP).astype(np.float32)


def trunk(nc, a, o, at, fixed_w):
    n_pool = a.cache_dsa_k.shape[1]
    with ExitStack() as ctx:
        def sb(name, shape, dt=F32):
            return ctx.enter_context(nc.sbuf_tensor(name, shape, dt))

        TMP = 2112
        ring = sb("ring", [P, NSLOT, KC, UC])
        bring = sb("bring", [P, 2, CPS, UC])
        xT = sb("xT", [P, KC, T])
        work = sb("work", [P, TMP + len(SLOTS) * CPS * T])
        tab = sb("tab", [P, fixed_w])
        tabs = sb("tabs", [P, 1024])
        pT = sb("pT", [P, KC, 31])
        qT = sb("qT", [P, CPS, 11])
        memkv = sb("memkv", [P, 2052])
        mkT = memkv[:, 0:NH * NMEM].rearrange("p (h m) -> p h m", h=NH)
        mvr = memkv[:, NH * NMEM:NH * NMEM + 2 * W].rearrange("p (t n) -> p t n", t=2)
        stg = sb("stg", [P, W])
        srow = memkv[0:NB, 0:PAST + 1]
        small = sb("small", [P, 1100])
        picked = sb("picked", [NB, KS], U32)
        m8 = sb("m8", [NB, 8])
        i8 = sb("i8", [NB, 8], U32)
        pm8 = sb("pm8", [P, 8])
        rowsU = sb("rowsU", [P, 2, NB], U32)
        pagesU = sb("pagesU", [P, 8], U32)
        pti = sb("pti", [P, 1 + NB * NPG], I32)

        mb = ctx.enter_context(nc.psum_tensor("mb", [P, 4, 512], F32))
        bb = ctx.enter_context(nc.psum_tensor("bb", [P, 4, 512], F32))

        def tb(name):
            o_, n = at[name]
            return tab[:, o_:o_ + n]

        ident, ones = tb("ident"), tb("ones")
        tri_ones = tab[:, at["tri"][0]:at["tri"][0] + 2 * P]
        nm = tab[:, at["future_t"][0]:at["future_t"][0] + 2 * P]
        cm = [tab[:, at["future"][0]:at["future"][0] + 2 * P], tab[:, at["zeros"][0]:at["zeros"][0] + 2 * P]]
        id8 = ident[0:NB, 0:NB]

        hbase = TMP

        def H(slot):
            b0 = hbase + slot * CPS * T
            return work[:, b0:b0 + CPS * T].rearrange("p (c n) -> p c n", n=T)

        def area(slot, off, n):
            b0 = hbase + slot * CPS * T + off
            return work[:, b0:b0 + n]

        tmpA = work[:, 0:CPS * T].rearrange("p (c n) -> p c n", n=T)
        tmpB = work[:, CPS * T:2 * CPS * T].rearrange("p (c n) -> p c n", n=T)
        tmps = [tmpA, tmpB]
        merged = work[:, hbase + LX * CPS * T:hbase + (LX + 4) * CPS * T].rearrange("p (c n) -> p c n", n=T)

        r1 = area(RQ, 0, D)
        r2 = area(RV, 0, W)
        memrow = area(DQ, 0, 2 * D).rearrange("p (t n) -> p t n", t=2)
        memT = area(GZ, 0, KC * NMEM).rearrange("p (c n) -> p c n", n=NMEM)
        xrow = memrow

        used = [0]

        def sm(n, parts=P):
            used[0] += n
            assert used[0] <= 1100
            return small[0:parts, used[0] - n:used[0]]

        abT = sm(T, NB)
        ikw = sm(T, 72)
        cols = sm(2, NB)
        negA = sm(1, NB)
        normw = sm(1)
        sp4 = sm(CPS)
        sn4 = sm(CPS)
        gbt = sm(32).rearrange("p (k t r) -> p k t r", k=2, t=2)
        gct = sm(2 * NH).rearrange("p (t h) -> p t h", t=2)
        ktl = sm(2 * NH).rearrange("p (t h) -> p t h", t=2)
        egb = sm(2 * IH * NB).rearrange("p (k h b) -> p k h b", k=2, h=IH)
        wtok = sm(2 * IH).rearrange("p (t h) -> p t h", t=2)
        wts = sm(IH, NB)
        ls = sm(64)
        pts = sm(96)
        nmx = sm(NH)
        rsm = sm(NH)
        lcount = sm(1)
        ptf = sm(1)
        goff = sm(9)
        rowf = sm(16)

        kvprod = sm(NH * NB)
        nsel = sm(1, NB)
        n88 = sm(IH, NB)
        pause = sm(1, NB)
        zT, spn, msk = (tmpA[0:NB, i_, :] for i_ in range(3))
        sln = spl = sm(CPS)
        spe, sle = spn, sln
        gate_mask, egs = msk[:, 0:128], msk[:, 128:144]

        def zarea(off, n, parts=P):
            return area(GZ, off, n)[0:parts]

        def garea(off, n, parts=P):
            return area(GQ, off, n)[0:parts]

        def heads4(ap):
            return ap.rearrange("p (h x) -> p h x", h=NH)

        def prob(n):
            return heads4((zarea, garea)[n](0, NH * NP))

        def probT(n):
            return (zarea, garea)[n](1024, 1024).rearrange("p (s h q) -> p s h q", s=2, h=NH)

        relus = garea(0, IH * NP)
        pmask = garea(2048, 2 * NP).rearrange("p (t k) -> p t k", t=2)
        pscore = garea(2560, NP)
        vrow = work[:, 0:2 * W].rearrange("p (t n) -> p t n", t=2)
        ik = zarea(0, 2048).rearrange("p (i x) -> p i x", i=2)
        ikT, ikr = zarea(2048, 1024), zarea(3072, 1024)
        lw = zarea(4096, 2 * NB * IH, NB)
        qd = zarea(4224, IH * NB).rearrange("p (h b) -> p h b", h=IH)
        dt_all = zarea(0, 1536)
        dt0, dt1 = heads4(zarea(0, 1024)), heads4(zarea(1024, 512))
        amat = ymat = heads4(zarea(1536, W))
        atm, xinv, xinvT = (heads4(zarea(o_, W)) for o_ in (2048, 2560, 3072))
        bmat, btT = (heads4(zarea(o_, W)) for o_ in (3584, 4096))

        def tri_t(t):
            return heads4(zarea(4608, W) if t == 0 else stg[:, :])

        bv = work[:, 0:1024].rearrange("p (t n) -> p t n", t=2)
        kzA = work[:, 1024:2048].rearrange("p (t n) -> p t n", t=2)
        rt0, rt1 = heads4(garea(0, 1024)), heads4(garea(1024, 512))
        rv = garea(1536, 1024).rearrange("p (t n) -> p t n", t=2)
        kzC = work[:, 0:1024].rearrange("p (t n) -> p t n", t=2)

        def sbuf(n):
            return (zarea, garea)[n](0, 2048).rearrange("p (i b e) -> p i b e", i=2, b=NB)

        def vmask(n):
            return (zarea, garea)[n](2048, 1024, NB)

        def ktok(n):
            return work[0:NB, 0:W]

        def kq(n):
            return work[:, 512:576].rearrange("p (h b k) -> p h b k", h=NH, b=NB)

        def prod(n):
            return work[:, 576:608]

        def vnew(n):
            return work[:, 608:640].rearrange("p (h b) -> p h b", h=NH)

        qkb = work[:, 640:672].rearrange("p (h b) -> p h b", h=NH)
        s8 = [work[:, 672 + 8 * i_:680 + 8 * i_] for i_ in range(2)]
        lruw = tabs[:, :].rearrange("p (i h j) -> p i h j", i=2, h=NH)

        def lru(i_):
            return H(i_) if i_ < 3 else tmpA

        kvb = garea(0, 2048).rearrange("p (i t n) -> p i t n", i=2, t=2)
        prodK = work[:, 0:1024].rearrange("p (t h d) -> p t h d", t=2, h=NH)
        qrow, lrow = work[0:NB, 1056:1568], work[0:32, 1568:1568 + KS + 1]
        maskrow = garea(2048, KS + 1, NB)
        gbuf = garea(2310, 2 * T).rearrange("p (c n) -> p c n", c=2)
        gprod = garea(2310 + 2 * T, T)
        hilo = work[0:NB, 0:2 * KS].rearrange("p (k n) -> p k n", k=2)
        hiloU = work[0:NB, 2 * KS:4 * KS].bitcast(U32).rearrange("p (k n) -> p k n", k=2)
        eqs = work[:, 0:NB * NPG].rearrange("p (b g) -> p b g", b=NB)
        KI = sb("KI", [P, T])
        Qblk = sb("Qblk", [P, P])
        ptB = sb("ptB", [P, NB * NPG])
        scs = sb("scs", [P, P])
        mws = sb("mws", [P, P])

        names = """tables x_in x_T x_ok pages_in pages_ok params_in mem_in param_T param_cols mem_T memT_ok chunk_mm stored
            small_a small_b small_c small_d small_e gt_mm gt_ok gc_mm dt_raw dt_ok tails tails_ok tail_out conv_done
            conv_act sq ss rs normed mean_mm rot_mm rot_ok ki_mm ki_ok qd_mm qd_ok new_mm new_ok ik_T ik_copied ik_mm
            ik_rel ik_sc sc_ok row_in pidx_mm pidx_rel pidx_acc topk_s tok_mm tok_ok kk_mm kk_ok bt_mm bt_ok inv_T
            inv_at at_mm lvl_bt y_mm y_ok z_mm z_ok u_mm u_ok pt_mm pt_ok o_mm st_ok st_out kq_ok qk_mm qk_ok sk_mm
            vn_ok vt_mm vm_ok op_mm s_new s_out lw_in lru_mm lru_act lru_a lru_b lru_c lru_o lru_out h_mm h_rows
            lg_mm lg_ok ex_ok pr_ok pT_mm pT_ok ov_mm y_e qr_mm qr_ok qb_mm kv_used lt_mm lt_ok lx_ok lp_ok lpt_mm
            lpt_ok sv_mm sy_ok hl_ok hl_mm rows_ok rows_out rows_mm rows_copied tab_in gate_act merged_ok out_ok
            ln_sum ln_cen ln_sq ln_ss ln_rs ln_x ln_done y_out se_ok mean_ok gtmp memv_out lc_ok decays_in v_chain a_chain
            cp_out""".split()
        sem = namedtuple("Semaphores", names)(*[ctx.enter_context(nc.semaphore(n)) for n in names])
        w_landed = [ctx.enter_context(nc.semaphore(f"w_landed{i}")) for i in range(NSLOT)]
        bw_landed = [ctx.enter_context(nc.semaphore(f"bw_landed{i}")) for i in range(2)]
        gath = [ctx.enter_context(nc.semaphore(f"gathered{i}")) for i in range(2)]
        stin = [ctx.enter_context(nc.semaphore(f"state_in{i}")) for i in range(2)]
        kv_in = [ctx.enter_context(nc.semaphore(f"kv_in{i}")) for i in range(2)]
        layer_sems = kv_in + list(sem) + w_landed + bw_landed + gath + stin

        def chain(eng, s):
            n = [0]

            def link(ins):
                n[0] += 1
                ins.then_inc(s, 1)
                eng.wait_ge(s, n[0])
            return link

        def clear_sems():
            nc.all_engine_barrier()
            nc.gpsimd.dma_reset()
            nc.all_engine_barrier()
            for s in layer_sems:
                nc.sync.sem_clear(s)
            nc.all_engine_barrier()

        with nc.Block() as block:
            @block.sync
            def _(sp):
                sp.dma_start(tab[:, :], a.fixed).then_inc(sem.tables, 16)
                sp.dma_start(xrow, a.x_prompt.rearrange("a (t p) n -> p (a t) n", p=P)).then_inc(sem.x_in, 16)
                sp.dma_start(r1[0:NB, :], a.x_sample.rearrange("b t n -> (b t) n")).then_inc(sem.x_in, 16)
                pt = a.page_table.rearrange("b g -> (b g)")
                sp.dma_start(pti[:, 0:1], pt.rearrange("(p o) -> p o", o=1)).then_inc(sem.pages_in, 16)
                sp.dma_start(pti[:, 1:], pt.partition_broadcast(P)).then_inc(sem.pages_in, 16)

            @block.tensor
            def _(pe):
                pe.wait_ge(sem.tables, 16)
                pe.wait_ge(sem.x_in, 32)
                for c in range(KC):
                    if c >= 4:
                        pe.wait_ge(sem.x_ok, c - 3)
                    for t in range(2):
                        pe.transpose(mb[:, c % 4, t * P:(t + 1) * P], xrow[:, t, c * P:(c + 1) * P], ident)
                    pe.transpose(mb[:, c % 4, NP:T], r1[0:NB, c * P:(c + 1) * P], id8).then_inc(sem.x_T, 1)

            @block.vector
            def _(dve):
                dve.memset(cols, 0.0)
                dve.memset(Qblk[:, :], 0.0)
                dve.memset(lcount, 0.0)
                dve.wait_ge(sem.pages_in, 32)
                dve.tensor_copy(ptf, pti[:, 0:1])
                dve.tensor_copy(ptB[:, :], pti[:, 1:])
                for c in range(KC):
                    dve.wait_ge(sem.x_T, c + 1)
                    dve.tensor_copy(xT[:, c, :], mb[:, c % 4, 0:T]).then_inc(sem.x_ok, 1)
        clear_sems()

        with nc.Fori(0, DEPTH) as l:
            def at_l(ap):
                n = len(ap.shape)
                rest = " ".join(f"x{i}" for i in range(1, n))
                return ap[bass.ds(l, 1)].rearrange(f"z {rest} -> (z x1) " + " ".join(f"x{i}" for i in range(2, n)))

            w_in = at_l(a.w_in).rearrange("(k p) n -> p k n", p=P)
            w_mem = at_l(a.w_mem_kv).rearrange("(k p) n -> p k n", p=P)
            w_out = at_l(a.w_out).rearrange("(k p) n -> p k n", p=P)
            w_branch = at_l(a.w_branch).rearrange("b (k p) n -> p b k n", p=P)

            with nc.Block() as block:
                @block.sync
                def _(sp):
                    sp.dma_start(r1[0:4, :], at_l(a.conv_w)).then_inc(sem.params_in, 16)
                    for i, v in enumerate((a.conv_b, a.ln_g, a.ln_b)):
                        sp.dma_start(r1[4 + i:5 + i, :], v[bass.ds(l, 1), :]).then_inc(sem.params_in, 16)
                    sp.dma_start(r1[7:31, :], at_l(a.cache_conv).rearrange("b j n -> (b j) n")).then_inc(sem.params_in, 16)
                    for i, v in enumerate((a.lru_lambda, a.lru_b_r, a.lru_b_i)):
                        sp.dma_start(r2[i:i + 1, :], v[bass.ds(l, 1), :]).then_inc(sem.params_in, 16)
                    sp.dma_start(r2[3:11, :], at_l(a.state_lru)).then_inc(sem.params_in, 16)
                    sp.dma_start(cols[0:NH, 0:1], a.gdn_dt_bias[bass.ds(l, 1), :].rearrange("z h -> h z")).then_inc(sem.params_in, 16)
                    sp.dma_start(cols[0:NH, 1:2], a.gdn_a_log[bass.ds(l, 1), :].rearrange("z h -> h z")).then_inc(sem.params_in, 16)
                    sp.dma_start(normw, a.gdn_norm_w[bass.ds(l, 1), :].rearrange("z d -> d z")).then_inc(sem.params_in, 16)
                    sp.dma_start(memrow, a.mem_prompt.rearrange("a (t p) n -> p (a t) n", p=P)).then_inc(sem.mem_in, 16)
                    sp.dma_start(tabs[:, :], a.levels).then_inc(sem.tab_in, 16)

                    def unit(u, src, dst=None):
                        if u >= NSLOT:
                            sp.wait_ge(sem.chunk_mm, done(u - NSLOT))
                        sp.dma_start(ring[:, u % NSLOT, :, :] if dst is None else dst, src).then_inc(w_landed[u % NSLOT], 16)

                    for i in range(MEMKV_U):
                        unit(i, w_mem[:, :, i * UC:(i + 1) * UC])
                    u = MEMKV_U
                    unit(u, w_in[:, :, COL_AB:COL_AB + 8], ring[:, u % NSLOT, :, 0:8])
                    sp.dma_start(ring[:, u % NSLOT, :, 8:80], w_in[:, :, COL_IK:COL_IK + 72]).then_inc(w_landed[u % NSLOT], 16)
                    for i, s in enumerate(SLOTS):
                        for k in range(2):
                            c0 = COL[s] + k * UC
                            unit(FIRST_U + 2 * i + k, w_in[:, :, c0:c0 + UC])
                    for n, (b, _) in enumerate(ORDER):
                        with sp.Fori(0, 2) as i:
                            for k in range(4):
                                u = GATE_U + 8 * n + k
                                sp.wait_ge(sem.chunk_mm, i * (done(u) - done(u - NSLOT)) + done(u - NSLOT))
                                sp.dma_start(ring[:, u % NSLOT, :, :],
                                             w_in[:, :, bass.ds(COL_GATE + b * D + k * UC + i * (4 * UC), UC)])\
                                    .then_inc(w_landed[u % NSLOT], 16)
                    with sp.Fori(0, 2) as i:
                        for k in range(4):
                            u = OUT_U + k
                            sp.wait_ge(sem.chunk_mm, i * (done(u) - done(u - NSLOT)) + done(u - NSLOT))
                            sp.dma_start(ring[:, u % NSLOT, :, :], w_out[:, :, bass.ds(k * UC + i * (4 * UC), UC)])\
                                .then_inc(w_landed[u % NSLOT], 16)

                @block.tensor
                def _(pe):
                    chunk = [0]
                    units = iter(range(FIRST_U, GATE_U))

                    def free_bank():
                        g = chunk[0]
                        chunk[0] += 1
                        if g >= 4:
                            pe.wait_ge(sem.stored, g - 3)
                        return mb[:, g % 4, :]

                    def unit():
                        u = next(units, None)
                        if u is None:
                            return
                        pe.wait_ge(w_landed[u % NSLOT], landed(u))
                        for c in range(2):
                            bank = free_bank()
                            for k in range(KC):
                                mm = pe.matmul(bank[:, 0:T], ring[:, u % NSLOT, k, c * P:(c + 1) * P], xT[:, k, :],
                                               start=(k == 0), stop=(k == KC - 1))
                            mm.then_inc(sem.chunk_mm, 1)

                    pe.wait_ge(sem.params_in, 16 * 12)
                    for c in range(KC):
                        pe.transpose(bb[:, 0, c * 31:(c + 1) * 31], r1[0:31, c * P:(c + 1) * P], ident[0:31, 0:31])
                    for c in range(CPS):
                        mm = pe.transpose(bb[:, 1, c * 11:(c + 1) * 11], r2[0:11, c * P:(c + 1) * P], ident[0:11, 0:11])
                    mm.then_inc(sem.param_T, 1)
                    pe.wait_ge(sem.mem_in, 16)
                    for t in range(2):
                        for q in range(4):
                            n = 4 * t + q
                            if n >= 4:
                                pe.wait_ge(sem.memT_ok, n - 3)
                            for c in range(4):
                                mm = pe.transpose(mb[:, n % 4, c * P:(c + 1) * P],
                                                  memrow[:, t, (4 * q + c) * P:(4 * q + c + 1) * P], ident)
                            mm.then_inc(sem.mem_T, 1)
                    pe.wait_ge(sem.memT_ok, 8)
                    for u in range(MEMKV_U):
                        pe.wait_ge(w_landed[u % NSLOT], landed(u))
                        for c in range(2):
                            bank = free_bank()
                            for k in range(KC):
                                w = ring[:, u % NSLOT, k, :]
                                if u < 2:
                                    mm = pe.matmul(bank[:, 0:NMEM], w[:, c * P:(c + 1) * P], memT[:, k, :],
                                                   start=(k == 0), stop=(k == KC - 1))
                                else:
                                    mm = pe.matmul(bank[:, 0:UC], memT[:, k, c * P:(c + 1) * P], w,
                                                   start=(k == 0), stop=(k == KC - 1))
                            mm.then_inc(sem.chunk_mm, 1)
                    u = MEMKV_U
                    pe.wait_ge(w_landed[u % NSLOT], landed(u))
                    for c0, m in ((0, 8), (8, 72)):
                        bank = free_bank()
                        for k in range(KC):
                            mm = pe.matmul(bank[0:m, 0:T], ring[:, u % NSLOT, k, c0:c0 + m], xT[:, k, :],
                                           start=(k == 0), stop=(k == KC - 1))
                        mm.then_inc(sem.chunk_mm, 1)

                    def to_rows(src, bank, cols_=(0, P)):
                        c0, c1 = cols_
                        for h in range(NH):
                            mm = pe.transpose(bb[0:c1 - c0, bank, h * P:(h + 1) * P], src[:, h, c0:c1], ident)
                        return mm

                    def attend(n, q, k, v):
                        for t in range(2):
                            if n == 0 and t == 0:
                                pe.wait_ge(sem.stored, ready(MQ))
                                pe.wait_ge(sem.rows_copied, 2)
                            for h in range(NH):
                                mm = pe.matmul(bb[:, h // 2, (h % 2) * NP:(h % 2 + 1) * NP], q[:, h, t * P:(t + 1) * P],
                                               k[:, h, 0:NP], start=True, stop=True)
                            mm.then_inc(sem.lg_mm, 1)
                            unit()
                            unit()
                            pe.wait_ge(sem.pr_ok, 2 * n + t + 1)
                            for s in range(2):
                                for h in range(NH):
                                    mm = pe.transpose(bb[:, 2 + s, h * P:(h + 1) * P],
                                                      prob(n)[:, h, s * P:(s + 1) * P], ident)
                            mm.then_inc(sem.pT_mm, 1)
                            pe.wait_ge(sem.pT_ok, 2 * n + t + 1)
                            for h in range(NH):
                                for s in range(2):
                                    mm = pe.matmul(bb[:, 0, h * P:(h + 1) * P], v[:, s, h * P:(h + 1) * P],
                                                   probT(n)[:, s, h, :], start=(s == 0), stop=(s == 1))
                            mm.then_inc(sem.ov_mm, 1)
                            pe.wait_ge(sem.y_e, 2 * n + t + 1)

                    pe.wait_ge(sem.stored, 8)
                    pe.wait_ge(sem.param_cols, 1)
                    for t in range(2):
                        to_rows(mkT, t, (t * P, (t + 1) * P)).then_inc(sem.rows_mm, 1)
                    unit()
                    unit()
                    attend(0, H(MQ), mkT, mvr)

                    pe.wait_ge(sem.small_e, 1)
                    for kind, src in enumerate((zT, abT)):
                        for t in range(2):
                            pe.transpose(bb[:, 0, (2 * kind + t) * 8:(2 * kind + t + 1) * 8],
                                         src[:, t * P:(t + 1) * P], id8)
                    mm = pe.matmul(bb[:, 1, 0:2 * IH * NB], ones[0:NB, :], gate_mask, start=True, stop=True)
                    mm.then_inc(sem.gt_mm, 1)
                    pe.wait_ge(sem.gt_ok, 1)
                    unit()
                    unit()

                    def rotate(n, slot, mat):
                        pe.wait_ge(sem.stored, ready(slot))
                        for c in range(CPS):
                            mm = pe.matmul(bb[:, c, 0:T], mat, H(slot)[:, c, :], start=True, stop=True)
                        mm.then_inc(sem.rot_mm, 1)

                    rotate(0, IQ, tb("rot64"))
                    pe.wait_ge(sem.rot_ok, 1)
                    pe.matmul(bb[:, 0, 0:T], tb("dup_lo")[0:ID, :], ikw[0:ID, :], start=True, stop=True)
                    pe.matmul(bb[:, 1, 0:T], tb("rot_dup")[0:ID, :], ikw[0:ID, :], start=True, stop=True)
                    for t in range(3):
                        m = P if t < 2 else NB
                        mm = pe.transpose(bb[0:m, 2, t * 72:(t + 1) * 72], ikw[0:72, t * P:t * P + m], ident[0:72, 0:72])
                    mm.then_inc(sem.ki_mm, 1)

                    for c in range(CPS):
                        for k, name in enumerate(("dup_lo", "dup_hi")):
                            j = 2 * c + k
                            pe.matmul(bb[:, 3, j * NB:(j + 1) * NB], tb(name), H(IQ)[:, c, NP:T], start=True, stop=True)
                    pe.wait_ge(sem.ki_ok, 1)
                    mm = pe.matmul(bb[:, 0, 0:P], lw, tb("blk_pages")[0:NB, :], start=True, stop=True)
                    mm.then_inc(sem.qd_mm, 1)
                    pe.wait_ge(sem.qd_ok, 1)
                    for j in range(IH):
                        mm = pe.matmul(bb[0:NB, 1, j * NB:(j + 1) * NB], qd[0:ID, j, :], KI[0:ID, NP:T], start=True, stop=True)
                    mm.then_inc(sem.new_mm, 1)
                    for j in range(8):
                        pe.wait_ge(gath[j % 2], 16 * (j // 2 + 1))
                        if j == 0:
                            pe.wait_ge(sem.new_ok, 1)
                        for u in range(8):
                            mm = pe.transpose(bb[:, u // 4, (u % 4) * P:(u % 4 + 1) * P], ik[:, j % 2, u * P:(u + 1) * P], ident)
                        mm.then_inc(sem.ik_T, 1)
                        pe.wait_ge(sem.ik_copied, j + 1)
                        for u in range(2):
                            mm = pe.matmul(bb[:, 2 + u, :], Qblk[:, :], ikT[:, u * 512:(u + 1) * 512], start=True, stop=True)
                        mm.then_inc(sem.ik_mm, 1)
                        pe.wait_ge(sem.ik_rel, j + 1)
                        for u in range(8):
                            mm = pe.matmul(bb[:, 0, 2 * u:2 * u + 2], ikr[:, u * P:(u + 1) * P], tb("parity"), start=True, stop=True)
                        mm.then_inc(sem.ik_sc, 1)
                        pe.wait_ge(sem.sc_ok, j + 1)
                        if j % 4 == 3:
                            unit()

                    pe.matmul(bb[:, 0, 0:NH], tri_ones[:, 0:P], gbt[:, 0, 0, 0:NH], start=True, stop=True)
                    pe.matmul(bb[:, 0, NH:2 * NH], ones, gbt[:, 0, 0, 0:NH], start=True, stop=False)
                    pe.matmul(bb[:, 0, NH:2 * NH], tri_ones[:, 0:P], gbt[:, 0, 1, 0:NH], start=False, stop=True)
                    for h in range(NH):
                        b_, c0 = 1 + h // 2, (h % 2) * NP
                        pe.matmul(bb[:, b_, c0:c0 + NP], gbt[:, 0, 0, h:h + 1].to_broadcast([P, P]), tri_ones,
                                  start=True, stop=False)
                        mm = pe.matmul(bb[:, b_, c0 + P:c0 + NP], gbt[:, 0, 1, h:h + 1].to_broadcast([P, P]),
                                       tri_ones[:, 0:P], start=False, stop=True)
                    mm.then_inc(sem.gc_mm, 1)

                    pe.wait_ge(sem.dt_raw, 1)

                    def tail(i, s):
                        pe.wait_ge(sem.stored, ready(s))
                        if i:
                            pe.wait_ge(sem.tails_ok, i)
                        for c in range(CPS):
                            mm = pe.transpose(bb[0:11, 0, c * P:(c + 1) * P], H(s)[:, c, NP - 3:T], ident)
                        mm.then_inc(sem.tails, 1)

                    def ones_sum(n, src):
                        pe.wait_ge(sem.sq, n)
                        for c in range(CPS):
                            mm = pe.matmul(bb[:, c, 0:T], ones, src[:, c, :], start=True, stop=True)
                        mm.then_inc(sem.ss, 1)

                    for i, s in enumerate((GQ, GK, GV)):
                        tail(i, s)
                        unit()
                    pe.wait_ge(sem.tails_ok, 3)
                    ones_sum(1, tmpA)
                    unit()
                    pe.wait_ge(sem.normed, 1)
                    ones_sum(2, tmpA)
                    unit()
                    pe.wait_ge(sem.normed, 2)

                    def inner_scores(n, kk, qq):
                        for h in range(NH):
                            pe.matmul(bb[:, h // 2, (h % 2) * NP:(h % 2 + 1) * NP], kk[:, h, 0:P], qq[:, h, 0:NP],
                                      start=True, stop=True)
                            mm = pe.matmul(bb[:, 2, h * P:(h + 1) * P], kk[:, h, P:NP], qq[:, h, P:NP], start=True, stop=True)
                        mm.then_inc(sem.pt_mm, 1)

                    def out_and_state(n, pt0, pt1, v0, v1, kz):
                        for h in range(NH):
                            b_, c0, hs = h // 2, (h % 2) * NP, slice(h * P, (h + 1) * P)
                            pe.matmul(bb[:, b_, c0:c0 + NP], v0[:, hs], pt0[:, h, :], start=True, stop=False)
                            pe.matmul(bb[:, b_, c0 + P:c0 + NP], v1[:, hs], pt1[:, h, :], start=False, stop=True)
                        for h in range(NH):
                            hs = slice(h * P, (h + 1) * P)
                            pe.matmul(bb[:, 2, hs], kz[:, 0, hs], v0[:, hs], start=True, stop=False)
                            mm = pe.matmul(bb[:, 2, hs], kz[:, 1, hs], v1[:, hs], start=False, stop=True)
                        mm.then_inc(sem.o_mm, 1)

                    gq, gk, gv = H(GQ), H(GK), H(GV)
                    for t in range(2):
                        to_rows(gv, t, (t * P, (t + 1) * P))
                        mm = to_rows(gk, 2 + t, (t * P, (t + 1) * P))
                    mm.then_inc(sem.tok_mm, 1)
                    pe.wait_ge(sem.tok_ok, 1)
                    for t in range(2):
                        for h in range(NH):
                            ks = gk[:, h, t * P:(t + 1) * P]
                            pe.matmul(bb[:, t, h * P:(h + 1) * P], ks, ks, start=True, stop=True)
                    for h in range(NH):
                        mm = pe.matmul(bb[:, 2, h * P:(h + 1) * P], gk[:, h, 0:P], gk[:, h, P:NP], start=True, stop=True)
                    mm.then_inc(sem.kk_mm, 1)
                    for t in range(2):
                        pe.wait_ge(sem.kk_ok, t + 1)
                        for h in range(NH):
                            mm = pe.transpose(bb[:, 3, h * P:(h + 1) * P], tri_t(t)[:, h, :], ident)
                        mm.then_inc(sem.inv_T, 1)
                        unit()
                        pe.wait_ge(sem.inv_at, t + 1)
                        for h in range(NH):
                            mm = pe.transpose(bb[:, 3, h * P:(h + 1) * P], amat[:, h, :], ident)
                        mm.then_inc(sem.at_mm, 1)
                        for lv in range(6):
                            n = 6 * t + lv
                            pe.wait_ge(sem.lvl_bt, n + 1)
                            for h in range(NH):
                                mm = pe.matmul(bb[:, 3, h * P:(h + 1) * P], bmat[:, h, :], xinv[:, h, :], start=True, stop=True)
                            mm.then_inc(sem.y_mm, 1)
                            pe.wait_ge(sem.y_ok, n + 1)
                            for h in range(NH):
                                pe.matmul(bb[:, 0, h * P:(h + 1) * P], ymat[:, h, :], xinvT[:, h, :], start=True, stop=True)
                                mm = pe.matmul(bb[:, 3, h * P:(h + 1) * P], xinvT[:, h, :], ymat[:, h, :], start=True, stop=True)
                            mm.then_inc(sem.z_mm, 1)
                            if lv in (1, 3, 5):
                                unit()
                        pe.wait_ge(sem.z_ok, 6 * (t + 1))
                        if t == 1:
                            for h in range(NH):
                                mm = pe.matmul(bb[:, 3, h * P:(h + 1) * P], btT[:, h, :], bv[:, 0, h * P:(h + 1) * P],
                                               start=True, stop=True)
                            mm.then_inc(sem.bt_mm, 1)
                            pe.wait_ge(sem.bt_ok, 1)
                        for h in range(NH):
                            mm = pe.matmul(bb[:, 3, h * P:(h + 1) * P], xinvT[:, h, :], bv[:, t, h * P:(h + 1) * P],
                                           start=True, stop=True)
                        mm.then_inc(sem.u_mm, 1)
                        pe.wait_ge(sem.u_ok, t + 1)
                    inner_scores(0, gk, gq)
                    pe.wait_ge(sem.pt_ok, 1)
                    out_and_state(0, dt0, dt1, bv[:, 0, :], bv[:, 1, :], kzA)

                    def samples_step(n, kslot, qslot, vslot):
                        pe.wait_ge(sem.kq_ok, n + 1)
                        pe.matmul(bb[:, 0, 0:NH * NB], ones, prod(n), start=True, stop=True)
                        mm = to_rows(H(kslot), 1, (NP, T))
                        mm.then_inc(sem.qk_mm, 1)
                        pe.wait_ge(sem.qk_ok, n + 1)
                        for h in range(NH):
                            m = NH * n + h
                            pe.wait_ge(stin[h % 2], 16 * (m // 2 + 1))
                            for b in range(NB):
                                mm = pe.matmul(bb[:, 0, 2 * b:2 * b + 2], sbuf(n)[:, h % 2, b, :], kq(n)[:, h, b, :],
                                               start=True, stop=True)
                            mm.then_inc(sem.sk_mm, 1)
                            pe.wait_ge(sem.vn_ok, m + 1)
                            pe.transpose(bb[0:NB, 1, 0:P], vnew(n)[:, h, :], ident).then_inc(sem.vt_mm, 1)
                            pe.wait_ge(sem.vm_ok, m + 1)
                            for j in range(2):
                                mm = pe.matmul(bb[:, 2 + j, :], ktok(n)[:, h * P:(h + 1) * P], vmask(n)[:, 512 * j:512 * (j + 1)],
                                               start=True, stop=True)
                            mm.then_inc(sem.op_mm, 1)
                        pe.wait_ge(sem.s_new, NH * (n + 1))

                    pe.wait_ge(sem.st_ok, 1)
                    samples_step(0, GK, GQ, GV)
                    ones_sum(3, tmpA)
                    for _ in range(3):
                        unit()
                    pe.wait_ge(sem.normed, 3)

                    for n, s in enumerate((RQ, RK)):
                        rotate(1 + n, s, tb("rot128"))
                        unit()
                        pe.wait_ge(sem.rot_ok, 2 + n)
                    for t in range(2):
                        to_rows(H(RV), t, (t * P, (t + 1) * P))
                        mm = to_rows(H(RK), 2 + t, (t * P, (t + 1) * P))
                    mm.then_inc(sem.tok_mm, 1)
                    unit()
                    pe.wait_ge(sem.tok_ok, 2)
                    inner_scores(1, H(RK), H(RQ))
                    pe.wait_ge(sem.pt_ok, 2)
                    out_and_state(1, rt0, rt1, rv[:, 0, :], rv[:, 1, :], kzC)
                    unit()
                    pe.wait_ge(sem.st_ok, 2)
                    samples_step(1, RK, RQ, RV)
                    for c in range(CPS):
                        mm = pe.matmul(bb[:, c, 0:T], ones, H(RQ)[:, c, :], start=True, stop=True)
                    mm.then_inc(sem.mean_mm, 1)
                    ones_sum(4, tmpA)
                    pe.wait_ge(sem.normed, 4)

                    tail(3, LX)
                    pe.wait_ge(sem.tails_ok, 4)
                    pe.wait_ge(sem.conv_act, 4)
                    pe.wait_ge(sem.lw_in, 32)
                    for i in range(2):
                        if i:
                            pe.wait_ge(sem.lru_act, 1)
                        for h in range(NH):
                            mm = pe.matmul(bb[:, h, 0:T], lruw[:, i, h, :], H(LX)[:, h, :], start=True, stop=True)
                        mm.then_inc(sem.lru_mm, 1)
                    for _ in range(4):
                        unit()
                    pe.wait_ge(sem.lru_act, 2)
                    pe.wait_ge(sem.lru_o, 1)
                    for h in range(NH):
                        mm = pe.transpose(bb[0:NB + 1, 0, h * P:(h + 1) * P], H(LX)[:, h, NP - 1:T], ident)
                    mm.then_inc(sem.h_mm, 1)

                    pe.wait_ge(sem.h_rows, 1)
                    for n, s in enumerate((DQ, DK)):
                        rotate(3 + n, s, tb("rot128"))
                        pe.wait_ge(sem.rot_ok, 4 + n)
                    for n, s in enumerate((DK, DV)):
                        for t in range(3):
                            if 3 * n + t:
                                pe.wait_ge(sem.rows_copied, 2 + 3 * n + t)
                            to_rows(H(s), 0, (t * P, t * P + P) if t < 2 else (NP, T)).then_inc(sem.rows_mm, 1)
                    pe.wait_ge(sem.rows_copied, 8)
                    for t in range(3):
                        m = P if t < 2 else NB
                        mm = pe.transpose(bb[0:m, 0, t * ID:(t + 1) * ID], KI[0:ID, t * P:t * P + m], ident[0:ID, 0:ID])
                    mm.then_inc(sem.rows_mm, 1)
                    pe.wait_ge(sem.rows_copied, 9)
                    for t in range(2):
                        if t:
                            pe.wait_ge(sem.pidx_rel, 1)
                        for j in range(IH):
                            p0 = ID * (j % 2)
                            mm = pe.matmul(bb[:, 2 * (j % 2) + j // 4, (j // 2 % 2) * NP:(j // 2 % 2 + 1) * NP],
                                           H(IQ)[p0:p0 + ID, j // 2, t * P:(t + 1) * P], KI[p0:p0 + ID, 0:NP],
                                           start=True, stop=True)
                        mm.then_inc(sem.pidx_mm, 1)
                    pe.wait_ge(sem.pidx_rel, 2)
                    attend(1, H(DQ), H(DK), vrow)

                    def sample_attend(n, qslot):
                        to_rows(H(qslot), 0, (NP, T)).then_inc(sem.qr_mm, 1)
                        pe.wait_ge(sem.qr_ok, n + 1)
                        for b in range(NB):
                            if b >= 2:
                                pe.wait_ge(sem.kv_used, NB * n + b - 1)
                            pe.matmul(bb[:, b % 2, :], id8[:, b:b + 1].to_broadcast([NB, P]), qrow, start=True, stop=True)\
                                .then_inc(sem.qb_mm, 1)
                        pe.wait_ge(sem.lx_ok, n + 1)
                        if n:
                            pe.matmul(bb[0:32, 2, 0:KS + 1], tb("rep_heads")[0:NB, :], maskrow, start=True, stop=True,
                                      skip_group_check=True)
                        for t in range(2):
                            mm = pe.matmul(bb[0:32, 2, t * P:(t + 1) * P], ls[:, 32 * t:32 * t + 32], ident,
                                           start=(n == 0), stop=True, skip_group_check=True)
                        if n:
                            mm = pe.matmul(bb[0:32, 2, KS:KS + 1], kvprod, ones[:, 0:1], start=False, stop=True,
                                           skip_group_check=True)
                        mm.then_inc(sem.lt_mm, 1)
                        pe.wait_ge(sem.lp_ok, n + 1)
                        for t in range(2):
                            mm = pe.transpose(bb[:, 3, 32 * t:32 * t + 32], lrow[:, t * P:(t + 1) * P], ident[0:32, 0:32])
                        if n:
                            mm = pe.matmul(bb[:, 3, 64:96], lrow[:, KS:KS + 1].to_broadcast([32, P]), ident[0:32, 0:32],
                                           start=True, stop=True)
                        mm.then_inc(sem.lpt_mm, 1)
                        pe.wait_ge(sem.lpt_ok, n + 1)
                        for b in range(NB):
                            pe.wait_ge(kv_in[b % 2], kv_count(n, NB + b))
                            for h in range(NH):
                                j = b * NH + h
                                for t in range(2):
                                    mm = pe.matmul(bb[:, 0, j:j + 1], kvb[:, b % 2, t, h * P:(h + 1) * P],
                                                   pts[:, 32 * t + j:32 * t + j + 1], start=(t == 0), stop=(t == 1))
                            mm.then_inc(sem.sv_mm, 1)
                        pe.wait_ge(sem.sy_ok, n + 1)

                    def gates(n, y):
                        with pe.Fori(0, 2) as i:
                            for k in range(4):
                                u = GATE_U + 8 * n + k
                                pe.wait_ge(w_landed[u % NSLOT], i * 16 + landed(u))
                                for c in range(2):
                                    if n == 0 and k == 0 and c == 0:
                                        pe.wait_ge(sem.stored, ready(SLOTS[-1]))
                                    pe.wait_ge(sem.gate_act, i * 8 + 2 * (8 * n + k) + c + 1)
                                    for q in range(KC):
                                        mm = pe.matmul(mb[:, c, 0:T], ring[:, u % NSLOT, q, c * P:(c + 1) * P], xT[:, q, :],
                                                       start=(q == 0), stop=(q == KC - 1))
                                    mm.then_inc(sem.chunk_mm, 1)
                                pe.wait_ge(bw_landed[k % 2], i * 32 + 16 * (4 * n + k // 2 + 1))
                                for c in range(2):
                                    pe.wait_ge(sem.merged_ok, i * 8 + 2 * (8 * n + k) + c + 1)
                                    for q in range(CPS):
                                        mm = pe.matmul(mb[:, 2 + c, 0:T], bring[:, k % 2, q, c * P:(c + 1) * P], y[:, q, :],
                                                       start=(q == 0), stop=(q == CPS - 1))
                                    mm.then_inc(sem.chunk_mm, 1)

                    sample_attend(0, MQ)
                    for n in range(4):
                        gates(n, H(ORDER[n][1]))
                    pe.wait_ge(sem.hl_ok, 1)
                    for k in range(2):
                        for t in range(2):
                            j = 2 * k + t
                            mm = pe.transpose(bb[:, 0, j * NB:(j + 1) * NB], hilo[:, k, t * P:(t + 1) * P], id8)
                    mm.then_inc(sem.hl_mm, 1)
                    pe.wait_ge(sem.rows_ok, 1)
                    sample_attend(1, DQ)
                    gates(4, H(ORDER[4][1]))

                    pe.wait_ge(sem.merged_ok, 2 + 2 * 8 * len(ORDER))
                    with pe.Fori(0, 2) as i:
                        for k in range(4):
                            u = OUT_U + k
                            pe.wait_ge(w_landed[u % NSLOT], i * 16 + landed(u))
                            for c in range(2):
                                m = 2 * k + c
                                pe.wait_ge(sem.out_ok, i * 8 + m + 1)
                                for q in range(KC):
                                    mm = pe.matmul(mb[:, m % 4, 0:T], ring[:, u % NSLOT, q, c * P:(c + 1) * P], merged[:, q, :],
                                                   start=(q == 0), stop=(q == KC - 1))
                                mm.then_inc(sem.chunk_mm, 1)
                    pe.wait_ge(sem.out_ok, 4 + KC)
                    for q in range(KC):
                        mm = pe.matmul(bb[:, 0, 0:T], ones, xT[:, q, :], start=(q == 0), stop=(q == KC - 1))
                    mm.then_inc(sem.ln_sum, 1)
                    for q in range(4):
                        pe.wait_ge(sem.ln_sq, q + 1)
                        for c in range(4):
                            mm = pe.matmul(bb[:, 1, 0:T], ones, tmps[q % 2][:, c, :], start=(q + c == 0), stop=(q + c == 6))
                        mm.then_inc(sem.ln_ss, 1)

                @block.scalar
                def _(act):
                    ch = chain(act, sem.a_chain)
                    chunk = [0]

                    def result():
                        g = chunk[0]
                        chunk[0] += 1
                        act.wait_ge(sem.chunk_mm, g + 1)
                        return mb[:, g % 4, :]

                    store_n = iter(range(2 * len(SLOTS)))

                    def unit():
                        n = next(store_n, None)
                        if n is None:
                            return
                        s = SLOTS[n // 2]
                        if s == GZ and n % 2 == 0:
                            act.wait_ge(sem.s_out, 16 * NH)
                        for c in range(2):
                            act.activation(H(s)[:, 2 * (n % 2) + c, :], result()[:, 0:T],
                                           ACT.Silu if s in (GZ, DZ, RZ, LZ, MZ) else ACT.Copy).then_inc(sem.stored, 1)

                    for u in range(MEMKV_U):
                        for c in range(2):
                            dst = mkT[:, 2 * u + c, :] if u < 2 else mvr[:, c, (u - 2) * UC:(u - 1) * UC]
                            act.activation(dst, result()[:, 0:UC], ACT.Copy).then_inc(sem.stored, 1)
                    act.activation(abT, result()[0:NB, 0:T], ACT.Copy).then_inc(sem.stored, 1)
                    act.activation(ikw[0:72, :], result()[0:72, 0:T], ACT.Copy).then_inc(sem.stored, 1)
                    unit()
                    unit()

                    def attend(n):
                        for t in range(2):
                            unit()
                            unit()
                            act.wait_ge(sem.lg_ok, 2 * n + t + 1)
                            for h in range(NH):
                                mm = act.activation(prob(n)[:, h, :], prob(n)[:, h, :], ACT.Exp, bias=nmx[:, h:h + 1],
                                                    accum_out=rsm[:, h:h + 1])
                            mm.then_inc(sem.ex_ok, 1)
                            act.wait_ge(sem.pT_mm, 2 * n + t + 1)
                            act.activation(probT(n).rearrange("p s h q -> p (s h q)"),
                                           bb[:, 2:4, :].rearrange("p s x -> p (s x)"), ACT.Copy).then_inc(sem.pT_ok, 1)

                    attend(0)
                    act.wait_ge(sem.small_a, 1)
                    act.activation(spe, spn, ACT.Exp, scale=-1.0)
                    act.activation(sle, sln, ACT.Exp, scale=-1.0)
                    ch(act.activation(negA, cols[:, 1:2], ACT.Exp))
                    act.activation(spe, spe, ACT.Ln, bias=1.0)
                    act.activation(sle, sle, ACT.Ln, bias=1.0)
                    act.activation(abT, abT, ACT.Sigmoid).then_inc(sem.small_b, 1)
                    act.wait_ge(sem.small_c, 1)
                    act.activation(egs[:, 0:8], zT[:, NP:T], ACT.Exp).then_inc(sem.small_d, 1)
                    unit()
                    unit()
                    for j in range(8):
                        act.wait_ge(sem.ik_T, j + 1)
                        act.activation(ikT, bb[:, 0:2, :].rearrange("p s x -> p (s x)"), ACT.Copy).then_inc(sem.ik_copied, 1)
                        if j % 4 == 3:
                            unit()

                    def conv_out(i, s):
                        act.wait_ge(sem.conv_done, i + 1)
                        act.activation(H(s), tmps[i % 2], ACT.Silu if s != LX else ACT.Copy).then_inc(sem.conv_act, 1)

                    def squares(n, src):
                        act.activation(tmpA, src, ACT.Square).then_inc(sem.sq, 1)

                    def roots(n, scale, eps):
                        act.wait_ge(sem.ss, n)
                        mm = act.activation(tmpA, bb[:, :, 0:T], ACT.Sqrt, scale=scale, bias=eps)
                        mm.then_inc(sem.rs, 1)

                    act.wait_ge(sem.dt_raw, 1)
                    act.activation(dt_all, dt_all, ACT.Exp)
                    act.activation(ktl.rearrange("p t h -> p (t h)"), ktl.rearrange("p t h -> p (t h)"), ACT.Exp)\
                        .then_inc(sem.dt_ok, 1)
                    eps = tb("eps")
                    for i, s in enumerate((GQ, GK, GV)):
                        unit()
                        conv_out(i, s)
                    act.wait_ge(sem.conv_act, 3)
                    squares(1, H(GQ))
                    unit()
                    roots(1, float(HD), eps[:, 0:1])
                    act.wait_ge(sem.normed, 1)
                    squares(2, H(GK))
                    unit()
                    roots(2, 1.0, eps[:, 1:2])
                    for t in range(2):
                        unit()
                        for lv in range(6):
                            n = 6 * t + lv
                            act.wait_ge(sem.y_mm, n + 1)
                            act.activation(ymat.rearrange("p h x -> p (h x)"), bb[:, 3, :], ACT.Copy).then_inc(sem.y_ok, 1)
                            if lv in (1, 3, 5):
                                unit()
                    act.wait_ge(sem.s_new, NH)
                    squares(3, H(GQ))
                    for _ in range(3):
                        unit()
                    roots(3, 1.0 / HD, eps[:, 1:2])
                    unit()
                    unit()
                    unit()
                    unit()
                    act.wait_ge(sem.mean_ok, 1)
                    squares(4, H(RQ))
                    roots(4, 1.0 / HD, eps[:, 2:3])
                    conv_out(3, LX)
                    act.wait_ge(sem.s_out, 16 * 2 * NH)
                    for i in range(2):
                        act.wait_ge(sem.lru_mm, i + 1)
                        for h in range(CPS):
                            mm = act.activation(lru(i)[:, h, :], bb[:, h, 0:T], ACT.Sigmoid, bias=qT[:, h, 1 + i:2 + i])
                        mm.then_inc(sem.lru_act, 1)
                    for _ in range(4):
                        unit()
                    for h in range(CPS):
                        act.activation(lru(2)[:, h, :], lru(0)[:, h, :], ACT.Exp, scale=sn4[:, h:h + 1])
                        mm = act.activation(lru(3)[:, h, :], lru(0)[:, h, :], ACT.Tanh, scale=sp4[:, h:h + 1])
                    mm.then_inc(sem.lru_a, 1)
                    act.wait_ge(sem.lru_b, 1)
                    act.activation(lru(0), lru(0), ACT.Sqrt).then_inc(sem.lru_c, 1)
                    for t in range(2):
                        act.wait_ge(sem.pidx_mm, t + 1)
                        if t:
                            act.wait_ge(sem.pidx_acc, 1)
                        act.activation(relus, bb[:, :, :].rearrange("p s x -> p (s x)"), ACT.Relu).then_inc(sem.pidx_rel, 1)
                    attend(1)

                    def sample_exp(n, w):
                        act.wait_ge(sem.lt_ok, n + 1)
                        act.activation(lrow[:, 0:w], lrow[:, 0:w], ACT.Exp, bias=nmx[0:32, 0:1],
                                       accum_out=rsm[0:32, 0:1]).then_inc(sem.se_ok, 1)

                    sample_exp(0, KS)
                    act.sem_inc(sem.gate_act, 2)

                    def gates(n):
                        with act.Fori(0, 2) as i:
                            for k in range(4):
                                u = GATE_U + 8 * n + k
                                act.wait_ge(sem.chunk_mm, i * (done(u + 2) - done(u - 2)) + done(u - 2))
                                act.dma_start(bring[:, k % 2, :, :],
                                              w_branch[:, ORDER[n][0], :, bass.ds(k * UC + i * (4 * UC), UC)])\
                                    .then_inc(bw_landed[k % 2], 16)
                                for c in range(2):
                                    act.wait_ge(sem.chunk_mm, i * 16 + (done(u - 1) + c + 1))
                                    act.wait_ge(sem.merged_ok, i * 8 + 2 * (8 * n + k) + c + 1)
                                    act.activation(gbuf[:, c, :], mb[:, c, 0:T], ACT.Sigmoid).then_inc(sem.gate_act, 1)

                    for n in range(4):
                        gates(n)
                    sample_exp(1, KS + 1)
                    gates(4)
                    for q in range(4):
                        act.wait_ge(sem.ln_cen, q + 1)
                        if q >= 2:
                            act.wait_ge(sem.ln_ss, q - 1)
                        act.activation(tmps[q % 2], xT[:, 4 * q:4 * q + 4, :], ACT.Square).then_inc(sem.ln_sq, 1)
                    act.wait_ge(sem.ln_ss, 4)
                    act.activation(tmpA[:, 0, :], bb[:, 1, 0:T], ACT.Sqrt, scale=1.0 / D, bias=eps[:, 2:3]).then_inc(sem.ln_rs, 1)
                    for q in range(KC):
                        act.wait_ge(sem.ln_x, q // 4 + 1)
                        act.activation(xT[:, q, :], xT[:, q, :], ACT.Identity, scale=pT[:, q, 5:6], bias=pT[:, q, 6:7])\
                            .then_inc(sem.ln_done, 1)

                @block.vector
                def _(dve):
                    v = chain(dve, sem.v_chain)

                    def bc(ap, n):
                        return ap.unsqueeze(2).to_broadcast([ap.shape[0], ap.shape[1], n])

                    def bh(ap, n=NH):
                        return ap.unsqueeze(1).to_broadcast([ap.shape[0], n, ap.shape[1]])

                    dve.wait_ge(sem.param_T, 1)
                    v(dve.tensor_copy(pT[:, :, :].rearrange("p c r -> p (c r)"), bb[:, 0, 0:KC * 31]))
                    dve.tensor_copy(qT[:, :, :].rearrange("p c r -> p (c r)"), bb[:, 1, 0:CPS * 11]).then_inc(sem.param_cols, 1)
                    dve.wait_ge(sem.param_cols, 1)
                    for t in range(2):
                        for q in range(4):
                            dve.wait_ge(sem.mem_T, 4 * t + q + 1)
                            dve.tensor_copy(memT[:, 4 * q:4 * q + 4, t * P:(t + 1) * P], heads4(mb[:, q, :])).then_inc(sem.memT_ok, 1)
                    v(dve.tensor_scalar(goff[:, 8:9], lcount, float(n_pool * 8), None, ALU.mult))
                    v(dve.scalar_tensor_tensor(goff[:, 8:9], ptf, 8.0, goff[:, 8:9], ALU.mult, ALU.add))
                    v(dve.tensor_scalar(goff[:, 0:8], tb("iota")[:, 0:8], goff[:, 8:9], None, ALU.add))
                    dve.tensor_copy(pagesU[:, :], goff[:, 0:8]).then_inc(sem.pages_ok, 1)
                    for t in range(2):
                        dve.wait_ge(sem.rows_mm, t + 1)
                        if t:
                            dve.wait_ge(sem.rows_out, 16)
                        dve.tensor_copy(stg[:, :], bb[:, t, :]).then_inc(sem.rows_copied, 1)

                    def attend(n):
                        for t in range(2):
                            dve.wait_ge(sem.lg_mm, 2 * n + t + 1)
                            pr = prob(n)
                            if n == 0:
                                v(dve.tensor_scalar(pr, bb[:, 0:2, :].rearrange("p s (x k) -> p (s x) k", k=NP), SCALE, None, ALU.mult))
                            else:
                                for j in range(2):
                                    v(dve.scalar_tensor_tensor(pr[:, 2 * j:2 * j + 2, :], bb[:, j, :].rearrange("p (x k) -> p x k", k=NP),
                                                               SCALE, bh(pmask[:, t, :], 2), ALU.mult, ALU.add))
                            dve.tensor_reduce(nmx, pr, AX.X, ALU.max, negate=True).then_inc(sem.lg_ok, 1)
                            dve.wait_ge(sem.ex_ok, 2 * n + t + 1)
                            v(dve.reciprocal(rsm, rsm))
                            dve.tensor_tensor(pr, pr, bc(rsm, NP), ALU.mult).then_inc(sem.pr_ok, 1)
                            dve.wait_ge(sem.ov_mm, 2 * n + t + 1)
                            c = slice(t * P, (t + 1) * P)
                            if n == 0:
                                dve.tensor_copy(H(MQ)[:, :, c], heads4(bb[:, 0, :])).then_inc(sem.y_e, 1)
                            else:
                                dve.tensor_tensor(H(DZ)[:, :, c], H(DZ)[:, :, c], heads4(bb[:, 0, :]), ALU.mult).then_inc(sem.y_e, 1)

                    attend(0)
                    dve.wait_ge(sem.stored, MEM_CH + SPECIAL_CH)
                    lam = qT[:, :, 0]
                    v(dve.tensor_scalar(zT, abT, cols[:, 0:1], None, ALU.add))
                    v(dve.scalar_tensor_tensor(spn, zT, -1.0, zT, ALU.mult, ALU.max))
                    dve.scalar_tensor_tensor(sln, lam, -1.0, lam, ALU.mult, ALU.max).then_inc(sem.small_a, 1)
                    dve.wait_ge(sem.small_b, 1)
                    v(dve.scalar_tensor_tensor(zT, zT, 0.0, spn, ALU.max, ALU.add))
                    v(dve.tensor_scalar(negA, negA, -1.0, None, ALU.mult))
                    v(dve.tensor_scalar(zT, zT, negA, None, ALU.mult))
                    v(dve.tensor_scalar(sp4, lam, -1.0, 0.0, ALU.mult, ALU.max))
                    v(dve.tensor_tensor(sp4, sp4, sln, ALU.add))
                    v(dve.tensor_scalar(sn4, sp4, -LRU_C, None, ALU.mult))
                    dve.tensor_scalar(sp4, sp4, LRU_C, None, ALU.mult).then_inc(sem.small_c, 1)
                    dve.wait_ge(sem.small_d, 1)
                    v(dve.tensor_copy(egs[:, 8:16], abT[:, NP:T]))
                    for k in range(2):
                        mm = dve.tensor_tensor(gate_mask[:, 64 * k:64 * k + 64].rearrange("p (r b) -> p r b", r=IH),
                                               bh(egs[:, 8 * k:8 * k + 8], IH), bc(id8, NB), ALU.mult)
                        if k == 0:
                            v(mm)
                    mm.then_inc(sem.small_e, 1)
                    dve.wait_ge(sem.gt_mm, 1)
                    v(dve.tensor_copy(gbt.rearrange("p k t r -> p (k t r)"), bb[:, 0, 0:32]))
                    dve.tensor_copy(egb.rearrange("p k h b -> p (k h b)"), bb[:, 1, 0:128]).then_inc(sem.gt_ok, 1)
                    dve.wait_ge(sem.gt_ok, 1)

                    def rotate(n, slot, dim, scale=1.0):
                        dve.wait_ge(sem.rot_mm, n + 1)
                        v(dve.scalar_tensor_tensor(tmpA, bb[:, :, 0:T], scale, bh(tb(f"sin{dim}")), ALU.mult, ALU.mult))
                        v(dve.scalar_tensor_tensor(H(slot), H(slot), scale, bh(tb(f"cos{dim}")), ALU.mult, ALU.mult))
                        dve.tensor_tensor(H(slot), H(slot), tmpA, ALU.add).then_inc(sem.rot_ok, 1)
                        dve.wait_ge(sem.rot_ok, n + 1)

                    rotate(0, IQ, ID)
                    dve.wait_ge(sem.ki_mm, 1)
                    v(dve.tensor_tensor(KI[:, :], bb[:, 0, 0:T], tb("cos64"), ALU.mult))
                    v(dve.tensor_tensor(tmpA[:, 0, :], bb[:, 1, 0:T], tb("sin64"), ALU.mult))
                    v(dve.tensor_tensor(KI[:, :], KI[:, :], tmpA[:, 0, :], ALU.add))
                    for t in range(2):
                        v(dve.tensor_scalar(wtok[:, t, :], bb[:, 2, t * 72 + ID:(t + 1) * 72], WSCALE, None, ALU.mult))
                    v(dve.tensor_scalar(wts, bb[0:NB, 2, 2 * 72 + ID:3 * 72], WSCALE, None, ALU.mult))
                    for k in range(2):
                        mm = dve.tensor_tensor(lw[:, 64 * k:64 * k + 64].rearrange("p (b h) -> p b h", b=NB), bh(wts, NB),
                                               tb("blk_heads")[0:NB, :].rearrange("p (b h) -> p b h", b=NB), ALU.mult)
                        if k == 0:
                            v(mm)
                    mm.then_inc(sem.ki_ok, 1)
                    dve.wait_ge(sem.qd_mm, 1)
                    v(dve.tensor_copy(qd.rearrange("p h b -> p (h b)"), bb[:, 3, 0:64]))
                    for k in range(2):
                        half = slice(ID * k, ID * (k + 1))
                        v(dve.tensor_copy(Qblk[half, 64 * k:64 * k + 64].rearrange("p (b h) -> p h b", b=NB),
                                          bb[half, 3, 0:64].rearrange("p (h b) -> p h b", h=IH)))
                    dve.tensor_copy(mws[:, :], bb[:, 0, 0:P]).then_inc(sem.qd_ok, 1)
                    dve.wait_ge(sem.new_mm, 1)
                    dve.wait_ge(sem.memv_out, 16)
                    new = tmpA[0:NB, 1, 0:64].rearrange("p (h b) -> p h b", h=IH)
                    v(dve.scalar_tensor_tensor(new, bb[0:NB, 1, 0:64].rearrange("p (h b) -> p h b", h=IH), 0.0, bh(id8, IH), ALU.max, ALU.mult))
                    v(dve.tensor_reduce(n88, new, AX.X, ALU.add))
                    v(dve.tensor_tensor(n88, n88, wts, ALU.mult))
                    dve.tensor_reduce(srow[:, PAST:PAST + 1], n88, AX.X, ALU.add).then_inc(sem.new_ok, 1)
                    for j in range(8):
                        dve.wait_ge(sem.ik_mm, j + 1)
                        dve.scalar_tensor_tensor(ikr.rearrange("p (u x) -> p u x", u=8), bb[:, 2:4, :].rearrange("p s (u x) -> p (s u) x", x=P),
                                                 0.0, bh(mws[:, :], 8), ALU.max, ALU.mult).then_inc(sem.ik_rel, 1)
                        dve.wait_ge(sem.ik_sc, j + 1)
                        dve.tensor_copy(scs[:, 16 * j:16 * j + 16], bb[:, 0, 0:16]).then_inc(sem.sc_ok, 1)
                    dve.wait_ge(sem.gc_mm, 1)
                    v(dve.tensor_copy(gct.rearrange("p t h -> p (t h)"), bb[:, 0, 0:2 * NH]))
                    gcb = bb[:, 1:3, :].rearrange("p s (x n) -> p (s x) n", n=NP)
                    for h in range(NH):
                        v(dve.scalar_tensor_tensor(dt0[:, h, :], gcb[:, h, :], gct[:, 0, h:h + 1], nm, ALU.subtract, ALU.add))
                        v(dve.scalar_tensor_tensor(dt1[:, h, :], gcb[:, h, P:NP], gct[:, 1, h:h + 1], nm[:, 0:P], ALU.subtract, ALU.add))
                    v(dve.tensor_tensor(ktl[:, 0, :], gcb[:, :, NP - 1], gct[:, 0, :], ALU.subtract))
                    dve.tensor_tensor(ktl[:, 1, :], gcb[:, :, NP - 1], gct[:, 1, :], ALU.subtract).then_inc(sem.dt_raw, 1)

                    def topk(first, n):
                        with dve.Fori(0, n) as r:
                            c0 = 4 * first
                            dve.max(m8[:, :], srow).then_inc(sem.topk_s, 1)
                            dve.wait_ge(sem.topk_s, r * 4 + (c0 + 1))
                            dve.memset(pause, 0.0)
                            dve.max_index(i8[:, :], m8[:, :], srow).then_inc(sem.topk_s, 1)
                            dve.match_replace(srow, m8[:, :], srow, TAKEN).then_inc(sem.topk_s, 1)
                            dve.wait_ge(sem.topk_s, r * 4 + (c0 + 3))
                            dve.tensor_copy(picked[:, bass.ds(r * 8 + 8 * first, 8)], i8[:, :]).then_inc(sem.topk_s, 1)
                            dve.wait_ge(sem.topk_s, r * 4 + (c0 + 4))
                            dve.memset(pause, 0.0)

                    ROUNDS = KS // 8

                    def conv(i, s):
                        dve.wait_ge(sem.stored, ready(s))
                        dve.wait_ge(sem.tails, i + 1)
                        if i == 0:
                            dve.wait_ge(sem.rows_out, 32)
                        elif i < 3:
                            dve.wait_ge(sem.tail_out, 32 * i)
                        else:
                            dve.wait_ge(sem.st_out, 32)
                        dve.tensor_copy(stg[0:11, :], bb[0:11, 0, :]).then_inc(sem.tails_ok, 1)
                        if i >= 2:
                            dve.wait_ge(sem.conv_act, i - 1)
                        out = tmps[i % 2]
                        for c in range(CPS):
                            q = CPS * s + c
                            x, y = H(s)[:, c, :], out[:, c, :]
                            v(dve.tensor_scalar(y, x, pT[:, q, 3:4], pT[:, q, 4:5], ALU.mult, ALU.add))
                            for k in range(1, 4):
                                wk = pT[:, q, 3 - k:4 - k]
                                v(dve.scalar_tensor_tensor(y[:, k:NP], x[:, 0:NP - k], wk, y[:, k:NP], ALU.mult, ALU.add))
                                mm = dve.scalar_tensor_tensor(y[:, NP:T], pT[:, q, 7 + 3 - k:31:3], wk, y[:, NP:T], ALU.mult, ALU.add)
                                if (c, k) != (CPS - 1, 3):
                                    v(mm)
                        mm.then_inc(sem.conv_done, 1)

                    def normed(n, s):
                        dve.wait_ge(sem.rs, n)
                        v(dve.reciprocal(tmpA, tmpA))
                        dve.tensor_tensor(H(s), H(s), tmpA, ALU.mult).then_inc(sem.normed, 1)
                        dve.wait_ge(sem.normed, n)

                    for i, s in enumerate((GQ, GK, GV)):
                        conv(i, s)
                    normed(1, GQ)
                    normed(2, GK)

                    dve.wait_ge(sem.tok_mm, 1)
                    dve.wait_ge(sem.dt_ok, 1)
                    for t in range(2):
                        v(dve.tensor_tensor(heads4(bv[:, t, :]), heads4(bb[:, t, :]), bc(gbt[:, 1, t, NH:2 * NH], P), ALU.mult))
                        mm = dve.tensor_tensor(heads4(kzA[:, t, :]), heads4(bb[:, 2 + t, :]), bc(ktl[:, t, :], P), ALU.mult)
                        if t == 0:
                            v(mm)
                    mm.then_inc(sem.tok_ok, 1)
                    dve.wait_ge(sem.kk_mm, 1)
                    dve.wait_ge(sem.tail_out, 96)
                    strict = bh(tb("strict_t"))
                    v(dve.tensor_tensor(btT, heads4(bb[:, 2, :]), dt0[:, :, P:NP], ALU.mult))
                    for t in range(2):
                        v(dve.tensor_tensor(tri_t(t), heads4(bb[:, t, :]), (dt0[:, :, 0:P], dt1)[t], ALU.mult))
                        dve.tensor_tensor(tri_t(t), tri_t(t), strict, ALU.mult).then_inc(sem.kk_ok, 1)
                    dve.wait_ge(sem.tab_in, 16)

                    def mask(i):
                        return bh(tabs[:, i * P:(i + 1) * P])

                    for t in range(2):
                        beta = bc(gbt[:, 1, t, NH:2 * NH], P)
                        dve.wait_ge(sem.inv_T, t + 1)
                        dve.tensor_tensor(amat, heads4(bb[:, 3, :]), beta, ALU.mult).then_inc(sem.inv_at, 1)
                        dve.wait_ge(sem.inv_at, t + 1)
                        v(dve.tensor_tensor(xinv, amat, mask(0), ALU.mult))
                        v(dve.tensor_tensor(xinv, bh(ident), xinv, ALU.subtract))
                        dve.wait_ge(sem.at_mm, t + 1)
                        v(dve.tensor_copy(atm, heads4(bb[:, 3, :])))
                        v(dve.tensor_tensor(xinvT, atm, mask(1), ALU.mult))
                        v(dve.tensor_tensor(xinvT, bh(ident), xinvT, ALU.subtract))
                        for lv in range(6):
                            n = 6 * t + lv
                            dve.tensor_tensor(bmat, atm, mask(2 + lv), ALU.mult).then_inc(sem.lvl_bt, 1)
                            dve.wait_ge(sem.z_mm, n + 1)
                            if lv < 5:
                                v(dve.tensor_tensor(xinv, xinv, heads4(bb[:, 3, :]), ALU.subtract))
                            dve.tensor_tensor(xinvT, xinvT, heads4(bb[:, 0, :]), ALU.subtract).then_inc(sem.z_ok, 1)
                            dve.wait_ge(sem.z_ok, n + 1)
                        if t == 1:
                            dve.wait_ge(sem.bt_mm, 1)
                            v(dve.tensor_tensor(bmat, heads4(bb[:, 3, :]), beta, ALU.mult))
                            dve.tensor_tensor(heads4(bv[:, 1, :]), heads4(bv[:, 1, :]), bmat, ALU.subtract).then_inc(sem.bt_ok, 1)
                        dve.wait_ge(sem.u_mm, t + 1)
                        dve.tensor_copy(bv[:, t, :], bb[:, 3, :]).then_inc(sem.u_ok, 1)
                    dve.wait_ge(sem.pt_mm, 1)
                    two = bb[:, 0:2, :].rearrange("p s (x n) -> p (s x) n", n=NP)
                    v(dve.tensor_tensor(dt0, dt0, two, ALU.mult))
                    dve.tensor_tensor(dt1, dt1, heads4(bb[:, 2, :]), ALU.mult).then_inc(sem.pt_ok, 1)
                    dve.wait_ge(sem.o_mm, 1)
                    v(dve.tensor_copy(H(GQ)[:, :, 0:NP], two))
                    dve.tensor_copy(stg[:, :], bb[:, 2, :]).then_inc(sem.st_ok, 1)

                    def samples_step(n, kslot, qslot, vslot):
                        ks, qs, vs = (H(s)[:, :, NP:T] for s in (kslot, qslot, vslot))
                        v(dve.tensor_copy(kq(n)[:, :, :, 0], ks))
                        v(dve.tensor_copy(kq(n)[:, :, :, 1], qs))
                        dve.tensor_tensor(prod(n).rearrange("p (h b) -> p h b", h=NH), ks, qs, ALU.mult).then_inc(sem.kq_ok, 1)
                        dve.wait_ge(sem.qk_mm, n + 1)
                        v(dve.tensor_copy(qkb.rearrange("p h b -> p (h b)"), bb[:, 0, 0:NH * NB]))
                        dve.tensor_copy(ktok(n), bb[0:NB, 1, :]).then_inc(sem.qk_ok, 1)
                        gam = egb[:, 0, 0:NH, :] if n == 0 else tb("gamma").rearrange("p (h b) -> p h b", h=NH)
                        for h in range(NH):
                            m = NH * n + h
                            eg = gam[:, h, :]
                            dve.wait_ge(sem.sk_mm, m + 1)
                            sk = bb[:, 0, 0:2 * NB].rearrange("p (b k) -> p b k", k=2)
                            if n == 0:
                                v(dve.tensor_tensor(s8[0], sk[:, :, 0], eg, ALU.mult))
                                v(dve.tensor_tensor(s8[0], vs[:, h, :], s8[0], ALU.subtract))
                                dve.tensor_tensor(vnew(n)[:, h, :], s8[0], egb[:, 1, NH + h, :], ALU.mult).then_inc(sem.vn_ok, 1)
                            else:
                                dve.tensor_copy(vnew(n)[:, h, :], vs[:, h, :]).then_inc(sem.vn_ok, 1)
                            dve.wait_ge(sem.vn_ok, m + 1)
                            v(dve.tensor_tensor(s8[0], sk[:, :, 1], eg, ALU.mult))
                            v(dve.tensor_tensor(s8[1], qkb[:, h, :], vnew(n)[:, h, :], ALU.mult))
                            v(dve.tensor_tensor(qs[:, h, :], s8[0], s8[1], ALU.add))
                            S = sbuf(n)[:, h % 2, :, :]
                            dve.wait_ge(stin[h % 2], 16 * (m // 2 + 1))
                            v(dve.tensor_tensor(S, S, bc(eg, HD), ALU.mult))
                            dve.wait_ge(sem.vt_mm, m + 1)
                            dve.tensor_tensor(vmask(n).rearrange("p (b e) -> p b e", b=NB), bh(bb[0:NB, 1, 0:P], NB), bc(id8, P), ALU.mult)\
                                .then_inc(sem.vm_ok, 1)
                            dve.wait_ge(sem.op_mm, m + 1)
                            dve.tensor_tensor(S, S, bb[:, 2:4, :].rearrange("p s (b e) -> p (s b) e", e=HD), ALU.add).then_inc(sem.s_new, 1)

                    samples_step(0, GK, GQ, GV)
                    dve.wait_ge(sem.rs, 3)
                    v(dve.reciprocal(tmpA, tmpA))
                    v(dve.scalar_tensor_tensor(H(GQ), H(GQ), normw, tmpA, ALU.mult, ALU.mult))
                    dve.wait_ge(sem.stored, ready(GZ))
                    dve.tensor_tensor(H(GZ), H(GZ), H(GQ), ALU.mult).then_inc(sem.normed, 1)
                    dve.wait_ge(sem.normed, 3)
                    dve.wait_ge(sem.row_in, 16)
                    topk(0, ROUNDS // 4)

                    rotate(1, RQ, HD)
                    rotate(2, RK, HD, SCALE)
                    dve.wait_ge(sem.tok_mm, 2)
                    for t in range(2):
                        v(dve.tensor_copy(rv[:, t, :], bb[:, t, :]))
                        mm = dve.tensor_tensor(heads4(kzC[:, t, :]), heads4(bb[:, 2 + t, :]), bc(tb("zeta")[:, NH * t:NH * t + NH], P), ALU.mult)
                        if t == 0:
                            v(mm)
                    mm.then_inc(sem.tok_ok, 1)
                    dve.wait_ge(sem.pt_mm, 2)
                    dve.wait_ge(sem.decays_in, 16)
                    rdm = heads4(tabs[:, :])
                    v(dve.tensor_tensor(rt0, two, rdm, ALU.mult))
                    dve.tensor_tensor(rt1, heads4(bb[:, 2, :]), rdm[:, :, 0:P], ALU.mult).then_inc(sem.pt_ok, 1)
                    dve.wait_ge(sem.o_mm, 2)
                    v(dve.tensor_copy(H(RQ)[:, :, 0:NP], two))
                    dve.wait_ge(sem.st_out, 16)
                    dve.tensor_copy(stg[:, :], bb[:, 2, :]).then_inc(sem.st_ok, 1)
                    samples_step(1, RK, RQ, RV)
                    dve.wait_ge(sem.mean_mm, 1)
                    dve.scalar_tensor_tensor(H(RQ), bb[:, :, 0:T], -1.0 / HD, H(RQ), ALU.mult, ALU.add).then_inc(sem.mean_ok, 1)
                    normed(4, RQ)
                    dve.wait_ge(sem.stored, ready(RZ))
                    v(dve.tensor_tensor(H(RZ), H(RZ), H(RQ), ALU.mult))
                    topk(ROUNDS // 4, ROUNDS // 4)

                    conv(3, LX)
                    dve.wait_ge(sem.lru_act, 2)
                    v(dve.tensor_tensor(lru(1), lru(1), H(LX), ALU.mult))
                    dve.wait_ge(sem.lru_a, 1)
                    v(dve.tensor_scalar(lru(0), lru(3), 1.0, None, ALU.add))
                    v(dve.reciprocal(lru(0), lru(0)))
                    dve.scalar_tensor_tensor(lru(0), lru(3), 2.0, lru(0), ALU.mult, ALU.mult).then_inc(sem.lru_b, 1)
                    dve.wait_ge(sem.lru_c, 1)
                    v(dve.tensor_tensor(lru(1), lru(1), lru(0), ALU.mult))
                    for c in range(CPS):
                        v(dve.tensor_tensor_scan(H(LX)[:, c, 0:NP], lru(2)[:, c, 0:NP], lru(1)[:, c, 0:NP], 0.0, ALU.mult, ALU.add))
                    v(dve.tensor_tensor(H(LX)[:, :, NP:T], lru(2)[:, :, NP:T], qT[:, :, 3:11], ALU.mult))
                    dve.tensor_tensor(H(LX)[:, :, NP:T], H(LX)[:, :, NP:T], lru(1)[:, :, NP:T], ALU.add).then_inc(sem.lru_o, 1)
                    dve.wait_ge(sem.lru_o, 1)
                    dve.wait_ge(sem.stored, ready(LZ))
                    v(dve.tensor_tensor(H(LZ), H(LZ), H(LX), ALU.mult))
                    dve.wait_ge(sem.h_mm, 1)
                    dve.wait_ge(sem.tail_out, 128)
                    dve.tensor_copy(stg[0:NB + 1, :], bb[0:NB + 1, 0, :]).then_inc(sem.h_rows, 1)

                    rotate(3, DQ, HD)
                    rotate(4, DK, HD)
                    dve.wait_ge(sem.lru_out, 32)
                    for j in range(7):
                        dve.wait_ge(sem.rows_mm, 3 + j)
                        if j and j not in (4,):
                            dve.wait_ge(sem.rows_out, 32 + 16 * j)
                        m = NB if j in (2, 5) else P
                        if j < 6:
                            dst = vrow[:, j - 3, :] if j in (3, 4) else stg[0:m, :]
                            dve.tensor_copy(dst, bb[0:m, 0, :]).then_inc(sem.rows_copied, 1)
                        else:
                            v(dve.tensor_copy(stg[:, 0:2 * ID], bb[:, 0, 0:2 * ID]))
                            dve.tensor_copy(stg[0:NB, 2 * ID:3 * ID], bb[0:NB, 0, 2 * ID:3 * ID]).then_inc(sem.rows_copied, 1)
                    for t in range(2):
                        dve.wait_ge(sem.pidx_rel, t + 1)
                        v(dve.scalar_tensor_tensor(pscore, relus[:, 0:NP], wtok[:, t, 0:1], cm[t], ALU.mult, ALU.add))
                        for j in range(1, IH):
                            mm = dve.scalar_tensor_tensor(pscore, relus[:, (4 * (j % 2) + j // 2) * NP:][:, 0:NP], wtok[:, t, j:j + 1], pscore, ALU.mult, ALU.add)
                            if j < IH - 1:
                                v(mm)
                        mm.then_inc(sem.pidx_acc, 1)
                        dve.wait_ge(sem.pidx_acc, t + 1)
                        for r in range(KP // 8):
                            v(dve.max(pm8[:, :], pscore))
                            v(dve.match_replace(pscore, pm8[:, :], pscore, TAKEN))
                        v(dve.tensor_scalar(pmask[:, t, :], pscore, TAKEN, None, ALU.is_equal))
                        v(dve.tensor_scalar(pmask[:, t, :], pmask[:, t, :], -1.0, BIG, ALU.add, ALU.mult))
                        v(dve.tensor_tensor(pmask[:, t, :], pmask[:, t, :], cm[t], ALU.add))
                    attend(1)
                    topk(ROUNDS // 2, ROUNDS // 4)

                    def sample_attend(n):
                        w = KS + n
                        dve.wait_ge(sem.qr_mm, n + 1)
                        if n:
                            v(dve.tensor_tensor(kvprod.rearrange("p (b h) -> p h b", b=NB), H(DK)[:, :, NP:T], H(DQ)[:, :, NP:T], ALU.mult))
                        dve.tensor_copy(qrow, bb[0:NB, 0, :]).then_inc(sem.qr_ok, 1)
                        for b in range(NB):
                            dve.wait_ge(sem.qb_mm, NB * n + b + 1)
                            dve.wait_ge(kv_in[b % 2], kv_count(n, b))
                            for t in range(2):
                                mm = dve.tensor_tensor(prodK[:, t, :, :].rearrange("p h d -> p (h d)"), kvb[:, b % 2, t, :],
                                                       bb[:, b % 2, :], ALU.mult)
                            mm.then_inc(sem.kv_used, 1)
                            dve.wait_ge(sem.kv_used, NB * n + b + 1)
                            mm = dve.tensor_reduce(ls.rearrange("p (t b h) -> p t b h", t=2, b=NB)[:, :, b, :], prodK, AX.X, ALU.add)
                            if b < NB - 1:
                                v(mm)
                        mm.then_inc(sem.lx_ok, 1)
                        dve.wait_ge(sem.lt_mm, n + 1)
                        v(dve.tensor_scalar(lrow[:, 0:w], bb[0:32, 2, 0:w], SCALE, None, ALU.mult))
                        dve.tensor_reduce(nmx[0:32, 0:1], lrow[:, 0:w], AX.X, ALU.max, negate=True).then_inc(sem.lt_ok, 1)
                        dve.wait_ge(sem.se_ok, n + 1)
                        v(dve.reciprocal(rsm[0:32, 0:1], rsm[0:32, 0:1]))
                        dve.tensor_scalar(lrow[:, 0:w], lrow[:, 0:w], rsm[0:32, 0:1], None, ALU.mult).then_inc(sem.lp_ok, 1)
                        dve.wait_ge(sem.lpt_mm, n + 1)
                        dve.tensor_copy(pts[:, 0:64 + 32 * n], bb[:, 3, 0:64 + 32 * n]).then_inc(sem.lpt_ok, 1)
                        dve.wait_ge(sem.lpt_ok, n + 1)
                        dve.wait_ge(sem.sv_mm, NB * (n + 1))
                        ov = bb[:, 0, 0:32].rearrange("p (b h) -> p h b", b=NB)
                        if n == 0:
                            v(dve.tensor_tensor(H(MZ)[:, :, 0:NP], H(MZ)[:, :, 0:NP], H(MQ)[:, :, 0:NP], ALU.mult))
                            dve.tensor_tensor(H(MZ)[:, :, NP:T], H(MZ)[:, :, NP:T], ov, ALU.mult).then_inc(sem.sy_ok, 1)
                        else:
                            pn = pts[:, 64:96].rearrange("p (b h) -> p h b", b=NB)
                            v(dve.tensor_tensor(pn, pn, H(DV)[:, :, NP:T], ALU.mult))
                            v(dve.tensor_tensor(pn, pn, ov, ALU.add))
                            dve.tensor_tensor(H(DZ)[:, :, NP:T], H(DZ)[:, :, NP:T], pn, ALU.mult).then_inc(sem.sy_ok, 1)
                        dve.wait_ge(sem.sy_ok, n + 1)

                    sample_attend(0)
                    topk(3 * ROUNDS // 4, ROUNDS // 4)
                    v(dve.tensor_scalar(hiloU[:, 0, :], picked[:, :], 7, None, ALU.logical_shift_right))
                    v(dve.tensor_scalar(hiloU[:, 1, :], picked[:, :], PAGE - 1, None, ALU.bitwise_and))
                    v(dve.tensor_copy(hilo, hiloU))
                    v(dve.tensor_scalar(maskrow[:, 0:KS], hilo[:, 0, :], float(NPG), -BIG, ALU.is_equal, ALU.mult))
                    v(dve.tensor_reduce(nsel, maskrow[:, 0:KS], AX.X, ALU.min))
                    dve.tensor_scalar(maskrow[:, KS:KS + 1], nsel, -1.0, -BIG, ALU.mult, ALU.add).then_inc(sem.hl_ok, 1)

                    dve.sem_inc(sem.merged_ok, 2)

                    def gates(n):
                        with dve.Fori(0, 2) as i:
                            for k in range(4):
                                u = GATE_U + 8 * n + k
                                for c in range(2):
                                    m = 2 * (8 * n + k) + c
                                    dve.wait_ge(sem.gate_act, i * 8 + (m + 3))
                                    dve.wait_ge(sem.chunk_mm, i * 16 + (done(u - 1) + 2 + c + 1))
                                    dst = merged[:, bass.ds(i * 8 + (2 * k + c), 1), :].rearrange("p c n -> p (c n)")
                                    if n == 0:
                                        dve.tensor_tensor(dst, gbuf[:, c, :], mb[:, 2 + c, 0:T], ALU.mult).then_inc(sem.merged_ok, 1)
                                    else:
                                        dve.wait_ge(sem.merged_ok, i * 8 + (m + 2))
                                        dve.tensor_tensor(gprod, gbuf[:, c, :], mb[:, 2 + c, 0:T], ALU.mult).then_inc(sem.gtmp, 1)
                                        dve.wait_ge(sem.gtmp, i * 8 + (m - 16 + 1))
                                        dve.tensor_tensor(dst, dst, gprod, ALU.add).then_inc(sem.merged_ok, 1)

                    for n in range(4):
                        gates(n)
                    dve.wait_ge(sem.hl_mm, 1)
                    hl = bb[:, 0, 0:32].rearrange("p (k t b) -> p k t b", k=2, t=2)
                    v(dve.tensor_scalar(goff[:, 8:9], lcount, float(n_pool * PAGE), None, ALU.mult))
                    for t in range(2):
                        v(dve.tensor_tensor(eqs, bh(tb("iota"), NB), bc(hl[:, 0, t, :], NPG), ALU.is_equal))
                        v(dve.tensor_tensor(eqs, eqs, ptB[:, :].rearrange("p (b g) -> p b g", b=NB), ALU.mult))
                        v(dve.tensor_reduce(rowf[:, NB * t:NB * t + NB], eqs, AX.X, ALU.add))
                    v(dve.scalar_tensor_tensor(rowf, rowf, float(PAGE), bb[:, 0, 16:32], ALU.mult, ALU.add))
                    v(dve.tensor_scalar(rowf, rowf, goff[:, 8:9], None, ALU.add))
                    dve.tensor_copy(rowsU[:, :, :].rearrange("p t b -> p (t b)"), rowf).then_inc(sem.rows_ok, 1)
                    sample_attend(1)
                    gates(4)

                    dve.sem_inc(sem.out_ok, 4)
                    with dve.Fori(0, 2) as i:
                        for m in range(8):
                            dve.wait_ge(sem.chunk_mm, i * 8 + (done(OUT_U - 1) + m + 1))
                            x = xT[:, bass.ds(i * 8 + m, 1), :].rearrange("p c n -> p (c n)")
                            dve.scalar_tensor_tensor(x, x, ALPHA, mb[:, m % 4, 0:T], ALU.mult, ALU.add).then_inc(sem.out_ok, 1)
                    dve.wait_ge(sem.ln_sum, 1)
                    for q in range(4):
                        x4 = xT[:, 4 * q:4 * q + 4, :]
                        dve.scalar_tensor_tensor(x4, bh(bb[:, 0, 0:T]), -1.0 / D, x4, ALU.mult, ALU.add).then_inc(sem.ln_cen, 1)
                    dve.wait_ge(sem.ln_rs, 1)
                    dve.wait_ge(sem.ln_cen, 4)
                    v(dve.reciprocal(tmpA[:, 0, :], tmpA[:, 0, :]))
                    for q in range(4):
                        x4 = xT[:, 4 * q:4 * q + 4, :]
                        dve.tensor_tensor(x4, x4, bh(tmpA[:, 0, :]), ALU.mult).then_inc(sem.ln_x, 1)
                    dve.tensor_scalar(lcount, lcount, 1.0, None, ALU.add).then_inc(sem.lc_ok, 1)

                @block.gpsimd
                def _(pool):
                    def flat(ap):
                        return at_l(ap).rearrange("b t h d -> (b t) (h d)")

                    outs = []

                    def put(dst, src, s):
                        pool.dma_start(dst, src).then_inc(s, 16)

                    for t in range(2):
                        pool.wait_ge(sem.rows_copied, t + 1)
                        put(flat(o.p_mem_k)[t * P:(t + 1) * P, :], stg[:, :], sem.rows_out)
                    pool.wait_ge(sem.stored, MEM_CH)
                    put(flat(o.p_mem_v).rearrange("(t p) n -> p t n", p=P), mvr, sem.memv_out)
                    pool.wait_ge(sem.y_e, 2)
                    pool.wait_ge(sem.pages_ok, 1)
                    ikp = a.cache_dsa_idx_k.rearrange("l g (j t) d -> (l g j) (t d)", j=8)
                    for j in range(8):
                        if j >= 2:
                            pool.wait_ge(sem.ik_T, j - 1)
                        pool.indirect_dma_start(ik[:, j % 2, :], None, ikp, bass.IndirectOffsetOnAxis(ap=pagesU[:, j:j + 1], axis=0))\
                            .then_inc(gath[j % 2], 16)
                    pool.wait_ge(sem.sc_ok, 8)
                    for b in range(NB):
                        pass
                    pool.dma_start(srow[:, 0:PAST], scs[:, :]).then_inc(sem.row_in, 16)

                    def tail(i, s):
                        pool.wait_ge(sem.tails_ok, i + 1)
                        c = slice(s * W, (s + 1) * W)
                        put(at_l(o.p_conv).rearrange("b j n -> (b j) n")[:, c], stg[0:3, :], sem.tail_out)
                        put(at_l(o.s_conv)[:, 2, c], stg[3:11, :], sem.tail_out)

                    for i, s in enumerate((GQ, GK, GV)):
                        tail(i, s)
                    put(at_l(o.s_conv)[:, 0:2, :], at_l(a.cache_conv)[:, 1:3, :], sem.cp_out)
                    pool.wait_ge(sem.z_ok, 12)
                    pool.dma_start(tabs[:, :], a.decays).then_inc(sem.decays_in, 16)

                    def states(n, src, pdst, dst):
                        pool.wait_ge(sem.st_ok, n + 1)
                        put(at_l(pdst).rearrange("b h d e -> d (b h) e"), heads4(stg[:, :]), sem.st_out)
                        s_in, s_to = (at_l(x).rearrange("b h d e -> d h b e") for x in (src, dst))
                        for h in range(2):
                            pool.dma_start(sbuf(n)[:, h, :, :], s_in[:, h, :, :]).then_inc(stin[h], 16)
                        for h in range(NH):
                            m = NH * n + h
                            pool.wait_ge(sem.s_new, m + 1)
                            put(s_to[:, h, :, :], sbuf(n)[:, h % 2, :, :], sem.s_out)
                            if h + 2 < NH:
                                pool.wait_ge(sem.s_out, 16 * (m + 1))
                                pool.dma_start(sbuf(n)[:, h % 2, :, :], s_in[:, h + 2, :, :]).then_inc(stin[h % 2], 16)

                    states(0, a.state_gdn, o.p_gdn, o.s_gdn)
                    pool.wait_ge(sem.pt_ok, 2)
                    for i, w in enumerate((a.lru_w_r, a.lru_w_i)):
                        pool.dma_start(lruw[:, i, :, :], at_l(w).rearrange("h i j -> i h j")).then_inc(sem.lw_in, 16)
                    states(1, a.state_ret, o.p_ret, o.s_ret)
                    tail(3, LX)
                    pool.wait_ge(sem.h_rows, 1)
                    put(o.p_lru[bass.ds(l, 1)].rearrange("z b n -> (z b) n"), stg[0:1, :], sem.lru_out)
                    put(at_l(o.s_lru), stg[1:NB + 1, :], sem.lru_out)
                    for j in range(6):
                        pool.wait_ge(sem.rows_copied, 3 + j)
                        pd, sd = (o.p_dsa_k, o.s_dsa_k) if j < 3 else (o.p_dsa_v, o.s_dsa_v)
                        t = j % 3
                        if t < 2:
                            put(flat(pd)[t * P:(t + 1) * P, :], stg[:, :] if j < 3 else vrow[:, t, :], sem.rows_out)
                        else:
                            put(flat(sd), stg[0:NB, :], sem.rows_out)
                    pool.wait_ge(sem.rows_copied, 9)
                    for t in range(2):
                        put(at_l(o.p_dsa_ik).rearrange("b t d -> (b t) d")[t * P:(t + 1) * P, :], stg[:, t * ID:(t + 1) * ID], sem.rows_out)
                    put(at_l(o.s_dsa_ik).rearrange("b t d -> (b t) d"), stg[0:NB, 2 * ID:3 * ID], sem.rows_out)

                    def kv_loads(n, k_src, v_src):
                        for kind, src in enumerate((k_src, v_src)):
                            for b in range(NB):
                                if kind == 0 and b < 2:
                                    if n:
                                        pool.wait_ge(sem.sv_mm, NB - 1 + b)
                                    else:
                                        pool.wait_ge(sem.y_e, 4)
                                elif kind == 0:
                                    pool.wait_ge(sem.kv_used, NB * n + b - 1)
                                elif b < 2:
                                    pool.wait_ge(sem.kv_used, NB * n + NB - 1 + b)
                                else:
                                    pool.wait_ge(sem.sv_mm, NB * n + b - 1)
                                if n == 0:
                                    pool.dma_start(kvb[:, b % 2, :, :], src[b].rearrange("(t p) h d -> p t (h d)", p=P))\
                                        .then_inc(kv_in[b % 2], 16)
                                else:
                                    for t in range(2):
                                        pool.indirect_dma_start(kvb[:, b % 2, t, :], None, src,
                                                                bass.IndirectOffsetOnAxis(ap=rowsU[:, t, b:b + 1], axis=0))\
                                            .then_inc(kv_in[b % 2], 16)

                    kv_loads(0, at_l(a.cache_mem_k), at_l(a.cache_mem_v))
                    pool.wait_ge(sem.rows_ok, 1)
                    kv_loads(1, a.cache_dsa_k.rearrange("l g t h d -> (l g t) (h d)"), a.cache_dsa_v.rearrange("l g t h d -> (l g t) (h d)"))
                    for s, n in ((sem.rows_out, 32 + 16 * 9), (sem.memv_out, 16), (sem.tail_out, 128), (sem.cp_out, 16),
                                 (sem.st_out, 32), (sem.s_out, 128), (sem.lru_out, 32)):
                        pool.wait_ge(s, n)
                    for s, n in ((gath[0], 64), (gath[1], 64), (sem.row_in, 16), (sem.lw_in, 32), (sem.decays_in, 16),
                                 (stin[0], 64), (stin[1], 64), (kv_in[0], kv_count(1, 14)), (kv_in[1], kv_count(1, 15))):
                        pool.wait_ge(s, n)
            clear_sems()

        with nc.Block() as block:
            @block.tensor
            def _(pe):
                n = 0
                for t in range(3):
                    m = P if t < 2 else NB
                    for q in range(4):
                        if n >= 4:
                            pe.wait_ge(sem.x_ok, n - 3)
                        for c in range(4):
                            mm = pe.transpose(mb[0:m, n % 4, c * P:(c + 1) * P], xT[:, 4 * q + c, t * P:t * P + m], ident)
                        mm.then_inc(sem.x_T, 1)
                        n += 1

            @block.vector
            def _(dve):
                for n in range(12):
                    t, q = divmod(n, 4)
                    m = P if t < 2 else NB
                    dst = xrow[0:m, t, :] if t < 2 else r1[0:NB, :]
                    dve.wait_ge(sem.x_T, n + 1)
                    dve.tensor_copy(dst[:, q * 512:(q + 1) * 512], mb[0:m, n % 4, :]).then_inc(sem.x_ok, 1)

            @block.sync
            def _(sp):
                sp.wait_ge(sem.x_ok, 8)
                sp.dma_start(o.y_prompt.rearrange("a (t p) n -> p (a t) n", p=P), xrow).then_inc(sem.y_out, 16)
                sp.wait_ge(sem.x_ok, 12)
                sp.dma_start(o.y_sample.rearrange("b t n -> (b t) n"), r1[0:NB, :]).then_inc(sem.y_out, 16)
                sp.wait_ge(sem.y_out, 32)


_INS = ['x_prompt', 'x_sample', 'cache_conv', 'cache_dsa_k', 'cache_dsa_v', 'cache_dsa_idx_k', 'cache_mem_k', 'cache_mem_v',
        'state_gdn', 'state_ret', 'state_lru', 'page_table', 'mem_prompt', 'w_in', 'conv_w', 'conv_b', 'gdn_a_log',
        'gdn_dt_bias', 'gdn_norm_w', 'lru_lambda', 'lru_w_r', 'lru_b_r', 'lru_w_i', 'lru_b_i', 'w_mem_kv', 'w_branch',
        'w_out', 'ln_g', 'ln_b']
_OUTS = [('y_prompt', (1, NP, D)), ('y_sample', (NB, 1, D)),
         ('p_conv', (DEPTH, 1, 3, D)), ('p_gdn', (DEPTH, 1, NH, HD, HD)), ('p_ret', (DEPTH, 1, NH, HD, HD)),
         ('p_lru', (DEPTH, 1, W)), ('p_dsa_k', (DEPTH, 1, NP, NH, HD)), ('p_dsa_v', (DEPTH, 1, NP, NH, HD)),
         ('p_dsa_ik', (DEPTH, 1, NP, ID)), ('p_mem_k', (DEPTH, 1, NMEM, NH, HD)), ('p_mem_v', (DEPTH, 1, NMEM, NH, HD)),
         ('s_conv', (DEPTH, NB, 3, D)), ('s_gdn', (DEPTH, NB, NH, HD, HD)), ('s_ret', (DEPTH, NB, NH, HD, HD)),
         ('s_lru', (DEPTH, NB, W)), ('s_dsa_k', (DEPTH, NB, 1, NH, HD)), ('s_dsa_v', (DEPTH, NB, 1, NH, HD)),
         ('s_dsa_ik', (DEPTH, NB, 1, ID))]


def kernel(**inputs):
    import numpy as _np
    import concourse.bacc as _bacc
    from concourse import mybir as _mybir
    from concourse.bass_utils import run_bass_kernel_spmd as _run

    nc = _bacc.Bacc("TRN2", target_bir_lowering=False, num_devices=1)
    arrays, ins = {}, {}
    fixed, at, levels, decays = tables()
    consts = {"fixed": fixed, "levels": levels, "decays": decays}
    for name in _INS + list(consts):
        x = _np.ascontiguousarray(consts[name] if name in consts else inputs[name])
        arrays[f"in_{name}_dram"] = x
        ins[name] = nc.dram_tensor(f"in_{name}_dram", x.shape, _mybir.dt.from_np(x.dtype), kind="ExternalInput").ap()
    outs = {}
    for name, shape in _OUTS:
        outs[name] = nc.dram_tensor(f"out_{name}_dram", shape, _mybir.dt.float32, kind="ExternalOutput").ap()
    trunk(nc, namedtuple("Inputs", ins)(**ins), namedtuple("Outputs", outs)(**outs), at, fixed.shape[1])
    r = _run(nc, [arrays], core_ids=[0])
    return tuple(r.results[0][f"out_{name}_dram"] for name, _ in _OUTS)
```

```python
import math
from contextlib import ExitStack
from itertools import islice
from collections import namedtuple

import numpy as np
import concourse.bass as bass
from concourse import mybir

ALU = mybir.AluOpType
ACT = mybir.ActivationFunctionType
AX = mybir.AxisListType
F32 = mybir.dt.float32
U32 = mybir.dt.uint32
I32 = mybir.dt.int32

P = 128
D = 2048
KC = D // P
W = 512
NH = 4
HD = 128
DEPTH = 2
NP = 256
NB = 8
T = NP + NB
NMEM = 256
PAGE = 128
NPG = 16
PAST = NPG * PAGE
IH, ID = 8, 64
KP = min(256, NP // 4)
KS = min(256, (PAST + 1) // 4)
UC = 256
CPS = W // P
SCALE = HD ** -0.5
WSCALE = (IH * ID) ** -0.5
ALPHA = (2 * DEPTH) ** 0.25
LN_EPS, NORM_EPS = 1e-5, 1e-6
BIG = 1e30
TAKEN = -2.0 ** 127
LRU_C = 8.0

GQ, GK, GV, LX, RQ, RK, RV, DQ, DK, DV, DZ, RZ, LZ, IQ, MQ, MZ, GZ = range(17)
COL = {GQ: 0, GK: 512, GV: 1024, LX: 1536, GZ: 2048, DQ: 2568, DK: 3080, DV: 3592, DZ: 4104, IQ: 4616,
       RQ: 5200, RK: 5712, RV: 6224, RZ: 6736, LZ: 7248, MQ: 7760, MZ: 8272}
COL_AB, COL_IK, COL_GATE = 2560, 5128, 8784
SLOTS = range(17)
NSLOT = 3

BRANCH = [(4, MZ), (0, GZ), (2, RZ), (3, LZ), (1, DZ)]


def plan():
    units = []

    def project(*slots):
        units.extend(("in", s, k) for s in slots for k in range(2))

    def gates(n):
        units.extend(("gate", n, k) for k in range(D // UC))

    project(MQ)
    units.append(("narrow", 0, 0))
    units.extend(("mem", 0, k) for k in range(2 * W // UC))
    project(MZ, IQ, DQ, LX, GQ, GK, GV, GZ, RQ, RK, RV)
    gates(0)
    project(RZ, LZ, DK, DV, DZ)
    for n in range(1, len(BRANCH)):
        gates(n)
    units.extend(("out", 0, k) for k in range(D // UC))
    return units


UNITS = plan()
CHUNKS = [(u, c) for u in range(len(UNITS)) for c in range(2)]
_kinds = [UNITS[u][0] for u, _ in CHUNKS]
RESULTS = [1 + (k == "gate") for k in _kinds]
FIRST_RESULT = [sum(RESULTS[:i]) for i in range(len(CHUNKS))]


def _freed():
    n, out = {"stored": 0, "gate_act": 0, "merged_ok": 0, "out_ok": 0}, []
    for k in _kinds:
        for s in {"gate": ("gate_act", "merged_ok"), "out": ("out_ok",)}.get(k, ("stored",)):
            n[s] += 1
            out.append((s, n[s]))
    return out


FREED = _freed()
NARROW_U = UNITS.index(("narrow", 0, 0))
GATE_US = [u for u, x in enumerate(UNITS) if x[0] == "gate"]
MEMKV_READY, NARROW_READY = (FREED[FIRST_RESULT[max(i for i, k in enumerate(_kinds) if k == kind)]][1]
                             for kind in ("mem", "narrow"))


def landed(u):
    return 16 * (u // NSLOT + 1 + (u % NSLOT == NARROW_U % NSLOT and u >= NARROW_U))


def done(u):
    return FIRST_RESULT[2 * u + 1] + RESULTS[2 * u + 1]


def kv_count(n, i):
    return 16 * (i // 2 + 1) if n == 0 else 16 * NB + 32 * (i // 2 + 1)


def ready(slot):
    return FREED[FIRST_RESULT[2 * UNITS.index(("in", slot, 1)) + 1]][1]


def tables():
    at, parts = {}, []

    def add(name, a):
        a = np.asarray(a, np.float32)
        if a.shape[0] < P:
            a = np.concatenate([a, np.zeros((P - a.shape[0], a.shape[1]), np.float32)])
        at[name] = (sum(p.shape[1] for p in parts), a.shape[1])
        parts.append(a)

    i = np.arange(P)
    eye = np.eye(P)
    add("ident", eye)
    add("tri", i[:, None] <= i[None, :])
    add("ones", np.ones((P, P)))

    def rot(half, heads):
        m = np.zeros((P, P))
        for h in range(heads):
            for d in range(half):
                a, b = 2 * half * h + d, 2 * half * h + half + d
                m[b, a], m[a, b] = -1.0, 1.0
        return m

    r64 = rot(ID // 2, 2)
    add("rot128", rot(HD // 2, 1))
    add("rot64", r64)
    lo = np.zeros((P, P))
    lo[:ID] = np.concatenate([eye[:ID, :ID], eye[:ID, :ID]], 1)
    hi = np.zeros((P, P))
    hi[ID:] = lo[:ID]
    rd = np.zeros((P, P))
    rd[:ID] = np.concatenate([r64[:ID, :ID], r64[:ID, :ID]], 1)
    add("dup_lo", lo)
    add("dup_hi", hi)
    add("rot_dup", rd)
    pos = np.concatenate([np.arange(NP), np.full(NB, PAST)]).astype(np.float32)
    for dim in (HD, ID):
        half = dim // 2
        inv = (np.float32(10000.0) ** (-np.arange(half, dtype=np.float32) / np.float32(half))).astype(np.float32)
        ang = (pos[None, :] * inv[:, None]).astype(np.float32)
        reps = P // half
        add(f"cos{dim}", np.tile(np.cos(ang), (reps, 1)))
        add(f"sin{dim}", np.tile(np.sin(ang), (reps, 1)))
    add("future_t", np.where(i[None, :] < i[:, None], -BIG, 0.0))
    add("zeros", np.zeros((P, P)))
    add("future", np.where(i[None, :] > i[:, None], -BIG, 0.0))
    add("never", np.full((P, P), -BIG))
    add("strict_t", i[None, :] > i[:, None])
    gamma = 1.0 - 2.0 ** (-5.0 - np.arange(NH))
    lg = np.log(gamma.astype(np.float32)).astype(np.float64)
    zeta = np.exp((NP - 1 - (np.arange(2)[None, :, None] * P + i[:, None, None])) * lg[None, None, :])
    add("zeta", zeta.reshape(P, 2 * NH))
    add("gamma", np.tile(np.repeat(np.exp(lg), NB)[None], (P, 1)))
    e8 = np.eye(NB)
    add("blk_pages", np.repeat(e8, NPG, 1))
    add("blk_heads", np.repeat(e8, IH, 1))
    add("rep_heads", np.repeat(e8, NH, 1))
    add("parity", np.stack([i < ID, i >= ID], 1))
    add("iota", np.tile(np.arange(NPG)[None], (P, 1)))
    add("eps", np.tile(np.array([[HD * NORM_EPS, NORM_EPS, LN_EPS]]), (P, 1)))
    fixed = np.concatenate(parts, 1)

    def level(s):
        same = i[:, None] // (2 * s) == i[None, :] // (2 * s)
        return same & (i[:, None] % (2 * s) >= s) & (i[None, :] % (2 * s) < s)

    lv = np.concatenate([level(1)] + [level(s).T for s in (1, 2, 4, 8, 16, 32, 64)], 1)
    k = np.arange(NP)
    dist = k[None, None, :] - i[:, None, None]
    rd = np.where(dist >= 0, np.exp(np.maximum(dist, 0) * lg[None, :, None]), 0.0)
    return fixed, at, lv.astype(np.float32), rd.reshape(P, NH * NP).astype(np.float32)


def trunk(nc, a, o, at, fixed_w):
    n_pool = a.cache_dsa_k.shape[1]
    with ExitStack() as ctx:
        def sb(name, shape, dt=F32):
            return ctx.enter_context(nc.sbuf_tensor(name, shape, dt))

        TMP = 2112
        ring = sb("ring", [P, NSLOT, KC, UC])
        bring = sb("bring", [P, 2, CPS, UC])
        xT = sb("xT", [P, KC, T])
        merged = sb("merged", [P, KC, T])
        gbuf = sb("gbuf", [P, 2, T])
        work = sb("work", [P, TMP + len(SLOTS) * CPS * T])
        tab = sb("tab", [P, fixed_w])
        tabs = sb("tabs", [P, 1024])
        pT = sb("pT", [P, KC, 31])
        qT = sb("qT", [P, CPS, 11])
        memkv = sb("memkv", [P, 2052])
        mkT = memkv[:, 0:NH * NMEM].rearrange("p (h m) -> p h m", h=NH)
        mvr = memkv[:, NH * NMEM:NH * NMEM + 2 * W].rearrange("p (t n) -> p t n", t=2)
        stg = sb("stg", [P, W])
        srow = memkv[0:NB, 0:PAST + 1]
        small = sb("small", [P, 1100])
        picked = sb("picked", [NB, KS], U32)
        m8 = sb("m8", [NB, 8])
        i8 = sb("i8", [NB, 8], U32)
        pm8 = sb("pm8", [P, 8])
        rowsU = sb("rowsU", [P, 2, NB], U32)
        pagesU = sb("pagesU", [P, 8], U32)
        pti = sb("pti", [P, 1 + NB * NPG], I32)

        mb = ctx.enter_context(nc.psum_tensor("mb", [P, 4, 512], F32))
        bb = ctx.enter_context(nc.psum_tensor("bb", [P, 4, 512], F32))

        def tb(name):
            o_, n = at[name]
            return tab[:, o_:o_ + n]

        ident, ones = tb("ident"), tb("ones")
        tri_ones = tab[:, at["tri"][0]:at["tri"][0] + 2 * P]
        nm = tab[:, at["future_t"][0]:at["future_t"][0] + 2 * P]
        cm = [tab[:, at["future"][0]:at["future"][0] + 2 * P], tab[:, at["zeros"][0]:at["zeros"][0] + 2 * P]]
        id8 = ident[0:NB, 0:NB]

        hbase = TMP

        def H(slot):
            b0 = hbase + slot * CPS * T
            return work[:, b0:b0 + CPS * T].rearrange("p (c n) -> p c n", n=T)

        def area(slot, off, n):
            b0 = hbase + slot * CPS * T + off
            return work[:, b0:b0 + n]

        tmpA = work[:, 0:CPS * T].rearrange("p (c n) -> p c n", n=T)
        tmpB = work[:, CPS * T:2 * CPS * T].rearrange("p (c n) -> p c n", n=T)
        tmps = [tmpA, tmpB]
        r1 = area(RQ, 0, D)
        r2 = area(RV, 0, W)
        memrow = area(GQ, 0, 2 * D).rearrange("p (t n) -> p t n", t=2)
        memT = area(DK, 0, KC * NMEM).rearrange("p (c n) -> p c n", n=NMEM)
        xrow = memrow

        used = [0]

        def sm(n, parts=P):
            used[0] += n
            assert used[0] <= 1100
            return small[0:parts, used[0] - n:used[0]]

        abT = sm(T, NB)
        ikw = sm(T, 72)
        cols = sm(2, NB)
        negA = sm(1, NB)
        normw = sm(1)
        sp4 = sm(CPS)
        sn4 = sm(CPS)
        gbt = sm(32).rearrange("p (k t r) -> p k t r", k=2, t=2)
        gct = sm(2 * NH).rearrange("p (t h) -> p t h", t=2)
        ktl = sm(2 * NH).rearrange("p (t h) -> p t h", t=2)
        egb = sm(2 * IH * NB).rearrange("p (k h b) -> p k h b", k=2, h=IH)
        wtok = sm(2 * IH).rearrange("p (t h) -> p t h", t=2)
        wts = sm(IH, NB)
        ls = sm(64)
        pts = sm(96)
        nmx = sm(NH)
        rsm = sm(NH)
        lcount = sm(1)
        ptf = sm(1)
        goff = sm(9)
        rowf = sm(16)

        kvprod = sm(NH * NB)
        nsel = sm(1, NB)
        n88 = sm(IH, NB)
        pause = sm(1, NB)
        zT, spn, msk = (tmpA[0:NB, i_, :] for i_ in range(3))
        sln = spl = sm(CPS)
        spe, sle = spn, sln
        gate_mask, egs = msk[:, 0:128], msk[:, 128:144]

        def zarea(off, n, parts=P):
            return area(DK, off, n)[0:parts]

        def garea(off, n, parts=P):
            return area(GQ, off, n)[0:parts]

        def heads4(ap):
            return ap.rearrange("p (h x) -> p h x", h=NH)

        def prob(n):
            return heads4((zarea, garea)[n](0, NH * NP))

        def probT(n):
            return (zarea, garea)[n](1024, 1024).rearrange("p (s h q) -> p s h q", s=2, h=NH)

        relus = garea(0, IH * NP)
        pmask = garea(2048, 2 * NP).rearrange("p (t k) -> p t k", t=2)
        pscore = garea(2560, NP)
        vrow = work[:, 0:2 * W].rearrange("p (t n) -> p t n", t=2)
        ik = zarea(0, 2048).rearrange("p (i x) -> p i x", i=2)
        ikT, ikr = zarea(2048, 1024), zarea(3072, 1024)
        lw = zarea(4096, 2 * NB * IH, NB)
        qd = zarea(4224, IH * NB).rearrange("p (h b) -> p h b", h=IH)
        dt_all = zarea(0, 1536)
        dt0, dt1 = heads4(zarea(0, 1024)), heads4(zarea(1024, 512))
        amat = ymat = heads4(zarea(1536, W))
        atm, xinv, xinvT = (heads4(zarea(o_, W)) for o_ in (2048, 2560, 3072))
        bmat, btT = (heads4(zarea(o_, W)) for o_ in (3584, 4096))

        def tri_t(t):
            return heads4(zarea(4608, W) if t == 0 else stg[:, :])

        bv = work[:, 0:1024].rearrange("p (t n) -> p t n", t=2)
        kzA = work[:, 1024:2048].rearrange("p (t n) -> p t n", t=2)
        rt0, rt1 = heads4(garea(0, 1024)), heads4(garea(1024, 512))
        rv = garea(1536, 1024).rearrange("p (t n) -> p t n", t=2)
        kzC = work[:, 0:1024].rearrange("p (t n) -> p t n", t=2)

        def sbuf(n):
            return (zarea, garea)[n](0, 2048).rearrange("p (i b e) -> p i b e", i=2, b=NB)

        def vmask(n):
            return (zarea, garea)[n](2048, 1024, NB)

        def ktok(n):
            return work[0:NB, 0:W]

        def kq(n):
            return work[:, 512:576].rearrange("p (h b k) -> p h b k", h=NH, b=NB)

        def prod(n):
            return work[:, 576:608]

        def vnew(n):
            return work[:, 608:640].rearrange("p (h b) -> p h b", h=NH)

        qkb = work[:, 640:672].rearrange("p (h b) -> p h b", h=NH)
        s8 = [work[:, 672 + 8 * i_:680 + 8 * i_] for i_ in range(2)]
        lruw = tabs[:, :].rearrange("p (i h j) -> p i h j", i=2, h=NH)

        def lru(i_):
            return H(i_) if i_ < 3 else tmpA

        kvb = garea(0, 2048).rearrange("p (i t n) -> p i t n", i=2, t=2)
        prodK = work[:, 0:1024].rearrange("p (t h d) -> p t h d", t=2, h=NH)
        qrow, lrow = work[0:NB, 1056:1568], work[0:32, 1568:1568 + KS + 1]
        maskrow = garea(2048, KS + 1, NB)
        hilo = work[0:NB, 0:2 * KS].rearrange("p (k n) -> p k n", k=2)
        hiloU = work[0:NB, 2 * KS:4 * KS].bitcast(U32).rearrange("p (k n) -> p k n", k=2)
        eqs = work[:, 0:NB * NPG].rearrange("p (b g) -> p b g", b=NB)
        KI = sb("KI", [P, T])
        Qblk = sb("Qblk", [P, P])
        ptB = sb("ptB", [P, NB * NPG])
        scs = sb("scs", [P, P])
        mws = sb("mws", [P, P])

        names = """tables x_in x_T x_ok pages_in pages_ok params_in mem_in param_T param_cols mem_T memT_ok chunk_mm stored
            small_a small_b small_c small_d small_e gt_mm gt_ok gc_mm dt_raw dt_ok tails tails_ok tail_out conv_done
            conv_act sq ss rs normed mean_mm rot_mm rot_ok ki_mm ki_ok qd_mm qd_ok new_mm new_ok ik_T ik_copied ik_mm
            ik_rel ik_sc sc_ok row_in pidx_mm pidx_rel pidx_acc tok_mm tok_ok kk_mm kk_ok bt_mm bt_ok inv_T
            inv_at at_mm lvl_bt y_mm y_ok z_mm z_ok u_mm u_ok pt_mm pt_ok o_mm st_ok st_out kq_ok qk_mm qk_ok sk_mm
            vn_ok vt_mm vm_ok op_mm s_new s_out lw_in lru_mm lru_act lru_a lru_b lru_c lru_o lru_out h_mm h_rows
            lg_mm lg_ok ex_ok yc_ok pr_ok pT_mm pT_ok ov_mm y_e qr_mm qr_ok qb_mm kv_used lt_mm lt_ok lx_ok lp_ok lpt_mm
            lpt_ok sv_mm sy_ok hl_ok hl_mm rows_ok rows_out rows_mm rows_copied tab_in gate_act merged_ok out_ok
            ln_sum ln_cen ln_sq ln_ss ln_rs ln_x ln_done y_out se_ok mean_ok memv_out lc_ok decays_in v_chain a_chain
            cp_out""".split()
        sem = namedtuple("Semaphores", names)(*[ctx.enter_context(nc.semaphore(n)) for n in names])
        by_name = dict(zip(names, sem))
        w_landed = [ctx.enter_context(nc.semaphore(f"w_landed{i}")) for i in range(NSLOT)]
        bw_landed = [ctx.enter_context(nc.semaphore(f"bw_landed{i}")) for i in range(2)]
        gath = [ctx.enter_context(nc.semaphore(f"gathered{i}")) for i in range(2)]
        stin = [ctx.enter_context(nc.semaphore(f"state_in{i}")) for i in range(2)]
        kv_in = [ctx.enter_context(nc.semaphore(f"kv_in{i}")) for i in range(2)]
        layer_sems = kv_in + list(sem) + w_landed + bw_landed + gath + stin

        def chain(eng, s):
            n = [0]

            def link(ins):
                n[0] += 1
                ins.then_inc(s, 1)
                eng.wait_ge(s, n[0])
            return link

        def clear_sems():
            nc.all_engine_barrier()
            nc.gpsimd.dma_reset()
            nc.all_engine_barrier()
            for s in layer_sems:
                nc.sync.sem_clear(s)
            nc.all_engine_barrier()

        with nc.Block() as block:
            @block.sync
            def _(sp):
                sp.dma_start(tab[:, :], a.fixed).then_inc(sem.tables, 16)
                sp.dma_start(xrow, a.x_prompt.rearrange("a (t p) n -> p (a t) n", p=P)).then_inc(sem.x_in, 16)
                sp.dma_start(r1[0:NB, :], a.x_sample.rearrange("b t n -> (b t) n")).then_inc(sem.x_in, 16)
                pt = a.page_table.rearrange("b g -> (b g)")
                sp.dma_start(pti[:, 0:1], pt.rearrange("(p o) -> p o", o=1)).then_inc(sem.pages_in, 16)
                sp.dma_start(pti[:, 1:], pt.partition_broadcast(P)).then_inc(sem.pages_in, 16)

            @block.tensor
            def _(pe):
                pe.wait_ge(sem.tables, 16)
                pe.wait_ge(sem.x_in, 32)
                for c in range(KC):
                    if c >= 4:
                        pe.wait_ge(sem.x_ok, c - 3)
                    for t in range(2):
                        pe.transpose(mb[:, c % 4, t * P:(t + 1) * P], xrow[:, t, c * P:(c + 1) * P], ident)
                    pe.transpose(mb[:, c % 4, NP:T], r1[0:NB, c * P:(c + 1) * P], id8).then_inc(sem.x_T, 1)

            @block.vector
            def _(dve):
                dve.memset(cols, 0.0)
                dve.memset(Qblk[:, :], 0.0)
                dve.memset(lcount, 0.0)
                dve.wait_ge(sem.pages_in, 32)
                dve.tensor_copy(ptf, pti[:, 0:1])
                dve.tensor_copy(ptB[:, :], pti[:, 1:])
                for c in range(KC):
                    dve.wait_ge(sem.x_T, c + 1)
                    dve.tensor_copy(xT[:, c, :], mb[:, c % 4, 0:T]).then_inc(sem.x_ok, 1)
        clear_sems()

        with nc.Fori(0, DEPTH) as l:
            def at_l(ap):
                n = len(ap.shape)
                rest = " ".join(f"x{i}" for i in range(1, n))
                return ap[bass.ds(l, 1)].rearrange(f"z {rest} -> (z x1) " + " ".join(f"x{i}" for i in range(2, n)))

            w_in = at_l(a.w_in).rearrange("(k p) n -> p k n", p=P)
            w_mem = at_l(a.w_mem_kv).rearrange("(k p) n -> p k n", p=P)
            w_out = at_l(a.w_out).rearrange("(k p) n -> p k n", p=P)
            w_branch = at_l(a.w_branch).rearrange("b (k p) n -> p b k n", p=P)

            with nc.Block() as block:
                @block.sync
                def _(sp):
                    def branch_weights(u):
                        _, n, k = UNITS[u]
                        j = GATE_US.index(u)
                        if j >= 2:
                            sp.wait_ge(sem.chunk_mm, done(GATE_US[j - 2]))
                        sp.dma_start(bring[:, j % 2, :, :], w_branch[:, BRANCH[n][0], :, k * UC:(k + 1) * UC])\
                            .then_inc(bw_landed[j % 2], 16)

                    for u, (kind, x, k) in enumerate(UNITS):
                        if u - 1 in GATE_US:
                            branch_weights(u - 1)
                        if u >= NSLOT:
                            sp.wait_ge(sem.chunk_mm, done(u - NSLOT))
                        slot = ring[:, u % NSLOT, :, :]
                        if kind == "narrow":
                            sp.dma_start(slot[:, :, 0:8], w_in[:, :, COL_AB:COL_AB + 8]).then_inc(w_landed[u % NSLOT], 16)
                            sp.dma_start(slot[:, :, 8:80], w_in[:, :, COL_IK:COL_IK + 72]).then_inc(w_landed[u % NSLOT], 16)
                            continue
                        w = {"mem": w_mem, "out": w_out}.get(kind, w_in)
                        c0 = k * UC + (COL[x] if kind == "in" else COL_GATE + BRANCH[x][0] * D if kind == "gate" else 0)
                        sp.dma_start(slot, w[:, :, c0:c0 + UC]).then_inc(w_landed[u % NSLOT], 16)

                @block.tensor
                def _(pe):
                    chunks = iter(range(len(CHUNKS)))

                    def stream(n=1):
                        for i in islice(chunks, n):
                            (u, c), g = CHUNKS[i], FIRST_RESULT[i]
                            kind, x, k = UNITS[u]
                            w = ring[:, u % NSLOT, :, :]
                            if c == 0:
                                pe.wait_ge(w_landed[u % NSLOT], landed(u))
                            if kind == "out" and (c, k) == (0, 0):
                                pe.wait_ge(sem.merged_ok, 2 * len(GATE_US))
                            m0, m1 = ((0, 8), (8, 80))[c] if kind == "narrow" else (c * P, (c + 1) * P)
                            if g >= 4:
                                s, count = FREED[g - 4]
                                pe.wait_ge(by_name[s], count)
                            bank = mb[:, g % 4, :]
                            for q in range(KC):
                                if kind == "mem":
                                    l_, r_, nn = (w[:, q, m0:m1], memT[:, q, :], NMEM) if k < 2 else (memT[:, q, m0:m1], w[:, q, :], UC)
                                else:
                                    l_, r_, nn = w[:, q, m0:m1], (merged if kind == "out" else xT)[:, q, :], T
                                mm = pe.matmul(bank[0:m1 - m0, 0:nn], l_, r_, start=(q == 0), stop=(q == KC - 1))
                            mm.then_inc(sem.chunk_mm, 1)
                            if kind == "gate":
                                j = GATE_US.index(u)
                                if c == 0:
                                    pe.wait_ge(bw_landed[j % 2], 16 * (j // 2 + 1))
                                s, count = FREED[g - 3]
                                pe.wait_ge(by_name[s], count)
                                y = H(BRANCH[x][1])
                                for q in range(CPS):
                                    mm = pe.matmul(mb[:, (g + 1) % 4, 0:T], bring[:, j % 2, q, m0:m1], y[:, q, :],
                                                   start=(q == 0), stop=(q == CPS - 1))
                                mm.then_inc(sem.chunk_mm, 1)

                    stream(4)
                    pe.wait_ge(sem.params_in, 16 * 12)
                    for c in range(KC):
                        pe.transpose(bb[:, 0, c * 31:(c + 1) * 31], r1[0:31, c * P:(c + 1) * P], ident[0:31, 0:31])
                    for c in range(CPS):
                        mm = pe.transpose(bb[:, 1, c * 11:(c + 1) * 11], r2[0:11, c * P:(c + 1) * P], ident[0:11, 0:11])
                    mm.then_inc(sem.param_T, 1)
                    stream(1)
                    pe.wait_ge(sem.mem_in, 16)
                    pe.wait_ge(sem.param_cols, 1)
                    for t in range(2):
                        for q in range(4):
                            n = 4 * t + q
                            if n >= 4:
                                pe.wait_ge(sem.memT_ok, n - 3)
                            for c in range(4):
                                mm = pe.transpose(bb[:, n % 4, c * P:(c + 1) * P],
                                                  memrow[:, t, (4 * q + c) * P:(4 * q + c + 1) * P], ident)
                            mm.then_inc(sem.mem_T, 1)
                    stream(1)
                    pe.wait_ge(sem.memT_ok, 8)
                    stream(8)

                    def to_rows(src, bank, cols_=(0, P)):
                        c0, c1 = cols_
                        for h in range(NH):
                            mm = pe.transpose(bb[0:c1 - c0, bank, h * P:(h + 1) * P], src[:, h, c0:c1], ident)
                        return mm

                    def attend(n, q, k, v):
                        for t in range(2):
                            if n == 0 and t == 0:
                                pe.wait_ge(sem.rows_copied, 2)
                            for h in range(NH):
                                mm = pe.matmul(bb[:, h // 2, (h % 2) * NP:(h % 2 + 1) * NP], q[:, h, t * P:(t + 1) * P],
                                               k[:, h, 0:NP], start=True, stop=True)
                            mm.then_inc(sem.lg_mm, 1)
                            stream(2)
                            pe.wait_ge(sem.pr_ok, 2 * n + t + 1)
                            for s in range(2):
                                for h in range(NH):
                                    mm = pe.transpose(bb[:, 2 + s, h * P:(h + 1) * P],
                                                      prob(n)[:, h, s * P:(s + 1) * P], ident)
                            mm.then_inc(sem.pT_mm, 1)
                            stream(1)
                            pe.wait_ge(sem.pT_ok, 2 * n + t + 1)
                            for h in range(NH):
                                for s in range(2):
                                    mm = pe.matmul(bb[:, 0, h * P:(h + 1) * P], v[:, s, h * P:(h + 1) * P],
                                                   probT(n)[:, s, h, :], start=(s == 0), stop=(s == 1))
                            mm.then_inc(sem.ov_mm, 1)
                            stream(1)
                            pe.wait_ge(sem.y_e, 2 * n + t + 1)

                    def sample_attend(n, qslot):
                        to_rows(H(qslot), 0, (NP, T)).then_inc(sem.qr_mm, 1)
                        stream(1)
                        pe.wait_ge(sem.qr_ok, n + 1)
                        for b in range(NB):
                            if b >= 2:
                                pe.wait_ge(sem.kv_used, NB * n + b - 1)
                            pe.matmul(bb[:, b % 2, :], id8[:, b:b + 1].to_broadcast([NB, P]), qrow, start=True, stop=True)\
                                .then_inc(sem.qb_mm, 1)
                            if b % 4 == 3:
                                stream(1)
                        pe.wait_ge(sem.lx_ok, n + 1)
                        if n:
                            pe.matmul(bb[0:32, 2, 0:KS + 1], tb("rep_heads")[0:NB, :], maskrow, start=True, stop=True,
                                      skip_group_check=True)
                        for t in range(2):
                            mm = pe.matmul(bb[0:32, 2, t * P:(t + 1) * P], ls[:, 32 * t:32 * t + 32], ident,
                                           start=(n == 0), stop=True, skip_group_check=True)
                        if n:
                            mm = pe.matmul(bb[0:32, 2, KS:KS + 1], kvprod, ones[:, 0:1], start=False, stop=True,
                                           skip_group_check=True)
                        mm.then_inc(sem.lt_mm, 1)
                        stream(1)
                        pe.wait_ge(sem.lp_ok, n + 1)
                        for t in range(2):
                            mm = pe.transpose(bb[:, 3, 32 * t:32 * t + 32], lrow[:, t * P:(t + 1) * P], ident[0:32, 0:32])
                        if n:
                            mm = pe.matmul(bb[:, 3, 64:96], lrow[:, KS:KS + 1].to_broadcast([32, P]), ident[0:32, 0:32],
                                           start=True, stop=True)
                        mm.then_inc(sem.lpt_mm, 1)
                        stream(1)
                        pe.wait_ge(sem.lpt_ok, n + 1)
                        for b in range(NB):
                            pe.wait_ge(kv_in[b % 2], kv_count(n, NB + b))
                            for h in range(NH):
                                j = b * NH + h
                                for t in range(2):
                                    mm = pe.matmul(bb[:, 0, j:j + 1], kvb[:, b % 2, t, h * P:(h + 1) * P],
                                                   pts[:, 32 * t + j:32 * t + j + 1], start=(t == 0), stop=(t == 1))
                            mm.then_inc(sem.sv_mm, 1)
                            if b == 3:
                                stream(1)
                        pe.wait_ge(sem.sy_ok, n + 1)

                    for t in range(2):
                        to_rows(mkT, t, (t * P, (t + 1) * P)).then_inc(sem.rows_mm, 1)
                    stream(2)
                    attend(0, H(MQ), mkT, mvr)
                    pe.wait_ge(sem.stored, ready(MZ))
                    sample_attend(0, MQ)

                    pe.wait_ge(sem.small_e, 1)
                    for kind, src in enumerate((zT, abT)):
                        for t in range(2):
                            pe.transpose(bb[:, 0, (2 * kind + t) * 8:(2 * kind + t + 1) * 8],
                                         src[:, t * P:(t + 1) * P], id8)
                    mm = pe.matmul(bb[:, 1, 0:2 * IH * NB], ones[0:NB, :], gate_mask, start=True, stop=True)
                    mm.then_inc(sem.gt_mm, 1)
                    stream(1)
                    pe.wait_ge(sem.gt_ok, 1)

                    def rotate(n, slot, mat):
                        pe.wait_ge(sem.stored, ready(slot))
                        for c in range(CPS):
                            mm = pe.matmul(bb[:, c, 0:T], mat, H(slot)[:, c, :], start=True, stop=True)
                        mm.then_inc(sem.rot_mm, 1)
                        stream(1)

                    rotate(0, IQ, tb("rot64"))
                    pe.wait_ge(sem.rot_ok, 1)
                    pe.matmul(bb[:, 0, 0:T], tb("dup_lo")[0:ID, :], ikw[0:ID, :], start=True, stop=True)
                    pe.matmul(bb[:, 1, 0:T], tb("rot_dup")[0:ID, :], ikw[0:ID, :], start=True, stop=True)
                    for t in range(3):
                        m = P if t < 2 else NB
                        mm = pe.transpose(bb[0:m, 2, t * 72:(t + 1) * 72], ikw[0:72, t * P:t * P + m], ident[0:72, 0:72])
                    mm.then_inc(sem.ki_mm, 1)
                    stream(1)

                    for c in range(CPS):
                        for k, name in enumerate(("dup_lo", "dup_hi")):
                            j = 2 * c + k
                            pe.matmul(bb[:, 3, j * NB:(j + 1) * NB], tb(name), H(IQ)[:, c, NP:T], start=True, stop=True)
                    pe.wait_ge(sem.ki_ok, 1)
                    mm = pe.matmul(bb[:, 0, 0:P], lw, tb("blk_pages")[0:NB, :], start=True, stop=True)
                    mm.then_inc(sem.qd_mm, 1)
                    pe.wait_ge(sem.qd_ok, 1)
                    for j in range(IH):
                        mm = pe.matmul(bb[0:NB, 1, j * NB:(j + 1) * NB], qd[0:ID, j, :], KI[0:ID, NP:T], start=True, stop=True)
                    mm.then_inc(sem.new_mm, 1)
                    stream(1)
                    for j in range(8):
                        pe.wait_ge(gath[j % 2], 16 * (j // 2 + 1))
                        if j == 0:
                            pe.wait_ge(sem.new_ok, 1)
                        for u in range(8):
                            mm = pe.transpose(bb[:, u // 4, (u % 4) * P:(u % 4 + 1) * P], ik[:, j % 2, u * P:(u + 1) * P], ident)
                        mm.then_inc(sem.ik_T, 1)
                        stream(1)
                        pe.wait_ge(sem.ik_copied, j + 1)
                        for u in range(2):
                            mm = pe.matmul(bb[:, 2 + u, :], Qblk[:, :], ikT[:, u * 512:(u + 1) * 512], start=True, stop=True)
                        mm.then_inc(sem.ik_mm, 1)
                        pe.wait_ge(sem.ik_rel, j + 1)
                        for u in range(8):
                            mm = pe.matmul(bb[:, 0, 2 * u:2 * u + 2], ikr[:, u * P:(u + 1) * P], tb("parity"), start=True, stop=True)
                        mm.then_inc(sem.ik_sc, 1)
                        pe.wait_ge(sem.sc_ok, j + 1)

                    pe.matmul(bb[:, 0, 0:NH], tri_ones[:, 0:P], gbt[:, 0, 0, 0:NH], start=True, stop=True)
                    pe.matmul(bb[:, 0, NH:2 * NH], ones, gbt[:, 0, 0, 0:NH], start=True, stop=False)
                    pe.matmul(bb[:, 0, NH:2 * NH], tri_ones[:, 0:P], gbt[:, 0, 1, 0:NH], start=False, stop=True)
                    for h in range(NH):
                        b_, c0 = 1 + h // 2, (h % 2) * NP
                        pe.matmul(bb[:, b_, c0:c0 + NP], gbt[:, 0, 0, h:h + 1].to_broadcast([P, P]), tri_ones,
                                  start=True, stop=False)
                        mm = pe.matmul(bb[:, b_, c0 + P:c0 + NP], gbt[:, 0, 1, h:h + 1].to_broadcast([P, P]),
                                       tri_ones[:, 0:P], start=False, stop=True)
                    mm.then_inc(sem.gc_mm, 1)
                    stream(1)
                    pe.wait_ge(sem.dt_raw, 1)

                    def tail(i, s):
                        pe.wait_ge(sem.stored, ready(s))
                        if i:
                            pe.wait_ge(sem.tails_ok, i)
                        for c in range(CPS):
                            mm = pe.transpose(bb[0:11, 0, c * P:(c + 1) * P], H(s)[:, c, NP - 3:T], ident)
                        mm.then_inc(sem.tails, 1)

                    def ones_sum(n, src):
                        pe.wait_ge(sem.sq, n)
                        for c in range(CPS):
                            mm = pe.matmul(bb[:, c, 0:T], ones, src[:, c, :], start=True, stop=True)
                        mm.then_inc(sem.ss, 1)
                        stream(1)

                    for i, s in enumerate((GQ, GK, GV)):
                        tail(i, s)
                        stream(1)
                    pe.wait_ge(sem.tails_ok, 3)
                    stream(1)
                    ones_sum(1, tmpA)
                    pe.wait_ge(sem.normed, 1)
                    ones_sum(2, tmpA)
                    pe.wait_ge(sem.normed, 2)

                    def inner_scores(n, kk, qq):
                        for h in range(NH):
                            pe.matmul(bb[:, h // 2, (h % 2) * NP:(h % 2 + 1) * NP], kk[:, h, 0:P], qq[:, h, 0:NP],
                                      start=True, stop=True)
                            mm = pe.matmul(bb[:, 2, h * P:(h + 1) * P], kk[:, h, P:NP], qq[:, h, P:NP], start=True, stop=True)
                        mm.then_inc(sem.pt_mm, 1)
                        stream(1)

                    def out_and_state(n, pt0, pt1, v0, v1, kz):
                        for h in range(NH):
                            b_, c0, hs = h // 2, (h % 2) * NP, slice(h * P, (h + 1) * P)
                            pe.matmul(bb[:, b_, c0:c0 + NP], v0[:, hs], pt0[:, h, :], start=True, stop=False)
                            pe.matmul(bb[:, b_, c0 + P:c0 + NP], v1[:, hs], pt1[:, h, :], start=False, stop=True)
                        for h in range(NH):
                            hs = slice(h * P, (h + 1) * P)
                            pe.matmul(bb[:, 2, hs], kz[:, 0, hs], v0[:, hs], start=True, stop=False)
                            mm = pe.matmul(bb[:, 2, hs], kz[:, 1, hs], v1[:, hs], start=False, stop=True)
                        mm.then_inc(sem.o_mm, 1)
                        stream(1)

                    gq, gk, gv = H(GQ), H(GK), H(GV)
                    for t in range(2):
                        to_rows(gv, t, (t * P, (t + 1) * P))
                        mm = to_rows(gk, 2 + t, (t * P, (t + 1) * P))
                    mm.then_inc(sem.tok_mm, 1)
                    stream(1)
                    pe.wait_ge(sem.tok_ok, 1)
                    for t in range(2):
                        for h in range(NH):
                            ks = gk[:, h, t * P:(t + 1) * P]
                            pe.matmul(bb[:, t, h * P:(h + 1) * P], ks, ks, start=True, stop=True)
                    for h in range(NH):
                        mm = pe.matmul(bb[:, 2, h * P:(h + 1) * P], gk[:, h, 0:P], gk[:, h, P:NP], start=True, stop=True)
                    mm.then_inc(sem.kk_mm, 1)
                    stream(1)
                    for t in range(2):
                        pe.wait_ge(sem.kk_ok, t + 1)
                        for h in range(NH):
                            mm = pe.transpose(bb[:, 3, h * P:(h + 1) * P], tri_t(t)[:, h, :], ident)
                        mm.then_inc(sem.inv_T, 1)
                        pe.wait_ge(sem.inv_at, t + 1)
                        for h in range(NH):
                            mm = pe.transpose(bb[:, 3, h * P:(h + 1) * P], amat[:, h, :], ident)
                        mm.then_inc(sem.at_mm, 1)
                        stream(1)
                        for lv in range(6):
                            n = 6 * t + lv
                            pe.wait_ge(sem.lvl_bt, n + 1)
                            for h in range(NH):
                                mm = pe.matmul(bb[:, 3, h * P:(h + 1) * P], bmat[:, h, :], xinv[:, h, :], start=True, stop=True)
                            mm.then_inc(sem.y_mm, 1)
                            pe.wait_ge(sem.y_ok, n + 1)
                            for h in range(NH):
                                pe.matmul(bb[:, 0, h * P:(h + 1) * P], ymat[:, h, :], xinvT[:, h, :], start=True, stop=True)
                                mm = pe.matmul(bb[:, 3, h * P:(h + 1) * P], xinvT[:, h, :], ymat[:, h, :], start=True, stop=True)
                            mm.then_inc(sem.z_mm, 1)
                            stream(1)
                        pe.wait_ge(sem.z_ok, 6 * (t + 1))
                        if t == 1:
                            for h in range(NH):
                                mm = pe.matmul(bb[:, 3, h * P:(h + 1) * P], btT[:, h, :], bv[:, 0, h * P:(h + 1) * P],
                                               start=True, stop=True)
                            mm.then_inc(sem.bt_mm, 1)
                            pe.wait_ge(sem.bt_ok, 1)
                        for h in range(NH):
                            mm = pe.matmul(bb[:, 3, h * P:(h + 1) * P], xinvT[:, h, :], bv[:, t, h * P:(h + 1) * P],
                                           start=True, stop=True)
                        mm.then_inc(sem.u_mm, 1)
                        stream(1)
                        pe.wait_ge(sem.u_ok, t + 1)
                    inner_scores(0, gk, gq)
                    pe.wait_ge(sem.pt_ok, 1)
                    out_and_state(0, dt0, dt1, bv[:, 0, :], bv[:, 1, :], kzA)

                    def samples_step(n, kslot, qslot, vslot):
                        pe.wait_ge(sem.kq_ok, n + 1)
                        pe.matmul(bb[:, 0, 0:NH * NB], ones, prod(n), start=True, stop=True)
                        mm = to_rows(H(kslot), 1, (NP, T))
                        mm.then_inc(sem.qk_mm, 1)
                        stream(1)
                        pe.wait_ge(sem.qk_ok, n + 1)
                        for h in range(NH):
                            m = NH * n + h
                            pe.wait_ge(stin[h % 2], 16 * (m // 2 + 1))
                            for b in range(NB):
                                mm = pe.matmul(bb[:, 0, 2 * b:2 * b + 2], sbuf(n)[:, h % 2, b, :], kq(n)[:, h, b, :],
                                               start=True, stop=True)
                            mm.then_inc(sem.sk_mm, 1)
                            stream(1)
                            pe.wait_ge(sem.vn_ok, m + 1)
                            pe.transpose(bb[0:NB, 1, 0:P], vnew(n)[:, h, :], ident).then_inc(sem.vt_mm, 1)
                            pe.wait_ge(sem.vm_ok, m + 1)
                            for j in range(2):
                                mm = pe.matmul(bb[:, 2 + j, :], ktok(n)[:, h * P:(h + 1) * P], vmask(n)[:, 512 * j:512 * (j + 1)],
                                               start=True, stop=True)
                            mm.then_inc(sem.op_mm, 1)
                            if h % 2 == 0:
                                stream(1)
                        pe.wait_ge(sem.s_new, NH * (n + 1))

                    pe.wait_ge(sem.st_ok, 1)
                    samples_step(0, GK, GQ, GV)
                    ones_sum(3, tmpA)
                    pe.wait_ge(sem.normed, 3)

                    for n, s in enumerate((RQ, RK)):
                        rotate(1 + n, s, tb("rot128"))
                        pe.wait_ge(sem.rot_ok, 2 + n)
                    for t in range(2):
                        to_rows(H(RV), t, (t * P, (t + 1) * P))
                        mm = to_rows(H(RK), 2 + t, (t * P, (t + 1) * P))
                    mm.then_inc(sem.tok_mm, 1)
                    stream(1)
                    pe.wait_ge(sem.tok_ok, 2)
                    inner_scores(1, H(RK), H(RQ))
                    pe.wait_ge(sem.pt_ok, 2)
                    out_and_state(1, rt0, rt1, rv[:, 0, :], rv[:, 1, :], kzC)
                    pe.wait_ge(sem.st_ok, 2)
                    samples_step(1, RK, RQ, RV)
                    for c in range(CPS):
                        mm = pe.matmul(bb[:, c, 0:T], ones, H(RQ)[:, c, :], start=True, stop=True)
                    mm.then_inc(sem.mean_mm, 1)
                    stream(1)
                    ones_sum(4, tmpA)
                    pe.wait_ge(sem.yc_ok, 1)

                    tail(3, LX)
                    stream(1)
                    pe.wait_ge(sem.tails_ok, 4)
                    pe.wait_ge(sem.conv_act, 4)
                    pe.wait_ge(sem.lw_in, 32)
                    for i in range(2):
                        if i:
                            pe.wait_ge(sem.lru_act, 1)
                        for h in range(NH):
                            mm = pe.matmul(bb[:, h, 0:T], lruw[:, i, h, :], H(LX)[:, h, :], start=True, stop=True)
                        mm.then_inc(sem.lru_mm, 1)
                        stream(1)
                    pe.wait_ge(sem.lru_act, 2)
                    stream(4)
                    pe.wait_ge(sem.lru_o, 1)
                    for h in range(NH):
                        mm = pe.transpose(bb[0:NB + 1, 0, h * P:(h + 1) * P], H(LX)[:, h, NP - 1:T], ident)
                    mm.then_inc(sem.h_mm, 1)
                    stream(1)

                    pe.wait_ge(sem.h_rows, 1)
                    for n, s in enumerate((DQ, DK)):
                        rotate(3 + n, s, tb("rot128"))
                        pe.wait_ge(sem.rot_ok, 4 + n)
                    for n, s in enumerate((DK, DV)):
                        pe.wait_ge(sem.stored, ready(s))
                        for t in range(3):
                            if 3 * n + t:
                                pe.wait_ge(sem.rows_copied, 2 + 3 * n + t)
                            to_rows(H(s), 0, (t * P, t * P + P) if t < 2 else (NP, T)).then_inc(sem.rows_mm, 1)
                            if t != 1:
                                stream(1)
                    pe.wait_ge(sem.rows_copied, 8)
                    for t in range(3):
                        m = P if t < 2 else NB
                        mm = pe.transpose(bb[0:m, 0, t * ID:(t + 1) * ID], KI[0:ID, t * P:t * P + m], ident[0:ID, 0:ID])
                    mm.then_inc(sem.rows_mm, 1)
                    pe.wait_ge(sem.rows_copied, 9)
                    for t in range(2):
                        if t:
                            pe.wait_ge(sem.pidx_rel, 1)
                        for j in range(IH):
                            p0 = ID * (j % 2)
                            mm = pe.matmul(bb[:, 2 * (j % 2) + j // 4, (j // 2 % 2) * NP:(j // 2 % 2 + 1) * NP],
                                           H(IQ)[p0:p0 + ID, j // 2, t * P:(t + 1) * P], KI[p0:p0 + ID, 0:NP],
                                           start=True, stop=True)
                        mm.then_inc(sem.pidx_mm, 1)
                        stream(2)
                    pe.wait_ge(sem.pidx_rel, 2)
                    pe.wait_ge(sem.stored, ready(DZ))
                    attend(1, H(DQ), H(DK), vrow)

                    pe.wait_ge(sem.hl_ok, 1)
                    for k in range(2):
                        for t in range(2):
                            j = 2 * k + t
                            mm = pe.transpose(bb[:, 0, j * NB:(j + 1) * NB], hilo[:, k, t * P:(t + 1) * P], id8)
                    mm.then_inc(sem.hl_mm, 1)
                    stream(2)
                    pe.wait_ge(sem.rows_ok, 1)
                    sample_attend(1, DQ)
                    stream(None)
                    pe.wait_ge(sem.out_ok, KC)
                    for q in range(KC):
                        mm = pe.matmul(bb[:, 0, 0:T], ones, xT[:, q, :], start=(q == 0), stop=(q == KC - 1))
                    mm.then_inc(sem.ln_sum, 1)
                    for q in range(4):
                        pe.wait_ge(sem.ln_sq, q + 1)
                        for c in range(4):
                            mm = pe.matmul(bb[:, 1, 0:T], ones, tmps[q % 2][:, c, :], start=(q + c == 0), stop=(q + c == 6))
                        mm.then_inc(sem.ln_ss, 1)

                @block.scalar
                def _(act):
                    ch = chain(act, sem.a_chain)
                    chunks = iter(range(len(CHUNKS)))

                    def stream(n=1):
                        for i in islice(chunks, n):
                            (u, c), g = CHUNKS[i], FIRST_RESULT[i]
                            kind, x, k = UNITS[u]
                            if kind == "out":
                                continue
                            act.wait_ge(sem.chunk_mm, g + 1)
                            src = mb[:, g % 4, :]
                            if kind == "gate":
                                j = 2 * GATE_US.index(u) + c
                                if j >= 2:
                                    act.wait_ge(sem.merged_ok, j - 1)
                                act.activation(gbuf[:, c, :], src[:, 0:T], ACT.Sigmoid).then_inc(sem.gate_act, 1)
                            elif kind == "mem":
                                dst = mkT[:, 2 * k + c, :] if k < 2 else mvr[:, c, (k - 2) * UC:(k - 1) * UC]
                                act.activation(dst, src[:, 0:UC], ACT.Copy).then_inc(sem.stored, 1)
                            elif kind == "narrow":
                                dst = ikw[0:72, :] if c else abT
                                act.activation(dst, src[0:72 if c else NB, 0:T], ACT.Copy).then_inc(sem.stored, 1)
                            else:
                                if (x, k, c) == (RZ, 0, 0):
                                    act.wait_ge(sem.s_out, 16 * NH)
                                act.activation(H(x)[:, 2 * k + c, :], src[:, 0:T],
                                               ACT.Silu if x in (GZ, DZ, RZ, LZ, MZ) else ACT.Copy).then_inc(sem.stored, 1)

                    act.dma_start(r1[0:4, :], at_l(a.conv_w)).then_inc(sem.params_in, 16)
                    for i, v in enumerate((a.conv_b, a.ln_g, a.ln_b)):
                        act.dma_start(r1[4 + i:5 + i, :], v[bass.ds(l, 1), :]).then_inc(sem.params_in, 16)
                    act.dma_start(r1[7:31, :], at_l(a.cache_conv).rearrange("b j n -> (b j) n")).then_inc(sem.params_in, 16)
                    for i, v in enumerate((a.lru_lambda, a.lru_b_r, a.lru_b_i)):
                        act.dma_start(r2[i:i + 1, :], v[bass.ds(l, 1), :]).then_inc(sem.params_in, 16)
                    act.dma_start(r2[3:11, :], at_l(a.state_lru)).then_inc(sem.params_in, 16)
                    act.dma_start(cols[0:NH, 0:1], a.gdn_dt_bias[bass.ds(l, 1), :].rearrange("z h -> h z")).then_inc(sem.params_in, 16)
                    act.dma_start(cols[0:NH, 1:2], a.gdn_a_log[bass.ds(l, 1), :].rearrange("z h -> h z")).then_inc(sem.params_in, 16)
                    act.dma_start(normw, a.gdn_norm_w[bass.ds(l, 1), :].rearrange("z d -> d z")).then_inc(sem.params_in, 16)
                    act.dma_start(tabs[:, :], a.levels).then_inc(sem.tab_in, 16)
                    act.dma_start(memrow, a.mem_prompt.rearrange("a (t p) n -> p (a t) n", p=P)).then_inc(sem.mem_in, 16)

                    stream(4)
                    stream(2)
                    stream(8)
                    stream(2)

                    def attend(n):
                        for t in range(2):
                            act.wait_ge(sem.lg_ok, 2 * n + t + 1)
                            for h in range(NH):
                                mm = act.activation(prob(n)[:, h, :], prob(n)[:, h, :], ACT.Exp, bias=nmx[:, h:h + 1],
                                                    accum_out=rsm[:, h:h + 1])
                            mm.then_inc(sem.ex_ok, 1)
                            stream(2)
                            act.wait_ge(sem.pT_mm, 2 * n + t + 1)
                            act.activation(probT(n).rearrange("p s h q -> p (s h q)"),
                                           bb[:, 2:4, :].rearrange("p s x -> p (s x)"), ACT.Copy).then_inc(sem.pT_ok, 1)
                            stream(2)

                    def sample_attend(n, w):
                        stream(1 + NB // 4)
                        act.wait_ge(sem.lt_ok, n + 1)
                        act.activation(lrow[:, 0:w], lrow[:, 0:w], ACT.Exp, bias=nmx[0:32, 0:1],
                                       accum_out=rsm[0:32, 0:1]).then_inc(sem.se_ok, 1)
                        stream(3)

                    attend(0)
                    sample_attend(0, KS)
                    act.wait_ge(sem.small_a, 1)
                    act.activation(spe, spn, ACT.Exp, scale=-1.0)
                    act.activation(sle, sln, ACT.Exp, scale=-1.0)
                    ch(act.activation(negA, cols[:, 1:2], ACT.Exp))
                    act.activation(spe, spe, ACT.Ln, bias=1.0)
                    act.activation(sle, sle, ACT.Ln, bias=1.0)
                    act.activation(abT, abT, ACT.Sigmoid).then_inc(sem.small_b, 1)
                    act.wait_ge(sem.small_c, 1)
                    act.activation(egs[:, 0:8], zT[:, NP:T], ACT.Exp).then_inc(sem.small_d, 1)
                    stream(1)
                    stream(1)
                    stream(1)
                    stream(1)
                    for j in range(8):
                        act.wait_ge(sem.ik_T, j + 1)
                        act.activation(ikT, bb[:, 0:2, :].rearrange("p s x -> p (s x)"), ACT.Copy).then_inc(sem.ik_copied, 1)
                        stream(1)

                    def conv_out(i, s):
                        act.wait_ge(sem.conv_done, i + 1)
                        act.activation(H(s), tmps[i % 2], ACT.Silu if s != LX else ACT.Copy).then_inc(sem.conv_act, 1)

                    def squares(n, src):
                        act.activation(tmpA, src, ACT.Square).then_inc(sem.sq, 1)

                    def roots(n, scale, eps):
                        act.wait_ge(sem.ss, n)
                        mm = act.activation(tmpA, bb[:, :, 0:T], ACT.Sqrt, scale=scale, bias=eps)
                        mm.then_inc(sem.rs, 1)
                        stream(1)

                    act.wait_ge(sem.dt_raw, 1)
                    act.activation(dt_all, dt_all, ACT.Exp)
                    act.activation(ktl.rearrange("p t h -> p (t h)"), ktl.rearrange("p t h -> p (t h)"), ACT.Exp)\
                        .then_inc(sem.dt_ok, 1)
                    stream(1)
                    eps = tb("eps")
                    for i, s in enumerate((GQ, GK, GV)):
                        conv_out(i, s)
                        stream(1)
                    stream(1)
                    act.wait_ge(sem.conv_act, 3)
                    squares(1, H(GQ))
                    roots(1, float(HD), eps[:, 0:1])
                    act.wait_ge(sem.normed, 1)
                    squares(2, H(GK))
                    roots(2, 1.0, eps[:, 1:2])
                    stream(1)
                    stream(1)
                    for t in range(2):
                        stream(1)
                        for lv in range(6):
                            n = 6 * t + lv
                            act.wait_ge(sem.y_mm, n + 1)
                            act.activation(ymat.rearrange("p h x -> p (h x)"), bb[:, 3, :], ACT.Copy).then_inc(sem.y_ok, 1)
                            stream(1)
                        stream(1)
                    stream(1)
                    stream(1)
                    stream(1 + NH + NH // 2)
                    act.wait_ge(sem.s_new, NH)
                    squares(3, H(GQ))
                    roots(3, 1.0 / HD, eps[:, 1:2])
                    stream(2 + 1 + 1 + 1 + 1 + NH + NH // 2)
                    act.wait_ge(sem.mean_ok, 1)
                    squares(4, H(RQ))
                    stream(1)
                    roots(4, 1.0 / HD, eps[:, 2:3])
                    conv_out(3, LX)
                    stream(1)
                    act.wait_ge(sem.s_out, 16 * 2 * NH)
                    for i in range(2):
                        act.wait_ge(sem.lru_mm, i + 1)
                        for h in range(CPS):
                            mm = act.activation(lru(i)[:, h, :], bb[:, h, 0:T], ACT.Sigmoid, bias=qT[:, h, 1 + i:2 + i])
                        mm.then_inc(sem.lru_act, 1)
                        stream(1)
                    for h in range(CPS):
                        act.activation(lru(2)[:, h, :], lru(0)[:, h, :], ACT.Exp, scale=sn4[:, h:h + 1])
                        mm = act.activation(lru(3)[:, h, :], lru(0)[:, h, :], ACT.Tanh, scale=sp4[:, h:h + 1])
                    mm.then_inc(sem.lru_a, 1)
                    act.wait_ge(sem.lru_b, 1)
                    act.activation(lru(0), lru(0), ACT.Sqrt).then_inc(sem.lru_c, 1)
                    stream(4)
                    stream(1)
                    stream(2)
                    stream(4)
                    for t in range(2):
                        act.wait_ge(sem.pidx_mm, t + 1)
                        if t:
                            act.wait_ge(sem.pidx_acc, 1)
                        act.activation(relus, bb[:, :, :].rearrange("p s x -> p (s x)"), ACT.Relu).then_inc(sem.pidx_rel, 1)
                        stream(2)
                    attend(1)

                    stream(2)
                    sample_attend(1, KS + 1)
                    stream(None)
                    for q in range(4):
                        act.wait_ge(sem.ln_cen, q + 1)
                        if q >= 2:
                            act.wait_ge(sem.ln_ss, q - 1)
                        act.activation(tmps[q % 2], xT[:, 4 * q:4 * q + 4, :], ACT.Square).then_inc(sem.ln_sq, 1)
                    act.wait_ge(sem.ln_ss, 4)
                    act.activation(tmpA[:, 0, :], bb[:, 1, 0:T], ACT.Sqrt, scale=1.0 / D, bias=eps[:, 2:3]).then_inc(sem.ln_rs, 1)
                    for q in range(KC):
                        act.wait_ge(sem.ln_x, q // 4 + 1)
                        act.activation(xT[:, q, :], xT[:, q, :], ACT.Identity, scale=pT[:, q, 5:6], bias=pT[:, q, 6:7])\
                            .then_inc(sem.ln_done, 1)

                @block.vector
                def _(dve):
                    v = chain(dve, sem.v_chain)

                    def bc(ap, n):
                        return ap.unsqueeze(2).to_broadcast([ap.shape[0], ap.shape[1], n])

                    def bh(ap, n=NH):
                        return ap.unsqueeze(1).to_broadcast([ap.shape[0], n, ap.shape[1]])

                    chunks = iter(range(len(CHUNKS)))

                    def stream(n=1):
                        for i in islice(chunks, n):
                            (u, c), g = CHUNKS[i], FIRST_RESULT[i]
                            kind, x, k = UNITS[u]
                            m = 2 * k + c
                            if kind == "gate":
                                j = 2 * GATE_US.index(u) + c
                                gate, proj = gbuf[:, c, :], mb[:, (g + 1) % 4, 0:T]
                                dve.wait_ge(sem.gate_act, j + 1)
                                dve.wait_ge(sem.chunk_mm, g + 2)
                                if x == 0:
                                    dve.tensor_tensor(merged[:, m, :], gate, proj, ALU.mult).then_inc(sem.merged_ok, 1)
                                else:
                                    v(dve.tensor_tensor(gate, gate, proj, ALU.mult))
                                    dve.tensor_tensor(merged[:, m, :], merged[:, m, :], gate, ALU.add).then_inc(sem.merged_ok, 1)
                            elif kind == "out":
                                dve.wait_ge(sem.chunk_mm, g + 1)
                                dve.scalar_tensor_tensor(xT[:, m, :], xT[:, m, :], ALPHA, mb[:, g % 4, 0:T], ALU.mult, ALU.add)\
                                    .then_inc(sem.out_ok, 1)

                    rounds = iter(range(KS // 8))

                    def topk(n=1):
                        for _ in range(n):
                            r = next(rounds, None)
                            if r is None:
                                return
                            v(dve.max(m8[:, :], srow))
                            v(dve.max_index(i8[:, :], m8[:, :], srow))
                            v(dve.match_replace(srow, m8[:, :], srow, TAKEN))
                            v(dve.tensor_copy(picked[:, 8 * r:8 * r + 8], i8[:, :]))

                    dve.wait_ge(sem.param_T, 1)
                    v(dve.tensor_copy(pT[:, :, :].rearrange("p c r -> p (c r)"), bb[:, 0, 0:KC * 31]))
                    dve.tensor_copy(qT[:, :, :].rearrange("p c r -> p (c r)"), bb[:, 1, 0:CPS * 11]).then_inc(sem.param_cols, 1)
                    dve.wait_ge(sem.param_cols, 1)
                    for t in range(2):
                        for q in range(4):
                            dve.wait_ge(sem.mem_T, 4 * t + q + 1)
                            dve.tensor_copy(memT[:, 4 * q:4 * q + 4, t * P:(t + 1) * P], heads4(bb[:, q, :])).then_inc(sem.memT_ok, 1)
                    v(dve.tensor_scalar(goff[:, 8:9], lcount, float(n_pool * 8), None, ALU.mult))
                    v(dve.scalar_tensor_tensor(goff[:, 8:9], ptf, 8.0, goff[:, 8:9], ALU.mult, ALU.add))
                    v(dve.tensor_scalar(goff[:, 0:8], tb("iota")[:, 0:8], goff[:, 8:9], None, ALU.add))
                    dve.tensor_copy(pagesU[:, :], goff[:, 0:8]).then_inc(sem.pages_ok, 1)
                    for t in range(2):
                        dve.wait_ge(sem.rows_mm, t + 1)
                        if t:
                            dve.wait_ge(sem.rows_out, 16)
                        dve.tensor_copy(stg[:, :], bb[:, t, :]).then_inc(sem.rows_copied, 1)
                    stream(4 + 2 + 8 + 2)

                    def attend(n):
                        for t in range(2):
                            dve.wait_ge(sem.lg_mm, 2 * n + t + 1)
                            pr = prob(n)
                            if n == 0:
                                v(dve.tensor_scalar(pr, bb[:, 0:2, :].rearrange("p s (x k) -> p (s x) k", k=NP), SCALE, None, ALU.mult))
                            else:
                                for j in range(2):
                                    v(dve.scalar_tensor_tensor(pr[:, 2 * j:2 * j + 2, :], bb[:, j, :].rearrange("p (x k) -> p x k", k=NP),
                                                               SCALE, bh(pmask[:, t, :], 2), ALU.mult, ALU.add))
                            dve.tensor_reduce(nmx, pr, AX.X, ALU.max, negate=True).then_inc(sem.lg_ok, 1)
                            dve.wait_ge(sem.ex_ok, 2 * n + t + 1)
                            v(dve.reciprocal(rsm, rsm))
                            dve.tensor_tensor(pr, pr, bc(rsm, NP), ALU.mult).then_inc(sem.pr_ok, 1)
                            stream(3)
                            dve.wait_ge(sem.ov_mm, 2 * n + t + 1)
                            c = slice(t * P, (t + 1) * P)
                            if n == 0:
                                dve.tensor_copy(H(MQ)[:, :, c], heads4(bb[:, 0, :])).then_inc(sem.y_e, 1)
                            else:
                                dve.tensor_tensor(H(DZ)[:, :, c], H(DZ)[:, :, c], heads4(bb[:, 0, :]), ALU.mult).then_inc(sem.y_e, 1)
                            stream(1)

                    def sample_attend(n):
                        w = KS + n
                        dve.wait_ge(sem.qr_mm, n + 1)
                        if n:
                            v(dve.tensor_tensor(kvprod.rearrange("p (b h) -> p h b", b=NB), H(DK)[:, :, NP:T], H(DQ)[:, :, NP:T], ALU.mult))
                        dve.tensor_copy(qrow, bb[0:NB, 0, :]).then_inc(sem.qr_ok, 1)
                        stream(1)
                        for b in range(NB):
                            dve.wait_ge(sem.qb_mm, NB * n + b + 1)
                            dve.wait_ge(kv_in[b % 2], kv_count(n, b))
                            for t in range(2):
                                mm = dve.tensor_tensor(prodK[:, t, :, :].rearrange("p h d -> p (h d)"), kvb[:, b % 2, t, :],
                                                       bb[:, b % 2, :], ALU.mult)
                            mm.then_inc(sem.kv_used, 1)
                            dve.wait_ge(sem.kv_used, NB * n + b + 1)
                            mm = dve.tensor_reduce(ls.rearrange("p (t b h) -> p t b h", t=2, b=NB)[:, :, b, :], prodK, AX.X, ALU.add)
                            if b < NB - 1:
                                v(mm)
                            else:
                                mm.then_inc(sem.lx_ok, 1)
                            if b % 4 == 3:
                                stream(1)
                        dve.wait_ge(sem.lt_mm, n + 1)
                        v(dve.tensor_scalar(lrow[:, 0:w], bb[0:32, 2, 0:w], SCALE, None, ALU.mult))
                        dve.tensor_reduce(nmx[0:32, 0:1], lrow[:, 0:w], AX.X, ALU.max, negate=True).then_inc(sem.lt_ok, 1)
                        stream(1)
                        dve.wait_ge(sem.se_ok, n + 1)
                        v(dve.reciprocal(rsm[0:32, 0:1], rsm[0:32, 0:1]))
                        dve.tensor_scalar(lrow[:, 0:w], lrow[:, 0:w], rsm[0:32, 0:1], None, ALU.mult).then_inc(sem.lp_ok, 1)
                        dve.wait_ge(sem.lpt_mm, n + 1)
                        dve.tensor_copy(pts[:, 0:64 + 32 * n], bb[:, 3, 0:64 + 32 * n]).then_inc(sem.lpt_ok, 1)
                        dve.wait_ge(sem.lpt_ok, n + 1)
                        stream(2)
                        dve.wait_ge(sem.sv_mm, NB * (n + 1))
                        ov = bb[:, 0, 0:32].rearrange("p (b h) -> p h b", b=NB)
                        if n == 0:
                            v(dve.tensor_tensor(H(MZ)[:, :, 0:NP], H(MZ)[:, :, 0:NP], H(MQ)[:, :, 0:NP], ALU.mult))
                            dve.tensor_tensor(H(MZ)[:, :, NP:T], H(MZ)[:, :, NP:T], ov, ALU.mult).then_inc(sem.sy_ok, 1)
                        else:
                            pn = pts[:, 64:96].rearrange("p (b h) -> p h b", b=NB)
                            v(dve.tensor_tensor(pn, pn, H(DV)[:, :, NP:T], ALU.mult))
                            v(dve.tensor_tensor(pn, pn, ov, ALU.add))
                            dve.tensor_tensor(H(DZ)[:, :, NP:T], H(DZ)[:, :, NP:T], pn, ALU.mult).then_inc(sem.sy_ok, 1)
                        dve.wait_ge(sem.sy_ok, n + 1)

                    attend(0)
                    dve.wait_ge(sem.stored, ready(MZ))
                    sample_attend(0)
                    dve.wait_ge(sem.stored, NARROW_READY)
                    lam = qT[:, :, 0]
                    v(dve.tensor_scalar(zT, abT, cols[:, 0:1], None, ALU.add))
                    v(dve.scalar_tensor_tensor(spn, zT, -1.0, zT, ALU.mult, ALU.max))
                    dve.scalar_tensor_tensor(sln, lam, -1.0, lam, ALU.mult, ALU.max).then_inc(sem.small_a, 1)
                    dve.wait_ge(sem.small_b, 1)
                    v(dve.scalar_tensor_tensor(zT, zT, 0.0, spn, ALU.max, ALU.add))
                    v(dve.tensor_scalar(negA, negA, -1.0, None, ALU.mult))
                    v(dve.tensor_scalar(zT, zT, negA, None, ALU.mult))
                    v(dve.tensor_scalar(sp4, lam, -1.0, 0.0, ALU.mult, ALU.max))
                    v(dve.tensor_tensor(sp4, sp4, sln, ALU.add))
                    v(dve.tensor_scalar(sn4, sp4, -LRU_C, None, ALU.mult))
                    dve.tensor_scalar(sp4, sp4, LRU_C, None, ALU.mult).then_inc(sem.small_c, 1)
                    dve.wait_ge(sem.small_d, 1)
                    v(dve.tensor_copy(egs[:, 8:16], abT[:, NP:T]))
                    for k in range(2):
                        mm = dve.tensor_tensor(gate_mask[:, 64 * k:64 * k + 64].rearrange("p (r b) -> p r b", r=IH),
                                               bh(egs[:, 8 * k:8 * k + 8], IH), bc(id8, NB), ALU.mult)
                        if k == 0:
                            v(mm)
                    mm.then_inc(sem.small_e, 1)
                    dve.wait_ge(sem.gt_mm, 1)
                    v(dve.tensor_copy(gbt.rearrange("p k t r -> p (k t r)"), bb[:, 0, 0:32]))
                    dve.tensor_copy(egb.rearrange("p k h b -> p (k h b)"), bb[:, 1, 0:128]).then_inc(sem.gt_ok, 1)
                    stream(1)
                    dve.wait_ge(sem.gt_ok, 1)

                    def rotate(n, slot, dim, scale=1.0):
                        dve.wait_ge(sem.rot_mm, n + 1)
                        v(dve.scalar_tensor_tensor(tmpA, bb[:, :, 0:T], scale, bh(tb(f"sin{dim}")), ALU.mult, ALU.mult))
                        v(dve.scalar_tensor_tensor(H(slot), H(slot), scale, bh(tb(f"cos{dim}")), ALU.mult, ALU.mult))
                        dve.tensor_tensor(H(slot), H(slot), tmpA, ALU.add).then_inc(sem.rot_ok, 1)
                        stream(1)
                        dve.wait_ge(sem.rot_ok, n + 1)

                    rotate(0, IQ, ID)
                    dve.wait_ge(sem.ki_mm, 1)
                    v(dve.tensor_tensor(KI[:, :], bb[:, 0, 0:T], tb("cos64"), ALU.mult))
                    v(dve.tensor_tensor(tmpA[:, 0, :], bb[:, 1, 0:T], tb("sin64"), ALU.mult))
                    v(dve.tensor_tensor(KI[:, :], KI[:, :], tmpA[:, 0, :], ALU.add))
                    for t in range(2):
                        v(dve.tensor_scalar(wtok[:, t, :], bb[:, 2, t * 72 + ID:(t + 1) * 72], WSCALE, None, ALU.mult))
                    v(dve.tensor_scalar(wts, bb[0:NB, 2, 2 * 72 + ID:3 * 72], WSCALE, None, ALU.mult))
                    for k in range(2):
                        mm = dve.tensor_tensor(lw[:, 64 * k:64 * k + 64].rearrange("p (b h) -> p b h", b=NB), bh(wts, NB),
                                               tb("blk_heads")[0:NB, :].rearrange("p (b h) -> p b h", b=NB), ALU.mult)
                        if k == 0:
                            v(mm)
                    mm.then_inc(sem.ki_ok, 1)
                    stream(1)
                    dve.wait_ge(sem.qd_mm, 1)
                    v(dve.tensor_copy(qd.rearrange("p h b -> p (h b)"), bb[:, 3, 0:64]))
                    for k in range(2):
                        half = slice(ID * k, ID * (k + 1))
                        v(dve.tensor_copy(Qblk[half, 64 * k:64 * k + 64].rearrange("p (b h) -> p h b", b=NB),
                                          bb[half, 3, 0:64].rearrange("p (h b) -> p h b", h=IH)))
                    dve.tensor_copy(mws[:, :], bb[:, 0, 0:P]).then_inc(sem.qd_ok, 1)
                    dve.wait_ge(sem.new_mm, 1)
                    dve.wait_ge(sem.memv_out, 16)
                    new = tmpA[0:NB, 1, 0:64].rearrange("p (h b) -> p h b", h=IH)
                    v(dve.scalar_tensor_tensor(new, bb[0:NB, 1, 0:64].rearrange("p (h b) -> p h b", h=IH), 0.0, bh(id8, IH), ALU.max, ALU.mult))
                    v(dve.tensor_reduce(n88, new, AX.X, ALU.add))
                    v(dve.tensor_tensor(n88, n88, wts, ALU.mult))
                    dve.tensor_reduce(srow[:, PAST:PAST + 1], n88, AX.X, ALU.add).then_inc(sem.new_ok, 1)
                    stream(1)
                    for j in range(8):
                        dve.wait_ge(sem.ik_mm, j + 1)
                        dve.scalar_tensor_tensor(ikr.rearrange("p (u x) -> p u x", u=8), bb[:, 2:4, :].rearrange("p s (u x) -> p (s u) x", x=P),
                                                 0.0, bh(mws[:, :], 8), ALU.max, ALU.mult).then_inc(sem.ik_rel, 1)
                        dve.wait_ge(sem.ik_sc, j + 1)
                        dve.tensor_copy(scs[:, 16 * j:16 * j + 16], bb[:, 0, 0:16]).then_inc(sem.sc_ok, 1)
                        stream(1)
                    dve.wait_ge(sem.gc_mm, 1)
                    v(dve.tensor_copy(gct.rearrange("p t h -> p (t h)"), bb[:, 0, 0:2 * NH]))
                    gcb = bb[:, 1:3, :].rearrange("p s (x n) -> p (s x) n", n=NP)
                    for h in range(NH):
                        v(dve.scalar_tensor_tensor(dt0[:, h, :], gcb[:, h, :], gct[:, 0, h:h + 1], nm, ALU.subtract, ALU.add))
                        v(dve.scalar_tensor_tensor(dt1[:, h, :], gcb[:, h, P:NP], gct[:, 1, h:h + 1], nm[:, 0:P], ALU.subtract, ALU.add))
                    v(dve.tensor_tensor(ktl[:, 0, :], gcb[:, :, NP - 1], gct[:, 0, :], ALU.subtract))
                    dve.tensor_tensor(ktl[:, 1, :], gcb[:, :, NP - 1], gct[:, 1, :], ALU.subtract).then_inc(sem.dt_raw, 1)
                    stream(1)

                    def conv(i, s):
                        dve.wait_ge(sem.stored, ready(s))
                        dve.wait_ge(sem.tails, i + 1)
                        if i == 0:
                            dve.wait_ge(sem.rows_out, 32)
                        elif i < 3:
                            dve.wait_ge(sem.tail_out, 32 * i)
                        else:
                            dve.wait_ge(sem.st_out, 32)
                        dve.tensor_copy(stg[0:11, :], bb[0:11, 0, :]).then_inc(sem.tails_ok, 1)
                        if i >= 2:
                            dve.wait_ge(sem.conv_act, i - 1)
                        out = tmps[i % 2]
                        for c in range(CPS):
                            q = CPS * s + c
                            x, y = H(s)[:, c, :], out[:, c, :]
                            v(dve.tensor_scalar(y, x, pT[:, q, 3:4], pT[:, q, 4:5], ALU.mult, ALU.add))
                            for k in range(1, 4):
                                wk = pT[:, q, 3 - k:4 - k]
                                v(dve.scalar_tensor_tensor(y[:, k:NP], x[:, 0:NP - k], wk, y[:, k:NP], ALU.mult, ALU.add))
                                mm = dve.scalar_tensor_tensor(y[:, NP:T], pT[:, q, 7 + 3 - k:31:3], wk, y[:, NP:T], ALU.mult, ALU.add)
                                if (c, k) != (CPS - 1, 3):
                                    v(mm)
                        mm.then_inc(sem.conv_done, 1)

                    def normed(n, s):
                        dve.wait_ge(sem.rs, n)
                        v(dve.reciprocal(tmpA, tmpA))
                        dve.tensor_tensor(H(s), H(s), tmpA, ALU.mult).then_inc(sem.normed, 1)
                        stream(1)
                        dve.wait_ge(sem.normed, n)

                    for i, s in enumerate((GQ, GK, GV)):
                        conv(i, s)
                        stream(1)
                    stream(1)
                    normed(1, GQ)
                    normed(2, GK)

                    dve.wait_ge(sem.tok_mm, 1)
                    dve.wait_ge(sem.dt_ok, 1)
                    for t in range(2):
                        v(dve.tensor_tensor(heads4(bv[:, t, :]), heads4(bb[:, t, :]), bc(gbt[:, 1, t, NH:2 * NH], P), ALU.mult))
                        mm = dve.tensor_tensor(heads4(kzA[:, t, :]), heads4(bb[:, 2 + t, :]), bc(ktl[:, t, :], P), ALU.mult)
                        if t == 0:
                            v(mm)
                    mm.then_inc(sem.tok_ok, 1)
                    stream(1)
                    dve.wait_ge(sem.kk_mm, 1)
                    dve.wait_ge(sem.tail_out, 96)
                    strict = bh(tb("strict_t"))
                    v(dve.tensor_tensor(btT, heads4(bb[:, 2, :]), dt0[:, :, P:NP], ALU.mult))
                    for t in range(2):
                        v(dve.tensor_tensor(tri_t(t), heads4(bb[:, t, :]), (dt0[:, :, 0:P], dt1)[t], ALU.mult))
                        dve.tensor_tensor(tri_t(t), tri_t(t), strict, ALU.mult).then_inc(sem.kk_ok, 1)
                    stream(1)
                    dve.wait_ge(sem.row_in, 16)
                    dve.wait_ge(sem.tab_in, 16)

                    def mask(i):
                        return bh(tabs[:, i * P:(i + 1) * P])

                    for t in range(2):
                        beta = bc(gbt[:, 1, t, NH:2 * NH], P)
                        dve.wait_ge(sem.inv_T, t + 1)
                        dve.tensor_tensor(amat, heads4(bb[:, 3, :]), beta, ALU.mult).then_inc(sem.inv_at, 1)
                        dve.wait_ge(sem.inv_at, t + 1)
                        v(dve.tensor_tensor(xinv, amat, mask(0), ALU.mult))
                        v(dve.tensor_tensor(xinv, bh(ident), xinv, ALU.subtract))
                        dve.wait_ge(sem.at_mm, t + 1)
                        v(dve.tensor_copy(atm, heads4(bb[:, 3, :])))
                        v(dve.tensor_tensor(xinvT, atm, mask(1), ALU.mult))
                        v(dve.tensor_tensor(xinvT, bh(ident), xinvT, ALU.subtract))
                        for lv in range(6):
                            n = 6 * t + lv
                            dve.tensor_tensor(bmat, atm, mask(2 + lv), ALU.mult).then_inc(sem.lvl_bt, 1)
                            if lv:
                                topk()
                            stream(1)
                            dve.wait_ge(sem.z_mm, n + 1)
                            if lv < 5:
                                v(dve.tensor_tensor(xinv, xinv, heads4(bb[:, 3, :]), ALU.subtract))
                            dve.tensor_tensor(xinvT, xinvT, heads4(bb[:, 0, :]), ALU.subtract).then_inc(sem.z_ok, 1)
                            dve.wait_ge(sem.z_ok, n + 1)
                            if lv == 5:
                                topk()
                                stream(1)
                        if t == 1:
                            dve.wait_ge(sem.bt_mm, 1)
                            v(dve.tensor_tensor(bmat, heads4(bb[:, 3, :]), beta, ALU.mult))
                            dve.tensor_tensor(heads4(bv[:, 1, :]), heads4(bv[:, 1, :]), bmat, ALU.subtract).then_inc(sem.bt_ok, 1)
                        dve.wait_ge(sem.u_mm, t + 1)
                        dve.tensor_copy(bv[:, t, :], bb[:, 3, :]).then_inc(sem.u_ok, 1)
                        stream(1)
                    dve.wait_ge(sem.pt_mm, 1)
                    two = bb[:, 0:2, :].rearrange("p s (x n) -> p (s x) n", n=NP)
                    v(dve.tensor_tensor(dt0, dt0, two, ALU.mult))
                    dve.tensor_tensor(dt1, dt1, heads4(bb[:, 2, :]), ALU.mult).then_inc(sem.pt_ok, 1)
                    stream(1)
                    dve.wait_ge(sem.o_mm, 1)
                    v(dve.tensor_copy(H(GQ)[:, :, 0:NP], two))
                    dve.tensor_copy(stg[:, :], bb[:, 2, :]).then_inc(sem.st_ok, 1)
                    topk()
                    stream(1)

                    def samples_step(n, kslot, qslot, vslot):
                        ks, qs, vs = (H(s)[:, :, NP:T] for s in (kslot, qslot, vslot))
                        v(dve.tensor_copy(kq(n)[:, :, :, 0], ks))
                        v(dve.tensor_copy(kq(n)[:, :, :, 1], qs))
                        dve.tensor_tensor(prod(n).rearrange("p (h b) -> p h b", h=NH), ks, qs, ALU.mult).then_inc(sem.kq_ok, 1)
                        dve.wait_ge(sem.qk_mm, n + 1)
                        v(dve.tensor_copy(qkb.rearrange("p h b -> p (h b)"), bb[:, 0, 0:NH * NB]))
                        dve.tensor_copy(ktok(n), bb[0:NB, 1, :]).then_inc(sem.qk_ok, 1)
                        topk()
                        stream(1)
                        gam = egb[:, 0, 0:NH, :] if n == 0 else tb("gamma").rearrange("p (h b) -> p h b", h=NH)
                        for h in range(NH):
                            m = NH * n + h
                            eg = gam[:, h, :]
                            dve.wait_ge(sem.sk_mm, m + 1)
                            sk = bb[:, 0, 0:2 * NB].rearrange("p (b k) -> p b k", k=2)
                            if n == 0:
                                v(dve.tensor_tensor(s8[0], sk[:, :, 0], eg, ALU.mult))
                                v(dve.tensor_tensor(s8[0], vs[:, h, :], s8[0], ALU.subtract))
                                dve.tensor_tensor(vnew(n)[:, h, :], s8[0], egb[:, 1, NH + h, :], ALU.mult).then_inc(sem.vn_ok, 1)
                            else:
                                dve.tensor_copy(vnew(n)[:, h, :], vs[:, h, :]).then_inc(sem.vn_ok, 1)
                            dve.wait_ge(sem.vn_ok, m + 1)
                            v(dve.tensor_tensor(s8[0], sk[:, :, 1], eg, ALU.mult))
                            v(dve.tensor_tensor(s8[1], qkb[:, h, :], vnew(n)[:, h, :], ALU.mult))
                            v(dve.tensor_tensor(qs[:, h, :], s8[0], s8[1], ALU.add))
                            S = sbuf(n)[:, h % 2, :, :]
                            dve.wait_ge(stin[h % 2], 16 * (m // 2 + 1))
                            v(dve.tensor_tensor(S, S, bc(eg, HD), ALU.mult))
                            stream(1)
                            dve.wait_ge(sem.vt_mm, m + 1)
                            dve.tensor_tensor(vmask(n).rearrange("p (b e) -> p b e", b=NB), bh(bb[0:NB, 1, 0:P], NB), bc(id8, P), ALU.mult)\
                                .then_inc(sem.vm_ok, 1)
                            dve.wait_ge(sem.op_mm, m + 1)
                            dve.tensor_tensor(S, S, bb[:, 2:4, :].rearrange("p s (b e) -> p (s b) e", e=HD), ALU.add).then_inc(sem.s_new, 1)
                            topk()
                            if h % 2 == 0:
                                stream(1)

                    samples_step(0, GK, GQ, GV)
                    dve.wait_ge(sem.rs, 3)
                    v(dve.reciprocal(tmpA, tmpA))
                    v(dve.scalar_tensor_tensor(H(GQ), H(GQ), normw, tmpA, ALU.mult, ALU.mult))
                    dve.wait_ge(sem.stored, ready(GZ))
                    dve.tensor_tensor(H(GZ), H(GZ), H(GQ), ALU.mult).then_inc(sem.normed, 1)
                    topk()
                    stream(1)
                    dve.wait_ge(sem.normed, 3)

                    rotate(1, RQ, HD)
                    rotate(2, RK, HD, SCALE)
                    dve.wait_ge(sem.tok_mm, 2)
                    for t in range(2):
                        v(dve.tensor_copy(rv[:, t, :], bb[:, t, :]))
                        mm = dve.tensor_tensor(heads4(kzC[:, t, :]), heads4(bb[:, 2 + t, :]), bc(tb("zeta")[:, NH * t:NH * t + NH], P), ALU.mult)
                        if t == 0:
                            v(mm)
                    mm.then_inc(sem.tok_ok, 1)
                    topk()
                    stream(1)
                    dve.wait_ge(sem.pt_mm, 2)
                    dve.wait_ge(sem.decays_in, 16)
                    rdm = heads4(tabs[:, :])
                    v(dve.tensor_tensor(rt0, two, rdm, ALU.mult))
                    dve.tensor_tensor(rt1, heads4(bb[:, 2, :]), rdm[:, :, 0:P], ALU.mult).then_inc(sem.pt_ok, 1)
                    topk()
                    stream(1)
                    dve.wait_ge(sem.o_mm, 2)
                    v(dve.tensor_copy(H(RQ)[:, :, 0:NP], two))
                    dve.wait_ge(sem.st_out, 16)
                    dve.tensor_copy(stg[:, :], bb[:, 2, :]).then_inc(sem.st_ok, 1)
                    topk()
                    stream(1)
                    samples_step(1, RK, RQ, RV)
                    dve.wait_ge(sem.mean_mm, 1)
                    dve.scalar_tensor_tensor(H(RQ), bb[:, :, 0:T], -1.0 / HD, H(RQ), ALU.mult, ALU.add).then_inc(sem.mean_ok, 1)
                    stream(1)
                    normed(4, RQ)
                    dve.wait_ge(sem.stored, ready(RZ))
                    dve.tensor_tensor(H(RZ), H(RZ), H(RQ), ALU.mult).then_inc(sem.yc_ok, 1)

                    conv(3, LX)
                    stream(1 + 2)
                    dve.wait_ge(sem.lru_act, 2)
                    v(dve.tensor_tensor(lru(1), lru(1), H(LX), ALU.mult))
                    dve.wait_ge(sem.lru_a, 1)
                    v(dve.tensor_scalar(lru(0), lru(3), 1.0, None, ALU.add))
                    v(dve.reciprocal(lru(0), lru(0)))
                    dve.scalar_tensor_tensor(lru(0), lru(3), 2.0, lru(0), ALU.mult, ALU.mult).then_inc(sem.lru_b, 1)
                    dve.wait_ge(sem.lru_c, 1)
                    stream(2)
                    v(dve.tensor_tensor(lru(1), lru(1), lru(0), ALU.mult))
                    for c in range(CPS):
                        v(dve.tensor_tensor_scan(H(LX)[:, c, 0:NP], lru(2)[:, c, 0:NP], lru(1)[:, c, 0:NP], 0.0, ALU.mult, ALU.add))
                    v(dve.tensor_tensor(H(LX)[:, :, NP:T], lru(2)[:, :, NP:T], qT[:, :, 3:11], ALU.mult))
                    dve.tensor_tensor(H(LX)[:, :, NP:T], H(LX)[:, :, NP:T], lru(1)[:, :, NP:T], ALU.add).then_inc(sem.lru_o, 1)
                    topk(2)
                    stream(2)
                    dve.wait_ge(sem.lru_o, 1)
                    dve.wait_ge(sem.stored, ready(LZ))
                    v(dve.tensor_tensor(H(LZ), H(LZ), H(LX), ALU.mult))
                    dve.wait_ge(sem.h_mm, 1)
                    dve.wait_ge(sem.tail_out, 128)
                    dve.tensor_copy(stg[0:NB + 1, :], bb[0:NB + 1, 0, :]).then_inc(sem.h_rows, 1)
                    topk()
                    stream(1)

                    rotate(3, DQ, HD)
                    rotate(4, DK, HD)
                    dve.wait_ge(sem.lru_out, 32)
                    for j in range(7):
                        dve.wait_ge(sem.rows_mm, 3 + j)
                        if j and j not in (4,):
                            dve.wait_ge(sem.rows_out, 32 + 16 * j)
                        m = NB if j in (2, 5) else P
                        if j < 6:
                            dst = vrow[:, j - 3, :] if j in (3, 4) else stg[0:m, :]
                            dve.tensor_copy(dst, bb[0:m, 0, :]).then_inc(sem.rows_copied, 1)
                            if j % 3 != 1:
                                stream(1)
                        else:
                            v(dve.tensor_copy(stg[:, 0:2 * ID], bb[:, 0, 0:2 * ID]))
                            dve.tensor_copy(stg[0:NB, 2 * ID:3 * ID], bb[0:NB, 0, 2 * ID:3 * ID]).then_inc(sem.rows_copied, 1)
                    for t in range(2):
                        dve.wait_ge(sem.pidx_rel, t + 1)
                        v(dve.scalar_tensor_tensor(pscore, relus[:, 0:NP], wtok[:, t, 0:1], cm[t], ALU.mult, ALU.add))
                        for j in range(1, IH):
                            mm = dve.scalar_tensor_tensor(pscore, relus[:, (4 * (j % 2) + j // 2) * NP:][:, 0:NP], wtok[:, t, j:j + 1], pscore, ALU.mult, ALU.add)
                            if j < IH - 1:
                                v(mm)
                        mm.then_inc(sem.pidx_acc, 1)
                        dve.wait_ge(sem.pidx_acc, t + 1)
                        for r in range(KP // 8):
                            if r == 4:
                                stream(1)
                            v(dve.max(pm8[:, :], pscore))
                            v(dve.match_replace(pscore, pm8[:, :], pscore, TAKEN))
                        v(dve.tensor_scalar(pmask[:, t, :], pscore, TAKEN, None, ALU.is_equal))
                        v(dve.tensor_scalar(pmask[:, t, :], pmask[:, t, :], -1.0, BIG, ALU.add, ALU.mult))
                        v(dve.tensor_tensor(pmask[:, t, :], pmask[:, t, :], cm[t], ALU.add))
                        stream(1)
                    attend(1)
                    topk(KS // 8)

                    v(dve.tensor_scalar(hiloU[:, 0, :], picked[:, :], 7, None, ALU.logical_shift_right))
                    v(dve.tensor_scalar(hiloU[:, 1, :], picked[:, :], PAGE - 1, None, ALU.bitwise_and))
                    v(dve.tensor_copy(hilo, hiloU))
                    v(dve.tensor_scalar(maskrow[:, 0:KS], hilo[:, 0, :], float(NPG), -BIG, ALU.is_equal, ALU.mult))
                    v(dve.tensor_reduce(nsel, maskrow[:, 0:KS], AX.X, ALU.min))
                    dve.tensor_scalar(maskrow[:, KS:KS + 1], nsel, -1.0, -BIG, ALU.mult, ALU.add).then_inc(sem.hl_ok, 1)

                    dve.wait_ge(sem.hl_mm, 1)
                    hl = bb[:, 0, 0:32].rearrange("p (k t b) -> p k t b", k=2, t=2)
                    v(dve.tensor_scalar(goff[:, 8:9], lcount, float(n_pool * PAGE), None, ALU.mult))
                    for t in range(2):
                        v(dve.tensor_tensor(eqs, bh(tb("iota"), NB), bc(hl[:, 0, t, :], NPG), ALU.is_equal))
                        v(dve.tensor_tensor(eqs, eqs, ptB[:, :].rearrange("p (b g) -> p b g", b=NB), ALU.mult))
                        v(dve.tensor_reduce(rowf[:, NB * t:NB * t + NB], eqs, AX.X, ALU.add))
                    v(dve.scalar_tensor_tensor(rowf, rowf, float(PAGE), bb[:, 0, 16:32], ALU.mult, ALU.add))
                    v(dve.tensor_scalar(rowf, rowf, goff[:, 8:9], None, ALU.add))
                    dve.tensor_copy(rowsU[:, :, :].rearrange("p t b -> p (t b)"), rowf).then_inc(sem.rows_ok, 1)
                    stream(2)
                    sample_attend(1)
                    stream(None)

                    dve.wait_ge(sem.ln_sum, 1)
                    for q in range(4):
                        x4 = xT[:, 4 * q:4 * q + 4, :]
                        dve.scalar_tensor_tensor(x4, bh(bb[:, 0, 0:T]), -1.0 / D, x4, ALU.mult, ALU.add).then_inc(sem.ln_cen, 1)
                    dve.wait_ge(sem.ln_rs, 1)
                    dve.wait_ge(sem.ln_cen, 4)
                    v(dve.reciprocal(tmpA[:, 0, :], tmpA[:, 0, :]))
                    for q in range(4):
                        x4 = xT[:, 4 * q:4 * q + 4, :]
                        dve.tensor_tensor(x4, x4, bh(tmpA[:, 0, :]), ALU.mult).then_inc(sem.ln_x, 1)
                    dve.tensor_scalar(lcount, lcount, 1.0, None, ALU.add).then_inc(sem.lc_ok, 1)

                @block.gpsimd
                def _(pool):
                    def flat(ap):
                        return at_l(ap).rearrange("b t h d -> (b t) (h d)")

                    outs = []

                    def put(dst, src, s):
                        pool.dma_start(dst, src).then_inc(s, 16)

                    def kv_loads(n, k_src, v_src):
                        for kind, src in enumerate((k_src, v_src)):
                            for b in range(NB):
                                if kind == 0 and b < 2:
                                    if n:
                                        pool.wait_ge(sem.y_e, 4)
                                    else:
                                        pool.wait_ge(sem.memT_ok, 8)
                                elif kind == 0:
                                    pool.wait_ge(sem.kv_used, NB * n + b - 1)
                                elif b < 2:
                                    pool.wait_ge(sem.kv_used, NB * n + NB - 1 + b)
                                else:
                                    pool.wait_ge(sem.sv_mm, NB * n + b - 1)
                                if n == 0:
                                    pool.dma_start(kvb[:, b % 2, :, :], src[b].rearrange("(t p) h d -> p t (h d)", p=P))\
                                        .then_inc(kv_in[b % 2], 16)
                                else:
                                    for t in range(2):
                                        pool.indirect_dma_start(kvb[:, b % 2, t, :], None, src,
                                                                bass.IndirectOffsetOnAxis(ap=rowsU[:, t, b:b + 1], axis=0))\
                                            .then_inc(kv_in[b % 2], 16)

                    for t in range(2):
                        pool.wait_ge(sem.rows_copied, t + 1)
                        put(flat(o.p_mem_k)[t * P:(t + 1) * P, :], stg[:, :], sem.rows_out)
                    pool.wait_ge(sem.stored, MEMKV_READY)
                    put(flat(o.p_mem_v).rearrange("(t p) n -> p t n", p=P), mvr, sem.memv_out)
                    kv_loads(0, at_l(a.cache_mem_k), at_l(a.cache_mem_v))
                    pool.wait_ge(sem.y_e, 2)
                    pool.wait_ge(sem.pages_ok, 1)
                    ikp = a.cache_dsa_idx_k.rearrange("l g (j t) d -> (l g j) (t d)", j=8)
                    for j in range(8):
                        if j >= 2:
                            pool.wait_ge(sem.ik_T, j - 1)
                        pool.indirect_dma_start(ik[:, j % 2, :], None, ikp, bass.IndirectOffsetOnAxis(ap=pagesU[:, j:j + 1], axis=0))\
                            .then_inc(gath[j % 2], 16)
                    pool.wait_ge(sem.sc_ok, 8)
                    pool.dma_start(srow[:, 0:PAST], scs[:, :]).then_inc(sem.row_in, 16)

                    def tail(i, s):
                        pool.wait_ge(sem.tails_ok, i + 1)
                        c = slice(s * W, (s + 1) * W)
                        put(at_l(o.p_conv).rearrange("b j n -> (b j) n")[:, c], stg[0:3, :], sem.tail_out)
                        put(at_l(o.s_conv)[:, 2, c], stg[3:11, :], sem.tail_out)

                    for i, s in enumerate((GQ, GK, GV)):
                        tail(i, s)
                    put(at_l(o.s_conv)[:, 0:2, :], at_l(a.cache_conv)[:, 1:3, :], sem.cp_out)
                    pool.wait_ge(sem.z_ok, 12)
                    pool.dma_start(tabs[:, :], a.decays).then_inc(sem.decays_in, 16)

                    def states(n, src, pdst, dst):
                        pool.wait_ge(sem.st_ok, n + 1)
                        put(at_l(pdst).rearrange("b h d e -> d (b h) e"), heads4(stg[:, :]), sem.st_out)
                        s_in, s_to = (at_l(x).rearrange("b h d e -> d h b e") for x in (src, dst))
                        for h in range(2):
                            pool.dma_start(sbuf(n)[:, h, :, :], s_in[:, h, :, :]).then_inc(stin[h], 16)
                        for h in range(NH):
                            m = NH * n + h
                            pool.wait_ge(sem.s_new, m + 1)
                            put(s_to[:, h, :, :], sbuf(n)[:, h % 2, :, :], sem.s_out)
                            if h + 2 < NH:
                                pool.wait_ge(sem.s_out, 16 * (m + 1))
                                pool.dma_start(sbuf(n)[:, h % 2, :, :], s_in[:, h + 2, :, :]).then_inc(stin[h % 2], 16)

                    states(0, a.state_gdn, o.p_gdn, o.s_gdn)
                    pool.wait_ge(sem.pt_ok, 2)
                    for i, w in enumerate((a.lru_w_r, a.lru_w_i)):
                        pool.dma_start(lruw[:, i, :, :], at_l(w).rearrange("h i j -> i h j")).then_inc(sem.lw_in, 16)
                    states(1, a.state_ret, o.p_ret, o.s_ret)
                    tail(3, LX)
                    pool.wait_ge(sem.h_rows, 1)
                    put(o.p_lru[bass.ds(l, 1)].rearrange("z b n -> (z b) n"), stg[0:1, :], sem.lru_out)
                    put(at_l(o.s_lru), stg[1:NB + 1, :], sem.lru_out)
                    for j in range(6):
                        pool.wait_ge(sem.rows_copied, 3 + j)
                        pd, sd = (o.p_dsa_k, o.s_dsa_k) if j < 3 else (o.p_dsa_v, o.s_dsa_v)
                        t = j % 3
                        if t < 2:
                            put(flat(pd)[t * P:(t + 1) * P, :], stg[:, :] if j < 3 else vrow[:, t, :], sem.rows_out)
                        else:
                            put(flat(sd), stg[0:NB, :], sem.rows_out)
                    pool.wait_ge(sem.rows_copied, 9)
                    for t in range(2):
                        put(at_l(o.p_dsa_ik).rearrange("b t d -> (b t) d")[t * P:(t + 1) * P, :], stg[:, t * ID:(t + 1) * ID], sem.rows_out)
                    put(at_l(o.s_dsa_ik).rearrange("b t d -> (b t) d"), stg[0:NB, 2 * ID:3 * ID], sem.rows_out)

                    pool.wait_ge(sem.rows_ok, 1)
                    kv_loads(1, a.cache_dsa_k.rearrange("l g t h d -> (l g t) (h d)"), a.cache_dsa_v.rearrange("l g t h d -> (l g t) (h d)"))
                    for s, n in ((sem.rows_out, 32 + 16 * 9), (sem.memv_out, 16), (sem.tail_out, 128), (sem.cp_out, 16),
                                 (sem.st_out, 32), (sem.s_out, 128), (sem.lru_out, 32)):
                        pool.wait_ge(s, n)
                    for s, n in ((gath[0], 64), (gath[1], 64), (sem.row_in, 16), (sem.lw_in, 32), (sem.decays_in, 16),
                                 (stin[0], 64), (stin[1], 64), (kv_in[0], kv_count(1, 14)), (kv_in[1], kv_count(1, 15))):
                        pool.wait_ge(s, n)
            clear_sems()

        with nc.Block() as block:
            @block.tensor
            def _(pe):
                n = 0
                for t in range(3):
                    m = P if t < 2 else NB
                    for q in range(4):
                        if n >= 4:
                            pe.wait_ge(sem.x_ok, n - 3)
                        for c in range(4):
                            mm = pe.transpose(mb[0:m, n % 4, c * P:(c + 1) * P], xT[:, 4 * q + c, t * P:t * P + m], ident)
                        mm.then_inc(sem.x_T, 1)
                        n += 1

            @block.vector
            def _(dve):
                for n in range(12):
                    t, q = divmod(n, 4)
                    m = P if t < 2 else NB
                    dst = xrow[0:m, t, :] if t < 2 else r1[0:NB, :]
                    dve.wait_ge(sem.x_T, n + 1)
                    dve.tensor_copy(dst[:, q * 512:(q + 1) * 512], mb[0:m, n % 4, :]).then_inc(sem.x_ok, 1)

            @block.sync
            def _(sp):
                sp.wait_ge(sem.x_ok, 8)
                sp.dma_start(o.y_prompt.rearrange("a (t p) n -> p (a t) n", p=P), xrow).then_inc(sem.y_out, 16)
                sp.wait_ge(sem.x_ok, 12)
                sp.dma_start(o.y_sample.rearrange("b t n -> (b t) n"), r1[0:NB, :]).then_inc(sem.y_out, 16)
                sp.wait_ge(sem.y_out, 32)


_INS = ['x_prompt', 'x_sample', 'cache_conv', 'cache_dsa_k', 'cache_dsa_v', 'cache_dsa_idx_k', 'cache_mem_k', 'cache_mem_v',
        'state_gdn', 'state_ret', 'state_lru', 'page_table', 'mem_prompt', 'w_in', 'conv_w', 'conv_b', 'gdn_a_log',
        'gdn_dt_bias', 'gdn_norm_w', 'lru_lambda', 'lru_w_r', 'lru_b_r', 'lru_w_i', 'lru_b_i', 'w_mem_kv', 'w_branch',
        'w_out', 'ln_g', 'ln_b']
_OUTS = [('y_prompt', (1, NP, D)), ('y_sample', (NB, 1, D)),
         ('p_conv', (DEPTH, 1, 3, D)), ('p_gdn', (DEPTH, 1, NH, HD, HD)), ('p_ret', (DEPTH, 1, NH, HD, HD)),
         ('p_lru', (DEPTH, 1, W)), ('p_dsa_k', (DEPTH, 1, NP, NH, HD)), ('p_dsa_v', (DEPTH, 1, NP, NH, HD)),
         ('p_dsa_ik', (DEPTH, 1, NP, ID)), ('p_mem_k', (DEPTH, 1, NMEM, NH, HD)), ('p_mem_v', (DEPTH, 1, NMEM, NH, HD)),
         ('s_conv', (DEPTH, NB, 3, D)), ('s_gdn', (DEPTH, NB, NH, HD, HD)), ('s_ret', (DEPTH, NB, NH, HD, HD)),
         ('s_lru', (DEPTH, NB, W)), ('s_dsa_k', (DEPTH, NB, 1, NH, HD)), ('s_dsa_v', (DEPTH, NB, 1, NH, HD)),
         ('s_dsa_ik', (DEPTH, NB, 1, ID))]


def kernel(**inputs):
    import numpy as _np
    import concourse.bacc as _bacc
    from concourse import mybir as _mybir
    from concourse.bass_utils import run_bass_kernel_spmd as _run

    nc = _bacc.Bacc("TRN2", target_bir_lowering=False, num_devices=1)
    arrays, ins = {}, {}
    fixed, at, levels, decays = tables()
    consts = {"fixed": fixed, "levels": levels, "decays": decays}
    for name in _INS + list(consts):
        x = _np.ascontiguousarray(consts[name] if name in consts else inputs[name])
        arrays[f"in_{name}_dram"] = x
        ins[name] = nc.dram_tensor(f"in_{name}_dram", x.shape, _mybir.dt.from_np(x.dtype), kind="ExternalInput").ap()
    outs = {}
    for name, shape in _OUTS:
        outs[name] = nc.dram_tensor(f"out_{name}_dram", shape, _mybir.dt.float32, kind="ExternalOutput").ap()
    trunk(nc, namedtuple("Inputs", ins)(**ins), namedtuple("Outputs", outs)(**outs), at, fixed.shape[1])
    r = _run(nc, [arrays], core_ids=[0])
    return tuple(r.results[0][f"out_{name}_dram"] for name, _ in _OUTS)
```

```python
import math
from contextlib import ExitStack
from itertools import islice
from collections import namedtuple

import numpy as np
import concourse.bass as bass
from concourse import mybir

ALU = mybir.AluOpType
ACT = mybir.ActivationFunctionType
AX = mybir.AxisListType
F32 = mybir.dt.float32
F32R = mybir.dt.float32r
U32 = mybir.dt.uint32
I32 = mybir.dt.int32

P = 128
D = 2048
KC = D // P
W = 512
NH = 4
HD = 128
DEPTH = 2
NP = 256
NB = 8
T = NP + NB
NMEM = 256
PAGE = 128
NPG = 16
PAST = NPG * PAGE
IH, ID = 8, 64
KP = min(256, NP // 4)
KS = min(256, (PAST + 1) // 4)
CPS = W // P
SCALE = HD ** -0.5
WSCALE = (IH * ID) ** -0.5
ALPHA = (2 * DEPTH) ** 0.25
LN_EPS, NORM_EPS = 1e-5, 1e-6
BIG = 1e30
TAKEN = -2.0 ** 127
LRU_C = 8.0

GQ, GK, GV, LX, RQ, RK, RV, DQ, DK, DV, DZ, RZ, LZ, IQ, MQ, MZ, GZ = range(17)
COL = {GQ: 0, GK: 512, GV: 1024, LX: 1536, GZ: 2048, DQ: 2568, DK: 3080, DV: 3592, DZ: 4104, IQ: 4616,
       RQ: 5200, RK: 5712, RV: 6224, RZ: 6736, LZ: 7248, MQ: 7760, MZ: 8272}
COL_NARROW, COL_GATE = ((2560, 8), (5128, 72)), 8784
PLACE = {GQ: 0, GK: 1, GV: 2, RQ: 3, RK: 4, RV: 5, DQ: 6, DK: 7, DV: 8, DZ: 9, RZ: 10, LZ: 11, IQ: 12, MQ: 13, GZ: 13,
         MZ: 14, LX: 14}
PLACES = 1 + max(PLACE.values())
NRING = 2

BRANCH = [(4, MZ), (0, GZ), (2, RZ), (3, LZ), (1, DZ)]
LAST = len(BRANCH) - 1


def plan():
    chunks = []

    def project(*slots):
        chunks.extend(("in", s, m) for s in slots for m in range(CPS))

    def gates(n):
        chunks.extend(("gate", n, m) for m in range(KC))

    project(MQ)
    chunks.extend(("narrow", 0, m) for m in range(2))
    chunks.extend(("mem", 0, m) for m in range(2 * CPS))
    project(MZ, IQ, DQ, RQ, GQ, GK, GV, GZ, RK, RV)
    gates(0)
    project(LX, RZ, LZ, DK, DV, DZ)
    for n in range(1, len(BRANCH)):
        gates(n)
    chunks.extend(("out", 0, m) for m in range(KC))
    return chunks


CHUNKS = plan()
RESULTS = [1 + (k == "gate") for k, _, _ in CHUNKS]
FIRST_RESULT = [sum(RESULTS[:i]) for i in range(len(CHUNKS))]
SPLIT = [i for i, (k, _, _) in enumerate(CHUNKS) if k != "mem"]
SPLIT_N = {i: n for n, i in enumerate(SPLIT)}
GATES_I = [i for i, (k, _, _) in enumerate(CHUNKS) if k == "gate"]
GATE_N = {i: n for n, i in enumerate(GATES_I)}


def _freed():
    n, out = {"stored": 0, "gate_act": 0, "merged_ok": 0, "out_ok": 0}, []
    for k, _, _ in CHUNKS:
        for s in {"gate": ("gate_act", "merged_ok"), "out": ("out_ok",)}.get(k, ("stored",)):
            n[s] += 1
            out.append((s, n[s]))
    return out


FREED = _freed()
MEMKV_READY, NARROW_READY = (FREED[FIRST_RESULT[max(i for i, x in enumerate(CHUNKS) if x[0] == kind)]][1]
                             for kind in ("mem", "narrow"))


def landed(i):
    return 16 * (i // NRING + 1)


def products(i):
    return FIRST_RESULT[i] + 1


def kv_count(n, i):
    return 16 * (i // 2 + 1) if n == 0 else 16 * NB + 32 * (i // 2 + 1)


def ready(slot):
    return FREED[FIRST_RESULT[CHUNKS.index(("in", slot, CPS - 1))]][1]


def tables():
    at, parts = {}, []

    def add(name, a):
        a = np.asarray(a, np.float32)
        if a.shape[0] < P:
            a = np.concatenate([a, np.zeros((P - a.shape[0], a.shape[1]), np.float32)])
        at[name] = (sum(p.shape[1] for p in parts), a.shape[1])
        parts.append(a)

    i = np.arange(P)
    eye = np.eye(P)
    add("ident", eye)
    add("tri", i[:, None] <= i[None, :])
    add("ones", np.ones((P, P)))

    def rot(half, heads):
        m = np.zeros((P, P))
        for h in range(heads):
            for d in range(half):
                a, b = 2 * half * h + d, 2 * half * h + half + d
                m[b, a], m[a, b] = -1.0, 1.0
        return m

    r64 = rot(ID // 2, 2)
    add("rot128", rot(HD // 2, 1))
    add("rot64", r64)
    lo = np.zeros((P, P))
    lo[:ID] = np.concatenate([eye[:ID, :ID], eye[:ID, :ID]], 1)
    hi = np.zeros((P, P))
    hi[ID:] = lo[:ID]
    rd = np.zeros((P, P))
    rd[:ID] = np.concatenate([r64[:ID, :ID], r64[:ID, :ID]], 1)
    add("dup_lo", lo)
    add("dup_hi", hi)
    add("rot_dup", rd)
    pos = np.concatenate([np.arange(NP), np.full(NB, PAST)]).astype(np.float32)
    for dim in (HD, ID):
        half = dim // 2
        inv = (np.float32(10000.0) ** (-np.arange(half, dtype=np.float32) / np.float32(half))).astype(np.float32)
        ang = (pos[None, :] * inv[:, None]).astype(np.float32)
        reps = P // half
        add(f"cos{dim}", np.tile(np.cos(ang), (reps, 1)))
        add(f"sin{dim}", np.tile(np.sin(ang), (reps, 1)))
    add("future_t", np.where(i[None, :] < i[:, None], -BIG, 0.0))
    add("zeros", np.zeros((P, P)))
    add("future", np.where(i[None, :] > i[:, None], -BIG, 0.0))
    add("never", np.full((P, P), -BIG))
    add("strict_t", i[None, :] > i[:, None])
    gamma = 1.0 - 2.0 ** (-5.0 - np.arange(NH))
    lg = np.log(gamma.astype(np.float32)).astype(np.float64)
    zeta = np.exp((NP - 1 - (np.arange(2)[None, :, None] * P + i[:, None, None])) * lg[None, None, :])
    add("zeta", zeta.reshape(P, 2 * NH))
    add("gamma", np.tile(np.repeat(np.exp(lg), NB)[None], (P, 1)))
    e8 = np.eye(NB)
    add("blk_pages", np.repeat(e8, NPG, 1))
    add("blk_heads", np.repeat(e8, IH, 1))
    add("rep_heads", np.repeat(e8, NH, 1))
    add("parity", np.stack([i < ID, i >= ID], 1))
    add("iota", np.tile(np.arange(NPG)[None], (P, 1)))
    add("eps", np.tile(np.array([[HD * NORM_EPS, NORM_EPS, LN_EPS]]), (P, 1)))
    fixed = np.concatenate(parts, 1)

    def level(s):
        same = i[:, None] // (2 * s) == i[None, :] // (2 * s)
        return same & (i[:, None] % (2 * s) >= s) & (i[None, :] % (2 * s) < s)

    lv = np.concatenate([level(1)] + [level(s).T for s in (1, 2, 4, 8, 16, 32, 64)], 1)
    k = np.arange(NP)
    dist = k[None, None, :] - i[:, None, None]
    rd = np.where(dist >= 0, np.exp(np.maximum(dist, 0) * lg[None, :, None]), 0.0)
    return fixed, at, lv.astype(np.float32), rd.reshape(P, NH * NP).astype(np.float32)


def trunk(nc, a, o, at, fixed_w):
    n_pool = a.cache_dsa_k.shape[1]
    with ExitStack() as ctx:
        def sb(name, shape, dt=F32):
            return ctx.enter_context(nc.sbuf_tensor(name, shape, dt))

        TMP = 2112
        ring = sb("ring", [P, NRING, KC, P])
        wsplit = sb("wsplit", [P, 2, 2, KC, P])
        bring = sb("bring", [P, 2, CPS, P])
        xsplit = sb("xsplit", [P, 2, KC, T])
        merged = sb("merged", [P, KC, T])
        gbuf = sb("gbuf", [P, T])
        work = sb("work", [P, TMP + PLACES * CPS * T])
        tab = sb("tab", [P, fixed_w])
        tabs = sb("tabs", [P, 1024])
        pT = sb("pT", [P, KC, 31])
        qT = sb("qT", [P, CPS, 11])
        memkv = sb("memkv", [P, 2052])
        mkT = memkv[:, 0:NH * NMEM].rearrange("p (h m) -> p h m", h=NH)
        mvr = memkv[:, NH * NMEM:NH * NMEM + 2 * W].rearrange("p (t n) -> p t n", t=2)
        stg = sb("stg", [P, W])
        srow = memkv[0:NB, 0:PAST + 1]
        small = sb("small", [P, 1000])
        m8 = sb("m8", [NB, 8])
        i8 = sb("i8", [NB, 8], U32)
        pm8 = sb("pm8", [P, 8])
        rowsU = sb("rowsU", [P, 2, NB], U32)
        pagesU = sb("pagesU", [P, 8], U32)

        mb = ctx.enter_context(nc.psum_tensor("mb", [P, 4, 512], F32))
        bb = ctx.enter_context(nc.psum_tensor("bb", [P, 4, 512], F32))

        def tb(name):
            o_, n = at[name]
            return tab[:, o_:o_ + n]

        ident, ones = tb("ident"), tb("ones")
        tri_ones = tab[:, at["tri"][0]:at["tri"][0] + 2 * P]
        nm = tab[:, at["future_t"][0]:at["future_t"][0] + 2 * P]
        cm = [tab[:, at["future"][0]:at["future"][0] + 2 * P], tab[:, at["zeros"][0]:at["zeros"][0] + 2 * P]]
        id8 = ident[0:NB, 0:NB]

        hbase = TMP

        def H(slot):
            b0 = hbase + PLACE[slot] * CPS * T
            return work[:, b0:b0 + CPS * T].rearrange("p (c n) -> p c n", n=T)

        def area(slot, off, n):
            b0 = hbase + PLACE[slot] * CPS * T + off
            return work[:, b0:b0 + n]

        tmpA = work[:, 0:CPS * T].rearrange("p (c n) -> p c n", n=T)
        tmpB = work[:, CPS * T:2 * CPS * T].rearrange("p (c n) -> p c n", n=T)
        tmps = [tmpA, tmpB]
        r1 = area(RK, 0, D)
        r2 = area(DQ, 0, W)
        memrow = area(GQ, 0, 2 * D).rearrange("p (t n) -> p t n", t=2)
        memT = area(DK, 0, KC * NMEM).rearrange("p (c n) -> p c n", n=NMEM)
        xrow = memrow
        pti = area(DK, 0, 1 + NB * NPG).bitcast(I32)
        xnew = area(GQ, 0, KC * T).rearrange("p (c n) -> p c n", n=T)
        yrow = area(RK, 0, 2 * D).rearrange("p (t n) -> p t n", t=2)
        ysrow = area(DV, 0, D)

        def hi(ap):
            return ap.bitcast(F32R)


        used = [0]

        def sm(n, parts=P):
            used[0] += n
            assert used[0] <= 1000
            return small[0:parts, used[0] - n:used[0]]

        abT = sm(T, NB)
        ikw = sm(T, 72)
        cols = sm(2, NB)
        negA = sm(1, NB)
        normw = sm(1)
        sp4 = sm(CPS)
        sn4 = sm(CPS)
        gbt = sm(32).rearrange("p (k t r) -> p k t r", k=2, t=2)
        gct = sm(2 * NH).rearrange("p (t h) -> p t h", t=2)
        ktl = sm(2 * NH).rearrange("p (t h) -> p t h", t=2)
        egb = sm(2 * IH * NB).rearrange("p (k h b) -> p k h b", k=2, h=IH)
        wtok = sm(2 * IH).rearrange("p (t h) -> p t h", t=2)
        wts = sm(IH, NB)
        ls = sm(64)
        pts = sm(96)
        nmx = sm(NH)
        rsm = sm(NH)
        lcount = sm(1)
        ptf = sm(1)
        goff = sm(9)
        rowf = sm(16)

        kvprod = sm(NH * NB)
        nsel = sm(1, NB)
        n88 = sm(IH, NB)
        zT, spn, msk = (tmpA[0:NB, i_, :] for i_ in range(3))
        sln = spl = sm(CPS)
        spe, sle = spn, sln
        gate_mask, egs = msk[:, 0:128], msk[:, 128:144]

        def zarea(off, n, parts=P):
            return area(DK, off, n)[0:parts]

        def garea(off, n, parts=P):
            return area(GQ, off, n)[0:parts]

        def heads4(ap):
            return ap.rearrange("p (h x) -> p h x", h=NH)

        def prob(n):
            return heads4((zarea, garea)[n](0, NH * NP))

        def probT(n):
            return (zarea, garea)[n](1024, 1024).rearrange("p (s h q) -> p s h q", s=2, h=NH)

        relus = garea(0, IH * NP)
        pmask = garea(2048, 2 * NP).rearrange("p (t k) -> p t k", t=2)
        pscore = garea(2560, NP)
        vrow = work[:, 0:2 * W].rearrange("p (t n) -> p t n", t=2)
        ik = zarea(0, 2048).rearrange("p (i x) -> p i x", i=2)
        ikT, ikr = zarea(2048, 1024), zarea(3072, 1024)
        lw = zarea(4096, 2 * NB * IH, NB)
        qd = zarea(4224, IH * NB).rearrange("p (h b) -> p h b", h=IH)
        dt_all = zarea(0, 1536)
        dt0, dt1 = heads4(zarea(0, 1024)), heads4(zarea(1024, 512))
        amat = ymat = heads4(zarea(1536, W))
        atm, xinv, xinvT = (heads4(zarea(o_, W)) for o_ in (2048, 2560, 3072))
        bmat, btT = (heads4(zarea(o_, W)) for o_ in (3584, 4096))

        def tri_t(t):
            return heads4(zarea(4608, W) if t == 0 else stg[:, :])

        bv = work[:, 0:1024].rearrange("p (t n) -> p t n", t=2)
        kzA = work[:, 1024:2048].rearrange("p (t n) -> p t n", t=2)
        rt0, rt1 = heads4(garea(0, 1024)), heads4(garea(1024, 512))
        rv = garea(1536, 1024).rearrange("p (t n) -> p t n", t=2)
        kzC = work[:, 0:1024].rearrange("p (t n) -> p t n", t=2)

        def sbuf(n):
            return (zarea, garea)[n](0, 2048).rearrange("p (i b e) -> p i b e", i=2, b=NB)

        def vmask(n):
            return (zarea, garea)[n](2048, 1024, NB)

        def ktok(n):
            return work[0:NB, 0:W]

        def kq(n):
            return work[:, 512:576].rearrange("p (h b k) -> p h b k", h=NH, b=NB)

        def prod(n):
            return work[:, 576:608]

        def vnew(n):
            return work[:, 608:640].rearrange("p (h b) -> p h b", h=NH)

        qkb = work[:, 640:672].rearrange("p (h b) -> p h b", h=NH)
        s8 = [work[:, 672 + 8 * i_:680 + 8 * i_] for i_ in range(2)]
        lruw = tabs[:, :].rearrange("p (i h j) -> p i h j", i=2, h=NH)

        def lru(i_):
            return H(i_) if i_ < 3 else tmpA

        kvb = garea(0, 2048).rearrange("p (i t n) -> p i t n", i=2, t=2)
        prodK = work[:, 0:1024].rearrange("p (t h d) -> p t h d", t=2, h=NH)
        qrow, lrow = work[0:NB, 1056:1568], work[0:32, 1568:1568 + KS + 1]
        maskrow = garea(2048, KS + 1, NB)
        hilo = work[0:NB, 0:2 * KS].rearrange("p (k n) -> p k n", k=2)
        hiloU = work[0:NB, 2 * KS:4 * KS].bitcast(U32).rearrange("p (k n) -> p k n", k=2)
        eqs = work[:, 0:NB * NPG].rearrange("p (b g) -> p b g", b=NB)
        KI = sb("KI", [P, T])
        Qblk = sb("Qblk", [P, P])
        ptB = sb("ptB", [P, NB * NPG])
        scm = sb("scm", [P, 2 * P])
        scs, mws = scm[:, 0:P], scm[:, P:2 * P]
        picked = scm[0:NB, 0:KS].bitcast(U32)

        names = """tables x_in x_T x_ok pages_in pages_ok params_in mem_in param_T param_cols mem_T memT_ok chunk_mm stored
            small_a small_b small_c small_d small_e gt_mm gt_ok gc_mm dt_raw dt_ok tails tails_ok tail_out conv_done
            conv_act sq ss rs normed mean_mm rot_mm rot_ok ki_mm ki_ok qd_mm qd_ok new_mm new_ok ik_T ik_copied ik_mm
            ik_rel ik_sc sc_ok row_in pidx_mm pidx_rel pidx_acc tok_mm tok_ok kk_mm kk_ok bt_mm bt_ok inv_T
            inv_at at_mm lvl_bt y_mm y_ok z_mm z_ok u_mm u_ok pt_mm pt_ok o_mm st_ok st_out kq_ok qk_mm qk_ok sk_mm
            vn_ok vt_mm vm_ok op_mm s_new s_out lw_in lru_mm lru_act lru_a lru_b lru_c lru_o lru_out h_mm h_rows
            lg_mm lg_ok ex_ok yc_ok hi_ok lo_ok xh_ok mh_ok ms_ok pr_ok pT_mm pT_ok ov_mm y_e qr_mm qr_ok qb_mm kv_used lt_mm lt_ok lx_ok lp_ok lpt_mm
            lpt_ok sv_mm sy_ok hl_ok hl_mm rows_ok rows_out rows_mm rows_copied tab_in gate_act merged_ok out_ok
            ln_sum ln_cen ln_sq ln_ss ln_rs ln_x y_out se_ok mean_ok memv_out lc_ok decays_in v_chain a_chain
            cp_out""".split()
        sem = namedtuple("Semaphores", names)(*[ctx.enter_context(nc.semaphore(n)) for n in names])
        by_name = dict(zip(names, sem))
        w_landed = [ctx.enter_context(nc.semaphore(f"w_landed{i}")) for i in range(NRING)]
        bw_landed = [ctx.enter_context(nc.semaphore(f"bw_landed{i}")) for i in range(2)]
        gath = [ctx.enter_context(nc.semaphore(f"gathered{i}")) for i in range(2)]
        stin = [ctx.enter_context(nc.semaphore(f"state_in{i}")) for i in range(2)]
        kv_in = [ctx.enter_context(nc.semaphore(f"kv_in{i}")) for i in range(2)]
        layer_sems = kv_in + list(sem) + w_landed + bw_landed + gath + stin

        def chain(eng, s):
            n = [0]

            def link(ins):
                n[0] += 1
                ins.then_inc(s, 1)
                eng.wait_ge(s, n[0])
            return link

        def clear_sems():
            nc.all_engine_barrier()
            nc.gpsimd.dma_reset()
            nc.all_engine_barrier()
            for i, s in enumerate(layer_sems):
                (nc.sync, nc.scalar, nc.tensor, nc.vector)[i % 4].sem_clear(s)
            nc.all_engine_barrier()

        with nc.Block() as block:
            @block.sync
            def _(sp):
                sp.dma_start(tab[:, :], a.fixed).then_inc(sem.tables, 16)
                sp.dma_start(xrow, a.x_prompt.rearrange("a (t p) n -> p (a t) n", p=P)).then_inc(sem.x_in, 16)
                sp.dma_start(r1[0:NB, :], a.x_sample.rearrange("b t n -> (b t) n")).then_inc(sem.x_in, 16)
                pt = a.page_table.rearrange("b g -> (b g)")
                sp.dma_start(pti[:, 0:1], pt.rearrange("(p o) -> p o", o=1)).then_inc(sem.pages_in, 16)
                sp.dma_start(pti[:, 1:], pt.partition_broadcast(P)).then_inc(sem.pages_in, 16)

            @block.tensor
            def _(pe):
                pe.wait_ge(sem.tables, 16)
                pe.wait_ge(sem.x_in, 32)
                for c in range(KC):
                    if c >= 4:
                        pe.wait_ge(sem.x_ok, c - 3)
                    for t in range(2):
                        pe.transpose(mb[:, c % 4, t * P:(t + 1) * P], xrow[:, t, c * P:(c + 1) * P], ident)
                    pe.transpose(mb[:, c % 4, NP:T], r1[0:NB, c * P:(c + 1) * P], id8).then_inc(sem.x_T, 1)

            @block.scalar
            def _(act):
                for c in range(KC):
                    act.wait_ge(sem.x_T, c + 1)
                    act.activation(hi(xsplit[:, 0, c, :]), mb[:, c % 4, 0:T], ACT.Copy).then_inc(sem.xh_ok, 1)

            @block.vector
            def _(dve):
                dve.memset(cols, 0.0)
                dve.memset(Qblk[:, :], 0.0)
                dve.memset(lcount, 0.0)
                dve.wait_ge(sem.pages_in, 32)
                dve.tensor_copy(ptf, pti[:, 0:1])
                dve.tensor_copy(ptB[:, :], pti[:, 1:])
                for c in range(KC):
                    dve.wait_ge(sem.xh_ok, c + 1)
                    dve.tensor_tensor(hi(xsplit[:, 1, c, :]), mb[:, c % 4, 0:T], xsplit[:, 0, c, :], ALU.subtract).then_inc(sem.x_ok, 1)
        clear_sems()

        with nc.Fori(0, DEPTH) as l:
            def at_l(ap):
                n = len(ap.shape)
                rest = " ".join(f"x{i}" for i in range(1, n))
                return ap[bass.ds(l, 1)].rearrange(f"z {rest} -> (z x1) " + " ".join(f"x{i}" for i in range(2, n)))

            w_in = at_l(a.w_in).rearrange("(k p) n -> p k n", p=P)
            w_mem = at_l(a.w_mem_kv).rearrange("(k p) n -> p k n", p=P)
            w_out = at_l(a.w_out).rearrange("(k p) n -> p k n", p=P)
            w_branch = at_l(a.w_branch).rearrange("b (k p) n -> p b k n", p=P)

            with nc.Block() as block:
                @block.sync
                def _(sp):
                    for i, (kind, x, m) in enumerate(CHUNKS):
                        if i >= NRING:
                            if CHUNKS[i - NRING][0] == "mem":
                                sp.wait_ge(sem.chunk_mm, products(i - NRING))
                            else:
                                sp.wait_ge(sem.lo_ok, SPLIT_N[i - NRING] + 1)
                        if kind == "narrow":
                            c0, n = COL_NARROW[m]
                        else:
                            c0 = m * P + (COL[x] if kind == "in" else COL_GATE + BRANCH[x][0] * D if kind == "gate" else 0)
                            n = P
                        w = {"mem": w_mem, "out": w_out}.get(kind, w_in)
                        sp.dma_start(ring[:, i % NRING, :, 0:n], w[:, :, c0:c0 + n]).then_inc(w_landed[i % NRING], 16)
                        if i - 1 in GATE_N:
                            _, n, m = CHUNKS[i - 1]
                            j = GATE_N[i - 1]
                            if j >= 2:
                                sp.wait_ge(sem.chunk_mm, products(GATES_I[j - 2]) + 1)
                            sp.dma_start(bring[:, j % 2, :, :], w_branch[:, BRANCH[n][0], :, m * P:(m + 1) * P])\
                                .then_inc(bw_landed[j % 2], 16)

                @block.tensor
                def _(pe):
                    chunks = iter(range(len(CHUNKS)))

                    def stream(n=1):
                        for i in islice(chunks, n):
                            (kind, x, m), g = CHUNKS[i], FIRST_RESULT[i]
                            if kind == "mem":
                                pe.wait_ge(w_landed[i % NRING], landed(i))
                            else:
                                pe.wait_ge(sem.lo_ok, SPLIT_N[i] + 1)
                            if g >= 4:
                                s, count = FREED[g - 4]
                                pe.wait_ge(by_name[s], count)
                            bank = mb[:, g % 4, :]
                            n = COL_NARROW[m][1] if kind == "narrow" else P
                            for q in range(KC):
                                first, last = q == 0, q == KC - 1
                                if kind == "mem":
                                    w = ring[:, i % NRING, q, :]
                                    if m < CPS:
                                        mm = pe.matmul(bank[:, 0:NMEM], w, memT[:, q, :], start=first, stop=last)
                                    else:
                                        for t in range(2):
                                            mm = pe.matmul(bank[:, t * P:(t + 1) * P], memT[:, q, t * P:(t + 1) * P], w,
                                                           start=(first and t == 0), stop=last, skip_group_check=True)
                                    continue
                                wh, wl = (hi(wsplit[:, SPLIT_N[i] % 2, j, q, 0:n]) for j in range(2))
                                ah, al = (hi(xsplit[:, j, q, :]) for j in range(2))
                                if kind == "out" and m == 0 and q % 4 == 0:
                                    pe.wait_ge(sem.ms_ok, q // 4 + 1)
                                pe.matmul(bank[0:n, 0:T], wh, ah, start=first, stop=False)
                                pe.matmul(bank[0:n, 0:T], wh, al, start=False, stop=False)
                                mm = pe.matmul(bank[0:n, 0:T], wl, ah, start=False, stop=last)
                            mm.then_inc(sem.chunk_mm, 1)
                            if kind == "gate":
                                j = GATE_N[i]
                                pe.wait_ge(bw_landed[j % 2], 16 * (j // 2 + 1))
                                s, count = FREED[g - 3]
                                pe.wait_ge(by_name[s], count)
                                y = H(BRANCH[x][1])
                                for q in range(CPS):
                                    mm = pe.matmul(mb[:, (g + 1) % 4, 0:T], bring[:, j % 2, q, :], y[:, q, :],
                                                   start=(q == 0), stop=(q == CPS - 1))
                                mm.then_inc(sem.chunk_mm, 1)

                    stream(4)
                    pe.wait_ge(sem.params_in, 16 * 12)
                    for c in range(KC):
                        pe.transpose(bb[:, 0, c * 31:(c + 1) * 31], r1[0:31, c * P:(c + 1) * P], ident[0:31, 0:31])
                    for c in range(CPS):
                        mm = pe.transpose(bb[:, 1, c * 11:(c + 1) * 11], r2[0:11, c * P:(c + 1) * P], ident[0:11, 0:11])
                    mm.then_inc(sem.param_T, 1)
                    stream(1)
                    pe.wait_ge(sem.mem_in, 16)
                    pe.wait_ge(sem.param_cols, 1)
                    for t in range(2):
                        for q in range(4):
                            n = 4 * t + q
                            if n >= 4:
                                pe.wait_ge(sem.memT_ok, n - 3)
                            for c in range(4):
                                mm = pe.transpose(bb[:, n % 4, c * P:(c + 1) * P],
                                                  memrow[:, t, (4 * q + c) * P:(4 * q + c + 1) * P], ident)
                            mm.then_inc(sem.mem_T, 1)
                    stream(1)
                    pe.wait_ge(sem.memT_ok, 8)
                    stream(8)

                    def to_rows(src, bank, cols_=(0, P)):
                        c0, c1 = cols_
                        for h in range(NH):
                            mm = pe.transpose(bb[0:c1 - c0, bank, h * P:(h + 1) * P], src[:, h, c0:c1], ident)
                        return mm

                    def attend(n, q, k, v):
                        for t in range(2):
                            if n == 0 and t == 0:
                                pe.wait_ge(sem.rows_copied, 2)
                            for h in range(NH):
                                mm = pe.matmul(bb[:, h // 2, (h % 2) * NP:(h % 2 + 1) * NP], q[:, h, t * P:(t + 1) * P],
                                               k[:, h, 0:NP], start=True, stop=True)
                            mm.then_inc(sem.lg_mm, 1)
                            stream(2)
                            pe.wait_ge(sem.pr_ok, 2 * n + t + 1)
                            for s in range(2):
                                for h in range(NH):
                                    mm = pe.transpose(bb[:, 2 + s, h * P:(h + 1) * P],
                                                      prob(n)[:, h, s * P:(s + 1) * P], ident)
                            mm.then_inc(sem.pT_mm, 1)
                            stream(1)
                            pe.wait_ge(sem.pT_ok, 2 * n + t + 1)
                            for h in range(NH):
                                for s in range(2):
                                    mm = pe.matmul(bb[:, 0, h * P:(h + 1) * P], v[:, s, h * P:(h + 1) * P],
                                                   probT(n)[:, s, h, :], start=(s == 0), stop=(s == 1))
                            mm.then_inc(sem.ov_mm, 1)
                            stream(1)
                            pe.wait_ge(sem.y_e, 2 * n + t + 1)

                    def sample_attend(n, qslot):
                        to_rows(H(qslot), 0, (NP, T)).then_inc(sem.qr_mm, 1)
                        stream(1)
                        pe.wait_ge(sem.qr_ok, n + 1)
                        for b in range(NB):
                            if b >= 2:
                                pe.wait_ge(sem.kv_used, NB * n + b - 1)
                            pe.matmul(bb[:, b % 2, :], id8[:, b:b + 1].to_broadcast([NB, P]), qrow, start=True, stop=True)\
                                .then_inc(sem.qb_mm, 1)
                            if b % 4 == 3 or (n and b == 5):
                                stream(1)
                        pe.wait_ge(sem.lx_ok, n + 1)
                        if n:
                            pe.matmul(bb[0:32, 2, 0:KS + 1], tb("rep_heads")[0:NB, :], maskrow, start=True, stop=True,
                                      skip_group_check=True)
                        for t in range(2):
                            mm = pe.matmul(bb[0:32, 2, t * P:(t + 1) * P], ls[:, 32 * t:32 * t + 32], ident,
                                           start=(n == 0), stop=True, skip_group_check=True)
                        if n:
                            mm = pe.matmul(bb[0:32, 2, KS:KS + 1], kvprod, ones[:, 0:1], start=False, stop=True,
                                           skip_group_check=True)
                        mm.then_inc(sem.lt_mm, 1)
                        stream(1)
                        pe.wait_ge(sem.lp_ok, n + 1)
                        for t in range(2):
                            mm = pe.transpose(bb[:, 3, 32 * t:32 * t + 32], lrow[:, t * P:(t + 1) * P], ident[0:32, 0:32])
                        if n:
                            mm = pe.matmul(bb[:, 3, 64:96], lrow[:, KS:KS + 1].to_broadcast([32, P]), ident[0:32, 0:32],
                                           start=True, stop=True)
                        mm.then_inc(sem.lpt_mm, 1)
                        stream(1)
                        pe.wait_ge(sem.lpt_ok, n + 1)
                        for b in range(NB):
                            pe.wait_ge(kv_in[b % 2], kv_count(n, NB + b))
                            for h in range(NH):
                                j = b * NH + h
                                for t in range(2):
                                    mm = pe.matmul(bb[:, 0, j:j + 1], kvb[:, b % 2, t, h * P:(h + 1) * P],
                                                   pts[:, 32 * t + j:32 * t + j + 1], start=(t == 0), stop=(t == 1))
                            mm.then_inc(sem.sv_mm, 1)
                            if b == 3 or (n and b % 2):
                                stream(1)
                        pe.wait_ge(sem.sy_ok, n + 1)

                    for t in range(2):
                        to_rows(mkT, t, (t * P, (t + 1) * P)).then_inc(sem.rows_mm, 1)
                    stream(2)
                    attend(0, H(MQ), mkT, mvr)
                    pe.wait_ge(sem.stored, ready(MZ))
                    sample_attend(0, MQ)

                    stream(1)
                    pe.wait_ge(sem.small_e, 1)
                    for kind, src in enumerate((zT, abT)):
                        for t in range(2):
                            pe.transpose(bb[:, 0, (2 * kind + t) * 8:(2 * kind + t + 1) * 8],
                                         src[:, t * P:(t + 1) * P], id8)
                    mm = pe.matmul(bb[:, 1, 0:2 * IH * NB], ones[0:NB, :], gate_mask, start=True, stop=True)
                    mm.then_inc(sem.gt_mm, 1)
                    pe.wait_ge(sem.gt_ok, 1)

                    def rotate(n, slot, mat):
                        pe.wait_ge(sem.stored, ready(slot))
                        for c in range(CPS):
                            mm = pe.matmul(bb[:, c, 0:T], mat, H(slot)[:, c, :], start=True, stop=True)
                        mm.then_inc(sem.rot_mm, 1)
                        stream(1)

                    rotate(0, IQ, tb("rot64"))
                    pe.wait_ge(sem.rot_ok, 1)
                    pe.matmul(bb[:, 0, 0:T], tb("dup_lo")[0:ID, :], ikw[0:ID, :], start=True, stop=True)
                    pe.matmul(bb[:, 1, 0:T], tb("rot_dup")[0:ID, :], ikw[0:ID, :], start=True, stop=True)
                    for t in range(3):
                        m = P if t < 2 else NB
                        mm = pe.transpose(bb[0:m, 2, t * 72:(t + 1) * 72], ikw[0:72, t * P:t * P + m], ident[0:72, 0:72])
                    mm.then_inc(sem.ki_mm, 1)
                    stream(1)

                    for c in range(CPS):
                        for k, name in enumerate(("dup_lo", "dup_hi")):
                            j = 2 * c + k
                            pe.matmul(bb[:, 3, j * NB:(j + 1) * NB], tb(name), H(IQ)[:, c, NP:T], start=True, stop=True)
                    pe.wait_ge(sem.ki_ok, 1)
                    mm = pe.matmul(bb[:, 0, 0:P], lw, tb("blk_pages")[0:NB, :], start=True, stop=True)
                    mm.then_inc(sem.qd_mm, 1)
                    pe.wait_ge(sem.qd_ok, 1)
                    for j in range(IH):
                        mm = pe.matmul(bb[0:NB, 1, j * NB:(j + 1) * NB], qd[0:ID, j, :], KI[0:ID, NP:T], start=True, stop=True)
                    mm.then_inc(sem.new_mm, 1)
                    stream(1)
                    for j in range(8):
                        pe.wait_ge(gath[j % 2], 16 * (j // 2 + 1))
                        if j == 0:
                            pe.wait_ge(sem.new_ok, 1)
                        for u in range(8):
                            mm = pe.transpose(bb[:, u // 4, (u % 4) * P:(u % 4 + 1) * P], ik[:, j % 2, u * P:(u + 1) * P], ident)
                        mm.then_inc(sem.ik_T, 1)
                        stream(1)
                        pe.wait_ge(sem.ik_copied, j + 1)
                        for u in range(2):
                            mm = pe.matmul(bb[:, 2 + u, :], Qblk[:, :], ikT[:, u * 512:(u + 1) * 512], start=True, stop=True)
                        mm.then_inc(sem.ik_mm, 1)
                        pe.wait_ge(sem.ik_rel, j + 1)
                        for u in range(8):
                            mm = pe.matmul(bb[:, 0, 2 * u:2 * u + 2], ikr[:, u * P:(u + 1) * P], tb("parity"), start=True, stop=True)
                        mm.then_inc(sem.ik_sc, 1)
                        pe.wait_ge(sem.sc_ok, j + 1)

                    pe.matmul(bb[:, 0, 0:NH], tri_ones[:, 0:P], gbt[:, 0, 0, 0:NH], start=True, stop=True)
                    pe.matmul(bb[:, 0, NH:2 * NH], ones, gbt[:, 0, 0, 0:NH], start=True, stop=False)
                    pe.matmul(bb[:, 0, NH:2 * NH], tri_ones[:, 0:P], gbt[:, 0, 1, 0:NH], start=False, stop=True)
                    for h in range(NH):
                        b_, c0 = 1 + h // 2, (h % 2) * NP
                        pe.matmul(bb[:, b_, c0:c0 + NP], gbt[:, 0, 0, h:h + 1].to_broadcast([P, P]), tri_ones,
                                  start=True, stop=False)
                        mm = pe.matmul(bb[:, b_, c0 + P:c0 + NP], gbt[:, 0, 1, h:h + 1].to_broadcast([P, P]),
                                       tri_ones[:, 0:P], start=False, stop=True)
                    mm.then_inc(sem.gc_mm, 1)
                    stream(1)
                    pe.wait_ge(sem.dt_raw, 1)

                    def tail(i, s):
                        pe.wait_ge(sem.stored, ready(s))
                        if i:
                            pe.wait_ge(sem.tails_ok, i)
                        for c in range(CPS):
                            mm = pe.transpose(bb[0:11, 0, c * P:(c + 1) * P], H(s)[:, c, NP - 3:T], ident)
                        mm.then_inc(sem.tails, 1)

                    def ones_sum(n, src):
                        pe.wait_ge(sem.sq, n)
                        for c in range(CPS):
                            mm = pe.matmul(bb[:, c, 0:T], ones, src[:, c, :], start=True, stop=True)
                        mm.then_inc(sem.ss, 1)
                        stream(1 if n < 3 else 2)

                    for i, s in enumerate((GQ, GK, GV)):
                        tail(i, s)
                        stream(2)
                    pe.wait_ge(sem.tails_ok, 3)
                    stream(1)
                    ones_sum(1, tmpA)
                    pe.wait_ge(sem.normed, 1)
                    ones_sum(2, tmpA)
                    pe.wait_ge(sem.normed, 2)

                    def inner_scores(n, kk, qq):
                        for h in range(NH):
                            pe.matmul(bb[:, h // 2, (h % 2) * NP:(h % 2 + 1) * NP], kk[:, h, 0:P], qq[:, h, 0:NP],
                                      start=True, stop=True)
                            mm = pe.matmul(bb[:, 2, h * P:(h + 1) * P], kk[:, h, P:NP], qq[:, h, P:NP], start=True, stop=True)
                        mm.then_inc(sem.pt_mm, 1)
                        stream(1)

                    def out_and_state(n, pt0, pt1, v0, v1, kz):
                        for h in range(NH):
                            b_, c0, hs = h // 2, (h % 2) * NP, slice(h * P, (h + 1) * P)
                            pe.matmul(bb[:, b_, c0:c0 + NP], v0[:, hs], pt0[:, h, :], start=True, stop=False)
                            pe.matmul(bb[:, b_, c0 + P:c0 + NP], v1[:, hs], pt1[:, h, :], start=False, stop=True)
                        for h in range(NH):
                            hs = slice(h * P, (h + 1) * P)
                            pe.matmul(bb[:, 2, hs], kz[:, 0, hs], v0[:, hs], start=True, stop=False)
                            mm = pe.matmul(bb[:, 2, hs], kz[:, 1, hs], v1[:, hs], start=False, stop=True)
                        mm.then_inc(sem.o_mm, 1)
                        stream(1 + n)

                    gq, gk, gv = H(GQ), H(GK), H(GV)
                    for t in range(2):
                        to_rows(gv, t, (t * P, (t + 1) * P))
                        mm = to_rows(gk, 2 + t, (t * P, (t + 1) * P))
                    mm.then_inc(sem.tok_mm, 1)
                    stream(1)
                    pe.wait_ge(sem.tok_ok, 1)
                    for t in range(2):
                        for h in range(NH):
                            ks = gk[:, h, t * P:(t + 1) * P]
                            pe.matmul(bb[:, t, h * P:(h + 1) * P], ks, ks, start=True, stop=True)
                    for h in range(NH):
                        mm = pe.matmul(bb[:, 2, h * P:(h + 1) * P], gk[:, h, 0:P], gk[:, h, P:NP], start=True, stop=True)
                    mm.then_inc(sem.kk_mm, 1)
                    for t in range(2):
                        pe.wait_ge(sem.kk_ok, t + 1)
                        for h in range(NH):
                            mm = pe.transpose(bb[:, 3, h * P:(h + 1) * P], tri_t(t)[:, h, :], ident)
                        mm.then_inc(sem.inv_T, 1)
                        pe.wait_ge(sem.inv_at, t + 1)
                        for h in range(NH):
                            mm = pe.transpose(bb[:, 3, h * P:(h + 1) * P], amat[:, h, :], ident)
                        mm.then_inc(sem.at_mm, 1)
                        stream(1)
                        for lv in range(6):
                            n = 6 * t + lv
                            pe.wait_ge(sem.lvl_bt, n + 1)
                            for h in range(NH):
                                mm = pe.matmul(bb[:, 3, h * P:(h + 1) * P], bmat[:, h, :], xinv[:, h, :], start=True, stop=True)
                            mm.then_inc(sem.y_mm, 1)
                            pe.wait_ge(sem.y_ok, n + 1)
                            for h in range(NH):
                                pe.matmul(bb[:, 0, h * P:(h + 1) * P], ymat[:, h, :], xinvT[:, h, :], start=True, stop=True)
                                mm = pe.matmul(bb[:, 3, h * P:(h + 1) * P], xinvT[:, h, :], ymat[:, h, :], start=True, stop=True)
                            mm.then_inc(sem.z_mm, 1)
                            if lv not in (0, 2):
                                stream(1)
                        pe.wait_ge(sem.z_ok, 6 * (t + 1))
                        if t == 1:
                            for h in range(NH):
                                mm = pe.matmul(bb[:, 3, h * P:(h + 1) * P], btT[:, h, :], bv[:, 0, h * P:(h + 1) * P],
                                               start=True, stop=True)
                            mm.then_inc(sem.bt_mm, 1)
                            pe.wait_ge(sem.bt_ok, 1)
                        for h in range(NH):
                            mm = pe.matmul(bb[:, 3, h * P:(h + 1) * P], xinvT[:, h, :], bv[:, t, h * P:(h + 1) * P],
                                           start=True, stop=True)
                        mm.then_inc(sem.u_mm, 1)
                        stream(1)
                        pe.wait_ge(sem.u_ok, t + 1)
                    inner_scores(0, gk, gq)
                    pe.wait_ge(sem.pt_ok, 1)
                    out_and_state(0, dt0, dt1, bv[:, 0, :], bv[:, 1, :], kzA)

                    def samples_step(n, kslot, qslot, vslot):
                        pe.wait_ge(sem.kq_ok, n + 1)
                        pe.matmul(bb[:, 0, 0:NH * NB], ones, prod(n), start=True, stop=True)
                        mm = to_rows(H(kslot), 1, (NP, T))
                        mm.then_inc(sem.qk_mm, 1)
                        stream(1)
                        pe.wait_ge(sem.qk_ok, n + 1)
                        for h in range(NH):
                            m = NH * n + h
                            pe.wait_ge(stin[h % 2], 16 * (m // 2 + 1))
                            for b in range(NB):
                                mm = pe.matmul(bb[:, 0, 2 * b:2 * b + 2], sbuf(n)[:, h % 2, b, :], kq(n)[:, h, b, :],
                                               start=True, stop=True)
                            mm.then_inc(sem.sk_mm, 1)
                            stream(1)
                            pe.wait_ge(sem.vn_ok, m + 1)
                            pe.transpose(bb[0:NB, 1, 0:P], vnew(n)[:, h, :], ident).then_inc(sem.vt_mm, 1)
                            pe.wait_ge(sem.vm_ok, m + 1)
                            for j in range(2):
                                mm = pe.matmul(bb[:, 2 + j, :], ktok(n)[:, h * P:(h + 1) * P], vmask(n)[:, 512 * j:512 * (j + 1)],
                                               start=True, stop=True)
                            mm.then_inc(sem.op_mm, 1)
                            if h % 2 == 0:
                                stream(1)
                        pe.wait_ge(sem.s_new, NH * (n + 1))

                    pe.wait_ge(sem.st_ok, 1)
                    samples_step(0, GK, GQ, GV)
                    ones_sum(3, tmpA)
                    pe.wait_ge(sem.normed, 3)

                    for n, s in enumerate((RQ, RK)):
                        rotate(1 + n, s, tb("rot128"))
                        pe.wait_ge(sem.rot_ok, 2 + n)
                    for t in range(2):
                        to_rows(H(RV), t, (t * P, (t + 1) * P))
                        mm = to_rows(H(RK), 2 + t, (t * P, (t + 1) * P))
                    mm.then_inc(sem.tok_mm, 1)
                    stream(1)
                    pe.wait_ge(sem.tok_ok, 2)
                    inner_scores(1, H(RK), H(RQ))
                    pe.wait_ge(sem.pt_ok, 2)
                    out_and_state(1, rt0, rt1, rv[:, 0, :], rv[:, 1, :], kzC)
                    pe.wait_ge(sem.st_ok, 2)
                    samples_step(1, RK, RQ, RV)
                    for c in range(CPS):
                        mm = pe.matmul(bb[:, c, 0:T], ones, H(RQ)[:, c, :], start=True, stop=True)
                    mm.then_inc(sem.mean_mm, 1)
                    stream(1)
                    ones_sum(4, tmpA)
                    pe.wait_ge(sem.yc_ok, 1)

                    tail(3, LX)
                    stream(2)
                    pe.wait_ge(sem.tails_ok, 4)
                    pe.wait_ge(sem.conv_act, 4)
                    pe.wait_ge(sem.lw_in, 32)
                    for i in range(2):
                        if i:
                            pe.wait_ge(sem.lru_act, 1)
                        for h in range(NH):
                            mm = pe.matmul(bb[:, h, 0:T], lruw[:, i, h, :], H(LX)[:, h, :], start=True, stop=True)
                        mm.then_inc(sem.lru_mm, 1)
                        stream(1)
                    pe.wait_ge(sem.lru_act, 2)
                    stream(4)
                    pe.wait_ge(sem.lru_o, 1)
                    for h in range(NH):
                        mm = pe.transpose(bb[0:NB + 1, 0, h * P:(h + 1) * P], H(LX)[:, h, NP - 1:T], ident)
                    mm.then_inc(sem.h_mm, 1)
                    stream(1)

                    pe.wait_ge(sem.h_rows, 1)
                    for n, s in enumerate((DQ, DK)):
                        rotate(3 + n, s, tb("rot128"))
                        pe.wait_ge(sem.rot_ok, 4 + n)
                    for n, s in enumerate((DK, DV)):
                        pe.wait_ge(sem.stored, ready(s))
                        for t in range(3):
                            if 3 * n + t:
                                pe.wait_ge(sem.rows_copied, 2 + 3 * n + t)
                            to_rows(H(s), 0, (t * P, t * P + P) if t < 2 else (NP, T)).then_inc(sem.rows_mm, 1)
                            stream(1)
                    stream(1)
                    pe.wait_ge(sem.rows_copied, 8)
                    for t in range(3):
                        m = P if t < 2 else NB
                        mm = pe.transpose(bb[0:m, 0, t * ID:(t + 1) * ID], KI[0:ID, t * P:t * P + m], ident[0:ID, 0:ID])
                    mm.then_inc(sem.rows_mm, 1)
                    pe.wait_ge(sem.rows_copied, 9)
                    for t in range(2):
                        if t:
                            pe.wait_ge(sem.pidx_rel, 1)
                        for j in range(IH):
                            p0 = ID * (j % 2)
                            mm = pe.matmul(bb[:, 2 * (j % 2) + j // 4, (j // 2 % 2) * NP:(j // 2 % 2 + 1) * NP],
                                           H(IQ)[p0:p0 + ID, j // 2, t * P:(t + 1) * P], KI[p0:p0 + ID, 0:NP],
                                           start=True, stop=True)
                        mm.then_inc(sem.pidx_mm, 1)
                        stream(2)
                    pe.wait_ge(sem.pidx_rel, 2)
                    pe.wait_ge(sem.stored, ready(DZ))
                    attend(1, H(DQ), H(DK), vrow)

                    stream(3)
                    pe.wait_ge(sem.hl_ok, 1)
                    for k in range(2):
                        for t in range(2):
                            j = 2 * k + t
                            mm = pe.transpose(bb[:, 0, j * NB:(j + 1) * NB], hilo[:, k, t * P:(t + 1) * P], id8)
                    mm.then_inc(sem.hl_mm, 1)
                    stream(2)
                    pe.wait_ge(sem.rows_ok, 1)
                    sample_attend(1, DQ)
                    stream(None)
                    pe.wait_ge(sem.out_ok, KC)
                    for q in range(KC):
                        mm = pe.matmul(bb[:, 0, 0:T], ones, xnew[:, q, :], start=(q == 0), stop=(q == KC - 1))
                    mm.then_inc(sem.ln_sum, 1)
                    for q in range(4):
                        pe.wait_ge(sem.ln_sq, q + 1)
                        for c in range(4):
                            mm = pe.matmul(bb[:, 1, 0:T], ones, tmps[q % 2][:, c, :], start=(q + c == 0), stop=(q + c == 6))
                        mm.then_inc(sem.ln_ss, 1)

                @block.scalar
                def _(act):
                    ch = chain(act, sem.a_chain)
                    chunks = iter(range(len(CHUNKS)))
                    left = iter(SPLIT)
                    coming = [next(left)]

                    def split_to(i):
                        while coming[0] <= min(i, len(CHUNKS) - 1):
                            j = coming[0]
                            coming[0] = next(left, len(CHUNKS))
                            s = SPLIT_N[j]
                            n = COL_NARROW[CHUNKS[j][2]][1] if CHUNKS[j][0] == "narrow" else P
                            act.wait_ge(w_landed[j % NRING], landed(j))
                            if s >= 2:
                                act.wait_ge(sem.chunk_mm, products(SPLIT[s - 2]))
                            act.activation(hi(wsplit[:, s % 2, 0, :, 0:n]), ring[:, j % NRING, :, 0:n], ACT.Copy)\
                                .then_inc(sem.hi_ok, 1)

                    at_chunk = [0]

                    def ahead():
                        split_to(at_chunk[0] + 1)

                    def stream(n=1):
                        for i in islice(chunks, n):
                            (kind, x, m), g = CHUNKS[i], FIRST_RESULT[i]
                            if kind == "out" and m == 0:
                                act.wait_ge(sem.merged_ok, len(GATES_I))
                                for q in range(0, KC, 4):
                                    act.activation(hi(xsplit[:, 0, q:q + 4, :]), merged[:, q:q + 4, :], ACT.Copy).then_inc(sem.mh_ok, 1)
                            split_to(i + 1)
                            at_chunk[0] = i + 1
                            if kind == "out":
                                continue
                            act.wait_ge(sem.chunk_mm, g + 1)
                            src = mb[:, g % 4, :]
                            if kind == "gate":
                                if GATE_N[i]:
                                    act.wait_ge(sem.merged_ok, GATE_N[i])
                                act.activation(gbuf[:, :], src[:, 0:T], ACT.Sigmoid).then_inc(sem.gate_act, 1)
                            elif kind == "mem":
                                if m < CPS:
                                    dst, src = mkT[:, m, :], src[:, 0:NMEM]
                                else:
                                    dst = mvr[:, :, (m - CPS) * P:(m - CPS + 1) * P]
                                    src = src[:, 0:2 * P].rearrange("p (t n) -> p t n", t=2)
                                act.activation(dst, src, ACT.Copy).then_inc(sem.stored, 1)
                            elif kind == "narrow":
                                dst = ikw[0:72, :] if m else abT
                                act.activation(dst, src[0:COL_NARROW[m][1], 0:T], ACT.Copy).then_inc(sem.stored, 1)
                            else:
                                if (x, m) == (RZ, 0):
                                    act.wait_ge(sem.s_out, 16 * NH)
                                act.activation(H(x)[:, m, :], src[:, 0:T],
                                               ACT.Silu if x in (GZ, DZ, RZ, LZ, MZ) else ACT.Copy).then_inc(sem.stored, 1)

                    split_to(1)
                    act.dma_start(r1[0:4, :], at_l(a.conv_w)).then_inc(sem.params_in, 16)
                    for i, v in enumerate((a.conv_b, a.ln_g, a.ln_b)):
                        act.dma_start(r1[4 + i:5 + i, :], v[bass.ds(l, 1), :]).then_inc(sem.params_in, 16)
                    act.dma_start(r1[7:31, :], at_l(a.cache_conv).rearrange("b j n -> (b j) n")).then_inc(sem.params_in, 16)
                    for i, v in enumerate((a.lru_lambda, a.lru_b_r, a.lru_b_i)):
                        act.dma_start(r2[i:i + 1, :], v[bass.ds(l, 1), :]).then_inc(sem.params_in, 16)
                    act.dma_start(r2[3:11, :], at_l(a.state_lru)).then_inc(sem.params_in, 16)
                    act.dma_start(cols[0:NH, 0:1], a.gdn_dt_bias[bass.ds(l, 1), :].rearrange("z h -> h z")).then_inc(sem.params_in, 16)
                    act.dma_start(cols[0:NH, 1:2], a.gdn_a_log[bass.ds(l, 1), :].rearrange("z h -> h z")).then_inc(sem.params_in, 16)
                    act.dma_start(normw, a.gdn_norm_w[bass.ds(l, 1), :].rearrange("z d -> d z")).then_inc(sem.params_in, 16)
                    act.dma_start(tabs[:, :], a.levels).then_inc(sem.tab_in, 16)
                    act.dma_start(memrow, a.mem_prompt.rearrange("a (t p) n -> p (a t) n", p=P)).then_inc(sem.mem_in, 16)

                    stream(4)
                    stream(2)
                    stream(8)
                    stream(2)

                    def attend(n):
                        for t in range(2):
                            ahead()
                            act.wait_ge(sem.lg_ok, 2 * n + t + 1)
                            for h in range(NH):
                                mm = act.activation(prob(n)[:, h, :], prob(n)[:, h, :], ACT.Exp, bias=nmx[:, h:h + 1],
                                                    accum_out=rsm[:, h:h + 1])
                            mm.then_inc(sem.ex_ok, 1)
                            stream(2)
                            ahead()
                            act.wait_ge(sem.pT_mm, 2 * n + t + 1)
                            act.activation(probT(n).rearrange("p s h q -> p (s h q)"),
                                           bb[:, 2:4, :].rearrange("p s x -> p (s x)"), ACT.Copy).then_inc(sem.pT_ok, 1)
                            stream(2)

                    def sample_attend(n, w):
                        stream(1 + NB // 4 + n)
                        ahead()
                        act.wait_ge(sem.lt_ok, n + 1)
                        act.activation(lrow[:, 0:w], lrow[:, 0:w], ACT.Exp, bias=nmx[0:32, 0:1],
                                       accum_out=rsm[0:32, 0:1]).then_inc(sem.se_ok, 1)
                        stream(3 + 3 * n)

                    attend(0)
                    sample_attend(0, KS)
                    ahead()
                    act.wait_ge(sem.small_a, 1)
                    act.activation(spe, spn, ACT.Exp, scale=-1.0)
                    act.activation(sle, sln, ACT.Exp, scale=-1.0)
                    ch(act.activation(negA, cols[:, 1:2], ACT.Exp))
                    act.activation(spe, spe, ACT.Ln, bias=1.0)
                    act.activation(sle, sle, ACT.Ln, bias=1.0)
                    act.activation(abT, abT, ACT.Sigmoid).then_inc(sem.small_b, 1)
                    ahead()
                    act.wait_ge(sem.small_c, 1)
                    act.activation(egs[:, 0:8], zT[:, NP:T], ACT.Exp).then_inc(sem.small_d, 1)
                    stream(1)
                    stream(1)
                    stream(1)
                    stream(1)
                    for j in range(8):
                        ahead()
                        act.wait_ge(sem.ik_T, j + 1)
                        act.activation(ikT, bb[:, 0:2, :].rearrange("p s x -> p (s x)"), ACT.Copy).then_inc(sem.ik_copied, 1)
                        stream(1)

                    def conv_out(i, s):
                        act.wait_ge(sem.conv_done, i + 1)
                        act.activation(H(s), tmps[i % 2], ACT.Silu if s != LX else ACT.Copy).then_inc(sem.conv_act, 1)

                    def squares(n, src):
                        act.activation(tmpA, src, ACT.Square).then_inc(sem.sq, 1)

                    def roots(n, scale, eps):
                        ahead()
                        act.wait_ge(sem.ss, n)
                        mm = act.activation(tmpA, bb[:, :, 0:T], ACT.Sqrt, scale=scale, bias=eps)
                        mm.then_inc(sem.rs, 1)
                        stream(1 if n < 3 else 2)

                    ahead()
                    act.wait_ge(sem.dt_raw, 1)
                    act.activation(dt_all, dt_all, ACT.Exp)
                    act.activation(ktl.rearrange("p t h -> p (t h)"), ktl.rearrange("p t h -> p (t h)"), ACT.Exp)\
                        .then_inc(sem.dt_ok, 1)
                    stream(1)
                    eps = tb("eps")
                    for i, s in enumerate((GQ, GK, GV)):
                        stream(1)
                        ahead()
                        conv_out(i, s)
                        stream(1)
                    stream(1)
                    act.wait_ge(sem.conv_act, 3)
                    squares(1, H(GQ))
                    roots(1, float(HD), eps[:, 0:1])
                    act.wait_ge(sem.normed, 1)
                    squares(2, H(GK))
                    roots(2, 1.0, eps[:, 1:2])
                    stream(1)
                    for t in range(2):
                        stream(1)
                        for lv in range(6):
                            n = 6 * t + lv
                            act.wait_ge(sem.y_mm, n + 1)
                            act.activation(ymat.rearrange("p h x -> p (h x)"), bb[:, 3, :], ACT.Copy).then_inc(sem.y_ok, 1)
                            if lv not in (0, 2):
                                stream(1)
                        stream(1)
                    stream(1)
                    stream(1)
                    stream(1 + NH + NH // 2)
                    ahead()
                    act.wait_ge(sem.s_new, NH)
                    squares(3, H(GQ))
                    roots(3, 1.0 / HD, eps[:, 1:2])
                    stream(2 + 1 + 1 + 2 + 1 + NH + NH // 2)
                    ahead()
                    act.wait_ge(sem.mean_ok, 1)
                    squares(4, H(RQ))
                    stream(1)
                    roots(4, 1.0 / HD, eps[:, 2:3])
                    stream(1)
                    ahead()
                    conv_out(3, LX)
                    stream(1)
                    act.wait_ge(sem.s_out, 16 * 2 * NH)
                    for i in range(2):
                        ahead()
                        act.wait_ge(sem.lru_mm, i + 1)
                        for h in range(CPS):
                            mm = act.activation(lru(i)[:, h, :], bb[:, h, 0:T], ACT.Sigmoid, bias=qT[:, h, 1 + i:2 + i])
                        mm.then_inc(sem.lru_act, 1)
                        stream(1)
                    for h in range(CPS):
                        act.activation(lru(2)[:, h, :], lru(0)[:, h, :], ACT.Exp, scale=sn4[:, h:h + 1])
                        mm = act.activation(lru(3)[:, h, :], lru(0)[:, h, :], ACT.Tanh, scale=sp4[:, h:h + 1])
                    mm.then_inc(sem.lru_a, 1)
                    ahead()
                    stream(1)
                    ahead()
                    act.wait_ge(sem.lru_b, 1)
                    act.activation(lru(0), lru(0), ACT.Sqrt).then_inc(sem.lru_c, 1)
                    stream(3)
                    stream(1)
                    stream(2)
                    stream(7)
                    for t in range(2):
                        ahead()
                        act.wait_ge(sem.pidx_mm, t + 1)
                        if t:
                            act.wait_ge(sem.pidx_acc, 1)
                        act.activation(relus, bb[:, :, :].rearrange("p s x -> p (s x)"), ACT.Relu).then_inc(sem.pidx_rel, 1)
                        stream(2)
                    attend(1)

                    stream(3 + 2)
                    sample_attend(1, KS + 1)
                    stream(None)
                    for q in range(4):
                        act.wait_ge(sem.ln_cen, q + 1)
                        if q >= 2:
                            act.wait_ge(sem.ln_ss, q - 1)
                        act.activation(tmps[q % 2], xnew[:, 4 * q:4 * q + 4, :], ACT.Square).then_inc(sem.ln_sq, 1)
                    act.wait_ge(sem.ln_ss, 4)
                    act.activation(tmpA[:, 0, :], bb[:, 1, 0:T], ACT.Sqrt, scale=1.0 / D, bias=eps[:, 2:3]).then_inc(sem.ln_rs, 1)
                    for q in range(KC):
                        act.wait_ge(sem.ln_x, q + 1)
                        act.activation(hi(xsplit[:, 0, q, :]), xnew[:, q, :], ACT.Identity, bias=pT[:, q, 6:7]).then_inc(sem.xh_ok, 1)

                @block.vector
                def _(dve):
                    v = chain(dve, sem.v_chain)

                    def bc(ap, n):
                        return ap.unsqueeze(2).to_broadcast([ap.shape[0], ap.shape[1], n])

                    def bh(ap, n=NH):
                        return ap.unsqueeze(1).to_broadcast([ap.shape[0], n, ap.shape[1]])

                    chunks = iter(range(len(CHUNKS)))
                    left = iter(SPLIT)
                    coming = [next(left)]

                    def split_to(i):
                        while coming[0] <= min(i, len(CHUNKS) - 1):
                            j = coming[0]
                            coming[0] = next(left, len(CHUNKS))
                            s = SPLIT_N[j]
                            n = COL_NARROW[CHUNKS[j][2]][1] if CHUNKS[j][0] == "narrow" else P
                            dve.wait_ge(sem.hi_ok, s + 1)
                            dve.tensor_tensor(hi(wsplit[:, s % 2, 1, :, 0:n]), ring[:, j % NRING, :, 0:n],
                                              wsplit[:, s % 2, 0, :, 0:n], ALU.subtract).then_inc(sem.lo_ok, 1)

                    at_chunk = [0]

                    def ahead():
                        split_to(at_chunk[0] + 1)

                    def stream(n=1):
                        for i in islice(chunks, n):
                            (kind, x, m), g = CHUNKS[i], FIRST_RESULT[i]
                            if kind == "gate" and x == LAST and m < 4:
                                c = slice(4 * m, 4 * m + 4)
                                v(dve.tensor_tensor(xnew[:, c, :], xsplit[:, 0, c, :], xsplit[:, 1, c, :], ALU.add))
                            if kind == "out" and m == 0:
                                for q in range(0, KC, 4):
                                    dve.wait_ge(sem.mh_ok, q // 4 + 1)
                                    dve.tensor_tensor(hi(xsplit[:, 1, q:q + 4, :]), merged[:, q:q + 4, :], xsplit[:, 0, q:q + 4, :],
                                                      ALU.subtract).then_inc(sem.ms_ok, 1)
                            split_to(i + 1)
                            at_chunk[0] = i + 1
                            if kind == "gate":
                                proj = mb[:, (g + 1) % 4, 0:T]
                                dve.wait_ge(sem.gate_act, GATE_N[i] + 1)
                                dve.wait_ge(sem.chunk_mm, g + 2)
                                if x == 0:
                                    dve.tensor_tensor(merged[:, m, :], gbuf[:, :], proj, ALU.mult).then_inc(sem.merged_ok, 1)
                                else:
                                    v(dve.tensor_tensor(gbuf[:, :], gbuf[:, :], proj, ALU.mult))
                                    dve.tensor_tensor(merged[:, m, :], merged[:, m, :], gbuf[:, :], ALU.add).then_inc(sem.merged_ok, 1)
                            elif kind == "out":
                                dve.wait_ge(sem.chunk_mm, g + 1)
                                dve.scalar_tensor_tensor(xnew[:, m, :], xnew[:, m, :], ALPHA, mb[:, g % 4, 0:T], ALU.mult, ALU.add)\
                                    .then_inc(sem.out_ok, 1)

                    rounds = iter(range(KS // 8))

                    def topk(n=1):
                        for _ in range(n):
                            ahead()
                            r = next(rounds, None)
                            if r is None:
                                return
                            v(dve.max(m8[:, :], srow))
                            v(dve.max_index(i8[:, :], m8[:, :], srow))
                            v(dve.match_replace(srow, m8[:, :], srow, TAKEN))
                            v(dve.tensor_copy(picked[:, 8 * r:8 * r + 8], i8[:, :]))

                    split_to(0)
                    stream(4)
                    dve.wait_ge(sem.param_T, 1)
                    v(dve.tensor_copy(pT[:, :, :].rearrange("p c r -> p (c r)"), bb[:, 0, 0:KC * 31]))
                    dve.tensor_copy(qT[:, :, :].rearrange("p c r -> p (c r)"), bb[:, 1, 0:CPS * 11]).then_inc(sem.param_cols, 1)
                    dve.wait_ge(sem.param_cols, 1)
                    stream(1)
                    for t in range(2):
                        for q in range(4):
                            dve.wait_ge(sem.mem_T, 4 * t + q + 1)
                            dve.tensor_copy(memT[:, 4 * q:4 * q + 4, t * P:(t + 1) * P], heads4(bb[:, q, :])).then_inc(sem.memT_ok, 1)
                    stream(1 + 8)
                    v(dve.tensor_scalar(goff[:, 8:9], lcount, float(n_pool * 8), None, ALU.mult))
                    v(dve.scalar_tensor_tensor(goff[:, 8:9], ptf, 8.0, goff[:, 8:9], ALU.mult, ALU.add))
                    v(dve.tensor_scalar(goff[:, 0:8], tb("iota")[:, 0:8], goff[:, 8:9], None, ALU.add))
                    dve.tensor_copy(pagesU[:, :], goff[:, 0:8]).then_inc(sem.pages_ok, 1)
                    for t in range(2):
                        dve.wait_ge(sem.rows_mm, t + 1)
                        ahead()
                        if t:
                            dve.wait_ge(sem.rows_out, 16)
                        dve.tensor_copy(stg[:, :], bb[:, t, :]).then_inc(sem.rows_copied, 1)
                    stream(2)

                    def attend(n):
                        for t in range(2):
                            dve.wait_ge(sem.lg_mm, 2 * n + t + 1)
                            pr = prob(n)
                            if n == 0:
                                v(dve.tensor_scalar(pr, bb[:, 0:2, :].rearrange("p s (x k) -> p (s x) k", k=NP), SCALE, None, ALU.mult))
                            else:
                                for j in range(2):
                                    v(dve.scalar_tensor_tensor(pr[:, 2 * j:2 * j + 2, :], bb[:, j, :].rearrange("p (x k) -> p x k", k=NP),
                                                               SCALE, bh(pmask[:, t, :], 2), ALU.mult, ALU.add))
                            dve.tensor_reduce(nmx, pr, AX.X, ALU.max, negate=True).then_inc(sem.lg_ok, 1)
                            ahead()
                            dve.wait_ge(sem.ex_ok, 2 * n + t + 1)
                            v(dve.reciprocal(rsm, rsm))
                            dve.tensor_tensor(pr, pr, bc(rsm, NP), ALU.mult).then_inc(sem.pr_ok, 1)
                            stream(2)
                            if n:
                                topk()
                            stream(1)
                            dve.wait_ge(sem.ov_mm, 2 * n + t + 1)
                            c = slice(t * P, (t + 1) * P)
                            if n == 0:
                                dve.tensor_copy(H(MQ)[:, :, c], heads4(bb[:, 0, :])).then_inc(sem.y_e, 1)
                            else:
                                dve.tensor_tensor(H(DZ)[:, :, c], H(DZ)[:, :, c], heads4(bb[:, 0, :]), ALU.mult).then_inc(sem.y_e, 1)
                            stream(1)

                    def sample_attend(n):
                        w = KS + n
                        dve.wait_ge(sem.qr_mm, n + 1)
                        if n:
                            v(dve.tensor_tensor(kvprod.rearrange("p (b h) -> p h b", b=NB), H(DK)[:, :, NP:T], H(DQ)[:, :, NP:T], ALU.mult))
                        dve.tensor_copy(qrow, bb[0:NB, 0, :]).then_inc(sem.qr_ok, 1)
                        stream(1)
                        for b in range(NB):
                            dve.wait_ge(sem.qb_mm, NB * n + b + 1)
                            dve.wait_ge(kv_in[b % 2], kv_count(n, b))
                            for t in range(2):
                                mm = dve.tensor_tensor(prodK[:, t, :, :].rearrange("p h d -> p (h d)"), kvb[:, b % 2, t, :],
                                                       bb[:, b % 2, :], ALU.mult)
                            mm.then_inc(sem.kv_used, 1)
                            dve.wait_ge(sem.kv_used, NB * n + b + 1)
                            mm = dve.tensor_reduce(ls.rearrange("p (t b h) -> p t b h", t=2, b=NB)[:, :, b, :], prodK, AX.X, ALU.add)
                            if b < NB - 1:
                                v(mm)
                            else:
                                mm.then_inc(sem.lx_ok, 1)
                            if b % 4 == 3 or (n and b == 5):
                                stream(1)
                        dve.wait_ge(sem.lt_mm, n + 1)
                        v(dve.tensor_scalar(lrow[:, 0:w], bb[0:32, 2, 0:w], SCALE, None, ALU.mult))
                        dve.tensor_reduce(nmx[0:32, 0:1], lrow[:, 0:w], AX.X, ALU.max, negate=True).then_inc(sem.lt_ok, 1)
                        stream(1)
                        dve.wait_ge(sem.se_ok, n + 1)
                        v(dve.reciprocal(rsm[0:32, 0:1], rsm[0:32, 0:1]))
                        dve.tensor_scalar(lrow[:, 0:w], lrow[:, 0:w], rsm[0:32, 0:1], None, ALU.mult).then_inc(sem.lp_ok, 1)
                        dve.wait_ge(sem.lpt_mm, n + 1)
                        dve.tensor_copy(pts[:, 0:64 + 32 * n], bb[:, 3, 0:64 + 32 * n]).then_inc(sem.lpt_ok, 1)
                        dve.wait_ge(sem.lpt_ok, n + 1)
                        stream(2 + 3 * n)
                        dve.wait_ge(sem.sv_mm, NB * (n + 1))
                        ov = bb[:, 0, 0:32].rearrange("p (b h) -> p h b", b=NB)
                        if n == 0:
                            v(dve.tensor_tensor(H(MZ)[:, :, 0:NP], H(MZ)[:, :, 0:NP], H(MQ)[:, :, 0:NP], ALU.mult))
                            dve.tensor_tensor(H(MZ)[:, :, NP:T], H(MZ)[:, :, NP:T], ov, ALU.mult).then_inc(sem.sy_ok, 1)
                        else:
                            pn = pts[:, 64:96].rearrange("p (b h) -> p h b", b=NB)
                            v(dve.tensor_tensor(pn, pn, H(DV)[:, :, NP:T], ALU.mult))
                            v(dve.tensor_tensor(pn, pn, ov, ALU.add))
                            dve.tensor_tensor(H(DZ)[:, :, NP:T], H(DZ)[:, :, NP:T], pn, ALU.mult).then_inc(sem.sy_ok, 1)
                        dve.wait_ge(sem.sy_ok, n + 1)

                    attend(0)
                    dve.wait_ge(sem.stored, ready(MZ))
                    sample_attend(0)
                    dve.wait_ge(sem.stored, NARROW_READY)
                    lam = qT[:, :, 0]
                    v(dve.tensor_scalar(zT, abT, cols[:, 0:1], None, ALU.add))
                    v(dve.scalar_tensor_tensor(spn, zT, -1.0, zT, ALU.mult, ALU.max))
                    dve.scalar_tensor_tensor(sln, lam, -1.0, lam, ALU.mult, ALU.max).then_inc(sem.small_a, 1)
                    dve.wait_ge(sem.small_b, 1)
                    v(dve.scalar_tensor_tensor(zT, zT, 0.0, spn, ALU.max, ALU.add))
                    v(dve.tensor_scalar(negA, negA, -1.0, None, ALU.mult))
                    v(dve.tensor_scalar(zT, zT, negA, None, ALU.mult))
                    v(dve.tensor_scalar(sp4, lam, -1.0, 0.0, ALU.mult, ALU.max))
                    v(dve.tensor_tensor(sp4, sp4, sln, ALU.add))
                    v(dve.tensor_scalar(sn4, sp4, -LRU_C, None, ALU.mult))
                    dve.tensor_scalar(sp4, sp4, LRU_C, None, ALU.mult).then_inc(sem.small_c, 1)
                    dve.wait_ge(sem.small_d, 1)
                    v(dve.tensor_copy(egs[:, 8:16], abT[:, NP:T]))
                    for k in range(2):
                        mm = dve.tensor_tensor(gate_mask[:, 64 * k:64 * k + 64].rearrange("p (r b) -> p r b", r=IH),
                                               bh(egs[:, 8 * k:8 * k + 8], IH), bc(id8, NB), ALU.mult)
                        if k == 0:
                            v(mm)
                    mm.then_inc(sem.small_e, 1)
                    dve.wait_ge(sem.gt_mm, 1)
                    v(dve.tensor_copy(gbt.rearrange("p k t r -> p (k t r)"), bb[:, 0, 0:32]))
                    dve.tensor_copy(egb.rearrange("p k h b -> p (k h b)"), bb[:, 1, 0:128]).then_inc(sem.gt_ok, 1)
                    stream(1)
                    dve.wait_ge(sem.gt_ok, 1)

                    def rotate(n, slot, dim, scale=1.0):
                        dve.wait_ge(sem.rot_mm, n + 1)
                        v(dve.scalar_tensor_tensor(tmpA, bb[:, :, 0:T], scale, bh(tb(f"sin{dim}")), ALU.mult, ALU.mult))
                        v(dve.scalar_tensor_tensor(H(slot), H(slot), scale, bh(tb(f"cos{dim}")), ALU.mult, ALU.mult))
                        dve.tensor_tensor(H(slot), H(slot), tmpA, ALU.add).then_inc(sem.rot_ok, 1)
                        if n:
                            topk()
                        stream(1)
                        dve.wait_ge(sem.rot_ok, n + 1)

                    rotate(0, IQ, ID)
                    dve.wait_ge(sem.ki_mm, 1)
                    v(dve.tensor_tensor(KI[:, :], bb[:, 0, 0:T], tb("cos64"), ALU.mult))
                    v(dve.tensor_tensor(tmpA[:, 0, :], bb[:, 1, 0:T], tb("sin64"), ALU.mult))
                    v(dve.tensor_tensor(KI[:, :], KI[:, :], tmpA[:, 0, :], ALU.add))
                    for t in range(2):
                        v(dve.tensor_scalar(wtok[:, t, :], bb[:, 2, t * 72 + ID:(t + 1) * 72], WSCALE, None, ALU.mult))
                    v(dve.tensor_scalar(wts, bb[0:NB, 2, 2 * 72 + ID:3 * 72], WSCALE, None, ALU.mult))
                    for k in range(2):
                        mm = dve.tensor_tensor(lw[:, 64 * k:64 * k + 64].rearrange("p (b h) -> p b h", b=NB), bh(wts, NB),
                                               tb("blk_heads")[0:NB, :].rearrange("p (b h) -> p b h", b=NB), ALU.mult)
                        if k == 0:
                            v(mm)
                    mm.then_inc(sem.ki_ok, 1)
                    stream(1)
                    dve.wait_ge(sem.qd_mm, 1)
                    v(dve.tensor_copy(qd.rearrange("p h b -> p (h b)"), bb[:, 3, 0:64]))
                    for k in range(2):
                        half = slice(ID * k, ID * (k + 1))
                        v(dve.tensor_copy(Qblk[half, 64 * k:64 * k + 64].rearrange("p (b h) -> p h b", b=NB),
                                          bb[half, 3, 0:64].rearrange("p (h b) -> p h b", h=IH)))
                    dve.tensor_copy(mws, bb[:, 0, 0:P]).then_inc(sem.qd_ok, 1)
                    dve.wait_ge(sem.new_mm, 1)
                    dve.wait_ge(sem.memv_out, 16)
                    new = tmpA[0:NB, 1, 0:64].rearrange("p (h b) -> p h b", h=IH)
                    v(dve.scalar_tensor_tensor(new, bb[0:NB, 1, 0:64].rearrange("p (h b) -> p h b", h=IH), 0.0, bh(id8, IH), ALU.max, ALU.mult))
                    v(dve.tensor_reduce(n88, new, AX.X, ALU.add))
                    v(dve.tensor_tensor(n88, n88, wts, ALU.mult))
                    dve.tensor_reduce(srow[:, PAST:PAST + 1], n88, AX.X, ALU.add).then_inc(sem.new_ok, 1)
                    stream(1)
                    for j in range(8):
                        dve.wait_ge(sem.ik_mm, j + 1)
                        dve.scalar_tensor_tensor(ikr.rearrange("p (u x) -> p u x", u=8), bb[:, 2:4, :].rearrange("p s (u x) -> p (s u) x", x=P),
                                                 0.0, bh(mws, 8), ALU.max, ALU.mult).then_inc(sem.ik_rel, 1)
                        dve.wait_ge(sem.ik_sc, j + 1)
                        dve.tensor_copy(scs[:, 16 * j:16 * j + 16], bb[:, 0, 0:16]).then_inc(sem.sc_ok, 1)
                        stream(1)
                    dve.wait_ge(sem.gc_mm, 1)
                    v(dve.tensor_copy(gct.rearrange("p t h -> p (t h)"), bb[:, 0, 0:2 * NH]))
                    gcb = bb[:, 1:3, :].rearrange("p s (x n) -> p (s x) n", n=NP)
                    for h in range(NH):
                        dve.scalar_tensor_tensor(dt0[:, h, :], gcb[:, h, :], gct[:, 0, h:h + 1], nm, ALU.subtract, ALU.add)
                        dve.scalar_tensor_tensor(dt1[:, h, :], gcb[:, h, P:NP], gct[:, 1, h:h + 1], nm[:, 0:P], ALU.subtract, ALU.add)
                    v(dve.tensor_tensor(ktl[:, 0, :], gcb[:, :, NP - 1], gct[:, 0, :], ALU.subtract))
                    dve.tensor_tensor(ktl[:, 1, :], gcb[:, :, NP - 1], gct[:, 1, :], ALU.subtract).then_inc(sem.dt_raw, 1)
                    stream(1)

                    def conv(i, s):
                        dve.wait_ge(sem.stored, ready(s))
                        dve.wait_ge(sem.tails, i + 1)
                        if i == 0:
                            dve.wait_ge(sem.rows_out, 32)
                        elif i < 3:
                            dve.wait_ge(sem.tail_out, 32 * i)
                        else:
                            dve.wait_ge(sem.st_out, 32)
                        dve.tensor_copy(stg[0:11, :], bb[0:11, 0, :]).then_inc(sem.tails_ok, 1)
                        if i >= 2:
                            dve.wait_ge(sem.conv_act, i - 1)
                        out = tmps[i % 2]
                        ahead()
                        for k in range(4):
                            if k == 2:
                                stream(1)
                                ahead()
                            for c in range(CPS):
                                q = CPS * s + c
                                x, y = H(s)[:, c, :], out[:, c, :]
                                wk = pT[:, q, 3 - k:4 - k]
                                if k == 0:
                                    mm = dve.tensor_scalar(y, x, wk, pT[:, q, 4:5], ALU.mult, ALU.add)
                                else:
                                    dve.scalar_tensor_tensor(y[:, k:NP], x[:, 0:NP - k], wk, y[:, k:NP], ALU.mult, ALU.add)
                                    mm = dve.scalar_tensor_tensor(y[:, NP:T], pT[:, q, 7 + 3 - k:31:3], wk, y[:, NP:T], ALU.mult, ALU.add)
                            if k < 3:
                                v(mm)
                        mm.then_inc(sem.conv_done, 1)

                    def normed(n, s):
                        dve.wait_ge(sem.rs, n)
                        if n == 4:
                            ahead()
                        v(dve.reciprocal(tmpA, tmpA))
                        dve.tensor_tensor(H(s), H(s), tmpA, ALU.mult).then_inc(sem.normed, 1)
                        stream(1 if n < 3 else 2)
                        dve.wait_ge(sem.normed, n)

                    for i, s in enumerate((GQ, GK, GV)):
                        conv(i, s)
                        stream(1)
                    stream(1)
                    normed(1, GQ)
                    normed(2, GK)

                    dve.wait_ge(sem.tok_mm, 1)
                    dve.wait_ge(sem.dt_ok, 1)
                    for t in range(2):
                        v(dve.tensor_tensor(heads4(bv[:, t, :]), heads4(bb[:, t, :]), bc(gbt[:, 1, t, NH:2 * NH], P), ALU.mult))
                        mm = dve.tensor_tensor(heads4(kzA[:, t, :]), heads4(bb[:, 2 + t, :]), bc(ktl[:, t, :], P), ALU.mult)
                        if t == 0:
                            v(mm)
                    mm.then_inc(sem.tok_ok, 1)
                    stream(1)
                    dve.wait_ge(sem.kk_mm, 1)
                    dve.wait_ge(sem.tail_out, 96)
                    strict = bh(tb("strict_t"))
                    v(dve.tensor_tensor(btT, heads4(bb[:, 2, :]), dt0[:, :, P:NP], ALU.mult))
                    for t in range(2):
                        v(dve.tensor_tensor(tri_t(t), heads4(bb[:, t, :]), (dt0[:, :, 0:P], dt1)[t], ALU.mult))
                        dve.tensor_tensor(tri_t(t), tri_t(t), strict, ALU.mult).then_inc(sem.kk_ok, 1)
                    dve.wait_ge(sem.row_in, 16)
                    dve.wait_ge(sem.tab_in, 16)

                    def mask(i):
                        return bh(tabs[:, i * P:(i + 1) * P])

                    for t in range(2):
                        beta = bc(gbt[:, 1, t, NH:2 * NH], P)
                        dve.wait_ge(sem.inv_T, t + 1)
                        dve.tensor_tensor(amat, heads4(bb[:, 3, :]), beta, ALU.mult).then_inc(sem.inv_at, 1)
                        dve.wait_ge(sem.inv_at, t + 1)
                        v(dve.tensor_tensor(xinv, amat, mask(0), ALU.mult))
                        v(dve.tensor_tensor(xinv, bh(ident), xinv, ALU.subtract))
                        dve.wait_ge(sem.at_mm, t + 1)
                        v(dve.tensor_copy(atm, heads4(bb[:, 3, :])))
                        v(dve.tensor_tensor(xinvT, atm, mask(1), ALU.mult))
                        v(dve.tensor_tensor(xinvT, bh(ident), xinvT, ALU.subtract))
                        for lv in range(6):
                            n = 6 * t + lv
                            dve.tensor_tensor(bmat, atm, mask(2 + lv), ALU.mult).then_inc(sem.lvl_bt, 1)
                            if lv in (2, 4, 5):
                                topk()
                            if lv not in (1, 3):
                                stream(1)
                            dve.wait_ge(sem.z_mm, n + 1)
                            if lv < 5:
                                v(dve.tensor_tensor(xinv, xinv, heads4(bb[:, 3, :]), ALU.subtract))
                            dve.tensor_tensor(xinvT, xinvT, heads4(bb[:, 0, :]), ALU.subtract).then_inc(sem.z_ok, 1)
                            dve.wait_ge(sem.z_ok, n + 1)
                            if lv == 5:
                                stream(1)
                        if t == 1:
                            dve.wait_ge(sem.bt_mm, 1)
                            v(dve.tensor_tensor(bmat, heads4(bb[:, 3, :]), beta, ALU.mult))
                            dve.tensor_tensor(heads4(bv[:, 1, :]), heads4(bv[:, 1, :]), bmat, ALU.subtract).then_inc(sem.bt_ok, 1)
                        dve.wait_ge(sem.u_mm, t + 1)
                        dve.tensor_copy(bv[:, t, :], bb[:, 3, :]).then_inc(sem.u_ok, 1)
                        stream(1)
                    dve.wait_ge(sem.pt_mm, 1)
                    two = bb[:, 0:2, :].rearrange("p s (x n) -> p (s x) n", n=NP)
                    v(dve.tensor_tensor(dt0, dt0, two, ALU.mult))
                    dve.tensor_tensor(dt1, dt1, heads4(bb[:, 2, :]), ALU.mult).then_inc(sem.pt_ok, 1)
                    stream(1)
                    dve.wait_ge(sem.o_mm, 1)
                    v(dve.tensor_copy(H(GQ)[:, :, 0:NP], two))
                    dve.tensor_copy(stg[:, :], bb[:, 2, :]).then_inc(sem.st_ok, 1)

                    def samples_step(n, kslot, qslot, vslot):
                        ks, qs, vs = (H(s)[:, :, NP:T] for s in (kslot, qslot, vslot))
                        v(dve.tensor_copy(kq(n)[:, :, :, 0], ks))
                        v(dve.tensor_copy(kq(n)[:, :, :, 1], qs))
                        dve.tensor_tensor(prod(n).rearrange("p (h b) -> p h b", h=NH), ks, qs, ALU.mult).then_inc(sem.kq_ok, 1)
                        topk()
                        stream(1 + n)
                        dve.wait_ge(sem.qk_mm, n + 1)
                        v(dve.tensor_copy(qkb.rearrange("p h b -> p (h b)"), bb[:, 0, 0:NH * NB]))
                        dve.tensor_copy(ktok(n), bb[0:NB, 1, :]).then_inc(sem.qk_ok, 1)
                        topk()
                        stream(1)
                        gam = egb[:, 0, 0:NH, :] if n == 0 else tb("gamma").rearrange("p (h b) -> p h b", h=NH)
                        for h in range(NH):
                            m = NH * n + h
                            eg = gam[:, h, :]
                            dve.wait_ge(sem.sk_mm, m + 1)
                            sk = bb[:, 0, 0:2 * NB].rearrange("p (b k) -> p b k", k=2)
                            if n == 0:
                                v(dve.tensor_tensor(s8[0], sk[:, :, 0], eg, ALU.mult))
                                v(dve.tensor_tensor(s8[0], vs[:, h, :], s8[0], ALU.subtract))
                                dve.tensor_tensor(vnew(n)[:, h, :], s8[0], egb[:, 1, NH + h, :], ALU.mult).then_inc(sem.vn_ok, 1)
                            else:
                                dve.tensor_copy(vnew(n)[:, h, :], vs[:, h, :]).then_inc(sem.vn_ok, 1)
                            dve.wait_ge(sem.vn_ok, m + 1)
                            v(dve.tensor_tensor(s8[0], sk[:, :, 1], eg, ALU.mult))
                            v(dve.tensor_tensor(s8[1], qkb[:, h, :], vnew(n)[:, h, :], ALU.mult))
                            v(dve.tensor_tensor(qs[:, h, :], s8[0], s8[1], ALU.add))
                            S = sbuf(n)[:, h % 2, :, :]
                            dve.wait_ge(stin[h % 2], 16 * (m // 2 + 1))
                            v(dve.tensor_tensor(S, S, bc(eg, HD), ALU.mult))
                            stream(1)
                            dve.wait_ge(sem.vt_mm, m + 1)
                            dve.tensor_tensor(vmask(n).rearrange("p (b e) -> p b e", b=NB), bh(bb[0:NB, 1, 0:P], NB), bc(id8, P), ALU.mult)\
                                .then_inc(sem.vm_ok, 1)
                            dve.wait_ge(sem.op_mm, m + 1)
                            dve.tensor_tensor(S, S, bb[:, 2:4, :].rearrange("p s (b e) -> p (s b) e", e=HD), ALU.add).then_inc(sem.s_new, 1)
                            topk()
                            if h % 2 == 0:
                                stream(1)

                    samples_step(0, GK, GQ, GV)
                    dve.wait_ge(sem.rs, 3)
                    ahead()
                    v(dve.reciprocal(tmpA, tmpA))
                    v(dve.scalar_tensor_tensor(H(GQ), H(GQ), normw, tmpA, ALU.mult, ALU.mult))
                    dve.wait_ge(sem.stored, ready(GZ))
                    dve.tensor_tensor(H(GZ), H(GZ), H(GQ), ALU.mult).then_inc(sem.normed, 1)
                    topk()
                    stream(2)
                    dve.wait_ge(sem.normed, 3)

                    rotate(1, RQ, HD)
                    rotate(2, RK, HD, SCALE)
                    dve.wait_ge(sem.tok_mm, 2)
                    for t in range(2):
                        v(dve.tensor_copy(rv[:, t, :], bb[:, t, :]))
                        mm = dve.tensor_tensor(heads4(kzC[:, t, :]), heads4(bb[:, 2 + t, :]), bc(tb("zeta")[:, NH * t:NH * t + NH], P), ALU.mult)
                        if t == 0:
                            v(mm)
                    mm.then_inc(sem.tok_ok, 1)
                    topk()
                    stream(1)
                    dve.wait_ge(sem.pt_mm, 2)
                    dve.wait_ge(sem.decays_in, 16)
                    rdm = heads4(tabs[:, :])
                    v(dve.tensor_tensor(rt0, two, rdm, ALU.mult))
                    dve.tensor_tensor(rt1, heads4(bb[:, 2, :]), rdm[:, :, 0:P], ALU.mult).then_inc(sem.pt_ok, 1)
                    topk()
                    stream(1)
                    dve.wait_ge(sem.o_mm, 2)
                    v(dve.tensor_copy(H(RQ)[:, :, 0:NP], two))
                    ahead()
                    dve.wait_ge(sem.st_out, 16)
                    dve.tensor_copy(stg[:, :], bb[:, 2, :]).then_inc(sem.st_ok, 1)
                    samples_step(1, RK, RQ, RV)
                    dve.wait_ge(sem.mean_mm, 1)
                    dve.scalar_tensor_tensor(H(RQ), bb[:, :, 0:T], -1.0 / HD, H(RQ), ALU.mult, ALU.add).then_inc(sem.mean_ok, 1)
                    stream(1)
                    normed(4, RQ)
                    dve.wait_ge(sem.stored, ready(RZ))
                    dve.tensor_tensor(H(RZ), H(RZ), H(RQ), ALU.mult).then_inc(sem.yc_ok, 1)

                    conv(3, LX)
                    stream(1 + 2)
                    dve.wait_ge(sem.lru_act, 2)
                    v(dve.tensor_tensor(lru(1), lru(1), H(LX), ALU.mult))
                    ahead()
                    dve.wait_ge(sem.lru_a, 1)
                    ahead()
                    v(dve.tensor_scalar(lru(0), lru(3), 1.0, None, ALU.add))
                    v(dve.reciprocal(lru(0), lru(0)))
                    stream(1)
                    ahead()
                    dve.scalar_tensor_tensor(lru(0), lru(3), 2.0, lru(0), ALU.mult, ALU.mult).then_inc(sem.lru_b, 1)
                    dve.wait_ge(sem.lru_c, 1)
                    v(dve.tensor_tensor(lru(1), lru(1), lru(0), ALU.mult))
                    stream(1)
                    for c in range(CPS):
                        mm = dve.tensor_tensor_scan(H(LX)[:, c, 0:NP], lru(2)[:, c, 0:NP], lru(1)[:, c, 0:NP], 0.0, ALU.mult, ALU.add)
                    v(mm)
                    ahead()
                    v(dve.tensor_tensor(H(LX)[:, :, NP:T], lru(2)[:, :, NP:T], qT[:, :, 3:11], ALU.mult))
                    dve.tensor_tensor(H(LX)[:, :, NP:T], H(LX)[:, :, NP:T], lru(1)[:, :, NP:T], ALU.add).then_inc(sem.lru_o, 1)
                    topk(2)
                    stream(2)
                    dve.wait_ge(sem.lru_o, 1)
                    dve.wait_ge(sem.stored, ready(LZ))
                    v(dve.tensor_tensor(H(LZ), H(LZ), H(LX), ALU.mult))
                    dve.wait_ge(sem.h_mm, 1)
                    dve.wait_ge(sem.tail_out, 128)
                    dve.tensor_copy(stg[0:NB + 1, :], bb[0:NB + 1, 0, :]).then_inc(sem.h_rows, 1)
                    topk()
                    stream(1)

                    rotate(3, DQ, HD)
                    rotate(4, DK, HD)
                    dve.wait_ge(sem.lru_out, 32)
                    for j in range(7):
                        dve.wait_ge(sem.rows_mm, 3 + j)
                        ahead()
                        if j and j not in (4,):
                            dve.wait_ge(sem.rows_out, 32 + 16 * j)
                        m = NB if j in (2, 5) else P
                        if j < 6:
                            dst = vrow[:, j - 3, :] if j in (3, 4) else stg[0:m, :]
                            dve.tensor_copy(dst, bb[0:m, 0, :]).then_inc(sem.rows_copied, 1)
                            stream(1)
                            if j % 3 == 1:
                                topk()
                            if j == 5:
                                stream(1)
                        else:
                            v(dve.tensor_copy(stg[:, 0:2 * ID], bb[:, 0, 0:2 * ID]))
                            dve.tensor_copy(stg[0:NB, 2 * ID:3 * ID], bb[0:NB, 0, 2 * ID:3 * ID]).then_inc(sem.rows_copied, 1)
                    for t in range(2):
                        dve.wait_ge(sem.pidx_rel, t + 1)
                        v(dve.scalar_tensor_tensor(pscore, relus[:, 0:NP], wtok[:, t, 0:1], cm[t], ALU.mult, ALU.add))
                        for j in range(1, IH):
                            mm = dve.scalar_tensor_tensor(pscore, relus[:, (4 * (j % 2) + j // 2) * NP:][:, 0:NP], wtok[:, t, j:j + 1], pscore, ALU.mult, ALU.add)
                            if j < IH - 1:
                                v(mm)
                        mm.then_inc(sem.pidx_acc, 1)
                        dve.wait_ge(sem.pidx_acc, t + 1)
                        ahead()
                        for r in range(KP // 8):
                            if r == 4:
                                stream(1)
                                ahead()
                            v(dve.max(pm8[:, :], pscore))
                            v(dve.match_replace(pscore, pm8[:, :], pscore, TAKEN))
                        v(dve.tensor_scalar(pmask[:, t, :], pscore, TAKEN, None, ALU.is_equal))
                        v(dve.tensor_scalar(pmask[:, t, :], pmask[:, t, :], -1.0, BIG, ALU.add, ALU.mult))
                        v(dve.tensor_tensor(pmask[:, t, :], pmask[:, t, :], cm[t], ALU.add))
                        stream(1)
                    attend(1)
                    stream(2)
                    topk(KS // 8)
                    stream(1)

                    v(dve.tensor_scalar(hiloU[:, 0, :], picked, 7, None, ALU.logical_shift_right))
                    v(dve.tensor_scalar(hiloU[:, 1, :], picked, PAGE - 1, None, ALU.bitwise_and))
                    v(dve.tensor_copy(hilo, hiloU))
                    v(dve.tensor_scalar(maskrow[:, 0:KS], hilo[:, 0, :], float(NPG), -BIG, ALU.is_equal, ALU.mult))
                    v(dve.tensor_reduce(nsel, maskrow[:, 0:KS], AX.X, ALU.min))
                    dve.tensor_scalar(maskrow[:, KS:KS + 1], nsel, -1.0, -BIG, ALU.mult, ALU.add).then_inc(sem.hl_ok, 1)

                    dve.wait_ge(sem.hl_mm, 1)
                    hl = bb[:, 0, 0:32].rearrange("p (k t b) -> p k t b", k=2, t=2)
                    v(dve.tensor_scalar(goff[:, 8:9], lcount, float(n_pool * PAGE), None, ALU.mult))
                    for t in range(2):
                        v(dve.tensor_tensor(eqs, bh(tb("iota"), NB), bc(hl[:, 0, t, :], NPG), ALU.is_equal))
                        v(dve.tensor_tensor(eqs, eqs, ptB[:, :].rearrange("p (b g) -> p b g", b=NB), ALU.mult))
                        v(dve.tensor_reduce(rowf[:, NB * t:NB * t + NB], eqs, AX.X, ALU.add))
                    v(dve.scalar_tensor_tensor(rowf, rowf, float(PAGE), bb[:, 0, 16:32], ALU.mult, ALU.add))
                    v(dve.tensor_scalar(rowf, rowf, goff[:, 8:9], None, ALU.add))
                    dve.tensor_copy(rowsU[:, :, :].rearrange("p t b -> p (t b)"), rowf).then_inc(sem.rows_ok, 1)
                    stream(2)
                    sample_attend(1)
                    stream(None)

                    dve.wait_ge(sem.ln_sum, 1)
                    for q in range(4):
                        x4 = xnew[:, 4 * q:4 * q + 4, :]
                        dve.scalar_tensor_tensor(x4, bh(bb[:, 0, 0:T]), -1.0 / D, x4, ALU.mult, ALU.add).then_inc(sem.ln_cen, 1)
                    dve.wait_ge(sem.ln_rs, 1)
                    dve.wait_ge(sem.ln_cen, 4)
                    v(dve.reciprocal(tmpA[:, 0, :], tmpA[:, 0, :]))
                    for q in range(KC):
                        dve.scalar_tensor_tensor(xnew[:, q, :], xnew[:, q, :], pT[:, q, 5:6], tmpA[:, 0, :], ALU.mult, ALU.mult)\
                            .then_inc(sem.ln_x, 1)
                    for q in range(KC):
                        dve.wait_ge(sem.xh_ok, q + 1)
                        dve.scalar_tensor_tensor(hi(xsplit[:, 1, q, :]), xnew[:, q, :], pT[:, q, 6:7], xsplit[:, 0, q, :],
                                                 ALU.add, ALU.subtract).then_inc(sem.x_ok, 1)
                    dve.tensor_scalar(lcount, lcount, 1.0, None, ALU.add).then_inc(sem.lc_ok, 1)

                @block.gpsimd
                def _(pool):
                    def flat(ap):
                        return at_l(ap).rearrange("b t h d -> (b t) (h d)")

                    outs = []

                    def put(dst, src, s):
                        pool.dma_start(dst, src).then_inc(s, 16)

                    def kv_loads(n, k_src, v_src):
                        for kind, src in enumerate((k_src, v_src)):
                            for b in range(NB):
                                if kind == 0 and b < 2:
                                    if n:
                                        pool.wait_ge(sem.y_e, 4)
                                    else:
                                        pool.wait_ge(sem.memT_ok, 8)
                                elif kind == 0:
                                    pool.wait_ge(sem.kv_used, NB * n + b - 1)
                                elif b < 2:
                                    pool.wait_ge(sem.kv_used, NB * n + NB - 1 + b)
                                else:
                                    pool.wait_ge(sem.sv_mm, NB * n + b - 1)
                                if n == 0:
                                    pool.dma_start(kvb[:, b % 2, :, :], src[b].rearrange("(t p) h d -> p t (h d)", p=P))\
                                        .then_inc(kv_in[b % 2], 16)
                                else:
                                    for t in range(2):
                                        pool.indirect_dma_start(kvb[:, b % 2, t, :], None, src,
                                                                bass.IndirectOffsetOnAxis(ap=rowsU[:, t, b:b + 1], axis=0))\
                                            .then_inc(kv_in[b % 2], 16)

                    for t in range(2):
                        pool.wait_ge(sem.rows_copied, t + 1)
                        put(flat(o.p_mem_k)[t * P:(t + 1) * P, :], stg[:, :], sem.rows_out)
                    pool.wait_ge(sem.stored, MEMKV_READY)
                    put(flat(o.p_mem_v).rearrange("(t p) n -> p t n", p=P), mvr, sem.memv_out)
                    kv_loads(0, at_l(a.cache_mem_k), at_l(a.cache_mem_v))
                    pool.wait_ge(sem.y_e, 2)
                    pool.wait_ge(sem.pages_ok, 1)
                    ikp = a.cache_dsa_idx_k.rearrange("l g (j t) d -> (l g j) (t d)", j=8)
                    for j in range(8):
                        if j >= 2:
                            pool.wait_ge(sem.ik_T, j - 1)
                        pool.indirect_dma_start(ik[:, j % 2, :], None, ikp, bass.IndirectOffsetOnAxis(ap=pagesU[:, j:j + 1], axis=0))\
                            .then_inc(gath[j % 2], 16)
                    pool.wait_ge(sem.sc_ok, 8)
                    pool.dma_start(srow[:, 0:PAST], scs).then_inc(sem.row_in, 16)

                    def tail(i, s):
                        pool.wait_ge(sem.tails_ok, i + 1)
                        c = slice(s * W, (s + 1) * W)
                        put(at_l(o.p_conv).rearrange("b j n -> (b j) n")[:, c], stg[0:3, :], sem.tail_out)
                        put(at_l(o.s_conv)[:, 2, c], stg[3:11, :], sem.tail_out)

                    for i, s in enumerate((GQ, GK, GV)):
                        tail(i, s)
                    put(at_l(o.s_conv)[:, 0:2, :], at_l(a.cache_conv)[:, 1:3, :], sem.cp_out)
                    pool.wait_ge(sem.z_ok, 12)
                    pool.dma_start(tabs[:, :], a.decays).then_inc(sem.decays_in, 16)

                    def states(n, src, pdst, dst):
                        pool.wait_ge(sem.st_ok, n + 1)
                        put(at_l(pdst).rearrange("b h d e -> d (b h) e"), heads4(stg[:, :]), sem.st_out)
                        s_in, s_to = (at_l(x).rearrange("b h d e -> d h b e") for x in (src, dst))
                        for h in range(2):
                            pool.dma_start(sbuf(n)[:, h, :, :], s_in[:, h, :, :]).then_inc(stin[h], 16)
                        for h in range(NH):
                            m = NH * n + h
                            pool.wait_ge(sem.s_new, m + 1)
                            put(s_to[:, h, :, :], sbuf(n)[:, h % 2, :, :], sem.s_out)
                            if h + 2 < NH:
                                pool.wait_ge(sem.s_out, 16 * (m + 1))
                                pool.dma_start(sbuf(n)[:, h % 2, :, :], s_in[:, h + 2, :, :]).then_inc(stin[h % 2], 16)

                    states(0, a.state_gdn, o.p_gdn, o.s_gdn)
                    pool.wait_ge(sem.pt_ok, 2)
                    for i, w in enumerate((a.lru_w_r, a.lru_w_i)):
                        pool.dma_start(lruw[:, i, :, :], at_l(w).rearrange("h i j -> i h j")).then_inc(sem.lw_in, 16)
                    states(1, a.state_ret, o.p_ret, o.s_ret)
                    tail(3, LX)
                    pool.wait_ge(sem.h_rows, 1)
                    put(o.p_lru[bass.ds(l, 1)].rearrange("z b n -> (z b) n"), stg[0:1, :], sem.lru_out)
                    put(at_l(o.s_lru), stg[1:NB + 1, :], sem.lru_out)
                    for j in range(6):
                        pool.wait_ge(sem.rows_copied, 3 + j)
                        pd, sd = (o.p_dsa_k, o.s_dsa_k) if j < 3 else (o.p_dsa_v, o.s_dsa_v)
                        t = j % 3
                        if t < 2:
                            put(flat(pd)[t * P:(t + 1) * P, :], stg[:, :] if j < 3 else vrow[:, t, :], sem.rows_out)
                        else:
                            put(flat(sd), stg[0:NB, :], sem.rows_out)
                    pool.wait_ge(sem.rows_copied, 9)
                    for t in range(2):
                        put(at_l(o.p_dsa_ik).rearrange("b t d -> (b t) d")[t * P:(t + 1) * P, :], stg[:, t * ID:(t + 1) * ID], sem.rows_out)
                    put(at_l(o.s_dsa_ik).rearrange("b t d -> (b t) d"), stg[0:NB, 2 * ID:3 * ID], sem.rows_out)

                    pool.wait_ge(sem.rows_ok, 1)
                    kv_loads(1, a.cache_dsa_k.rearrange("l g t h d -> (l g t) (h d)"), a.cache_dsa_v.rearrange("l g t h d -> (l g t) (h d)"))
                    for s, n in ((sem.rows_out, 32 + 16 * 9), (sem.memv_out, 16), (sem.tail_out, 128), (sem.cp_out, 16),
                                 (sem.st_out, 32), (sem.s_out, 128), (sem.lru_out, 32)):
                        pool.wait_ge(s, n)
                    for s, n in ((gath[0], 64), (gath[1], 64), (sem.row_in, 16), (sem.lw_in, 32), (sem.decays_in, 16),
                                 (stin[0], 64), (stin[1], 64), (kv_in[0], kv_count(1, 14)), (kv_in[1], kv_count(1, 15))):
                        pool.wait_ge(s, n)
            clear_sems()

        with nc.Block() as block:
            @block.tensor
            def _(pe):
                n = 0
                pe.wait_ge(sem.x_in, 1)
                for t in range(3):
                    m = P if t < 2 else NB
                    for q in range(4):
                        if n >= 4:
                            pe.wait_ge(sem.x_ok, n - 3)
                        for c in range(4):
                            mm = pe.transpose(mb[0:m, n % 4, c * P:(c + 1) * P], xnew[:, 4 * q + c, t * P:t * P + m], ident)
                        mm.then_inc(sem.x_T, 1)
                        n += 1

            @block.vector
            def _(dve):
                dve.tensor_tensor(xnew, xsplit[:, 0, :, :], xsplit[:, 1, :, :], ALU.add).then_inc(sem.x_in, 1)
                for n in range(12):
                    t, q = divmod(n, 4)
                    m = P if t < 2 else NB
                    dst = yrow[0:m, t, :] if t < 2 else ysrow[0:NB, :]
                    dve.wait_ge(sem.x_T, n + 1)
                    dve.tensor_copy(dst[:, q * 512:(q + 1) * 512], mb[0:m, n % 4, :]).then_inc(sem.x_ok, 1)

            @block.sync
            def _(sp):
                sp.wait_ge(sem.x_ok, 8)
                sp.dma_start(o.y_prompt.rearrange("a (t p) n -> p (a t) n", p=P), yrow).then_inc(sem.y_out, 16)
                sp.wait_ge(sem.x_ok, 12)
                sp.dma_start(o.y_sample.rearrange("b t n -> (b t) n"), ysrow[0:NB, :]).then_inc(sem.y_out, 16)
                sp.wait_ge(sem.y_out, 32)


_INS = ['x_prompt', 'x_sample', 'cache_conv', 'cache_dsa_k', 'cache_dsa_v', 'cache_dsa_idx_k', 'cache_mem_k', 'cache_mem_v',
        'state_gdn', 'state_ret', 'state_lru', 'page_table', 'mem_prompt', 'w_in', 'conv_w', 'conv_b', 'gdn_a_log',
        'gdn_dt_bias', 'gdn_norm_w', 'lru_lambda', 'lru_w_r', 'lru_b_r', 'lru_w_i', 'lru_b_i', 'w_mem_kv', 'w_branch',
        'w_out', 'ln_g', 'ln_b']
_OUTS = [('y_prompt', (1, NP, D)), ('y_sample', (NB, 1, D)),
         ('p_conv', (DEPTH, 1, 3, D)), ('p_gdn', (DEPTH, 1, NH, HD, HD)), ('p_ret', (DEPTH, 1, NH, HD, HD)),
         ('p_lru', (DEPTH, 1, W)), ('p_dsa_k', (DEPTH, 1, NP, NH, HD)), ('p_dsa_v', (DEPTH, 1, NP, NH, HD)),
         ('p_dsa_ik', (DEPTH, 1, NP, ID)), ('p_mem_k', (DEPTH, 1, NMEM, NH, HD)), ('p_mem_v', (DEPTH, 1, NMEM, NH, HD)),
         ('s_conv', (DEPTH, NB, 3, D)), ('s_gdn', (DEPTH, NB, NH, HD, HD)), ('s_ret', (DEPTH, NB, NH, HD, HD)),
         ('s_lru', (DEPTH, NB, W)), ('s_dsa_k', (DEPTH, NB, 1, NH, HD)), ('s_dsa_v', (DEPTH, NB, 1, NH, HD)),
         ('s_dsa_ik', (DEPTH, NB, 1, ID))]


def kernel(**inputs):
    import numpy as _np
    import concourse.bacc as _bacc
    from concourse import mybir as _mybir
    from concourse.bass_utils import run_bass_kernel_spmd as _run

    nc = _bacc.Bacc("TRN2", target_bir_lowering=False, num_devices=1)
    arrays, ins = {}, {}
    fixed, at, levels, decays = tables()
    consts = {"fixed": fixed, "levels": levels, "decays": decays}
    for name in _INS + list(consts):
        x = _np.ascontiguousarray(consts[name] if name in consts else inputs[name])
        arrays[f"in_{name}_dram"] = x
        ins[name] = nc.dram_tensor(f"in_{name}_dram", x.shape, _mybir.dt.from_np(x.dtype), kind="ExternalInput").ap()
    outs = {}
    for name, shape in _OUTS:
        outs[name] = nc.dram_tensor(f"out_{name}_dram", shape, _mybir.dt.float32, kind="ExternalOutput").ap()
    trunk(nc, namedtuple("Inputs", ins)(**ins), namedtuple("Outputs", outs)(**outs), at, fixed.shape[1])
    r = _run(nc, [arrays], core_ids=[0])
    return tuple(r.results[0][f"out_{name}_dram"] for name, _ in _OUTS)
```
